# Optimizing a Trainium2 kernel written in Bass

```python
import math
import jax, jax.numpy as jnp
from jax import lax
import numpy as np

D_MODEL = 1024
BATCH = 1
SEQ = 512
DEPTH = 2

N_GROUPS = 4
GROUP_WIDTH = D_MODEL // N_GROUPS
D_MIX = N_GROUPS * GROUP_WIDTH
HEAD_DIM = 64
N_HEADS_G = GROUP_WIDTH // HEAD_DIM
RWKV_LORA = 32
RWKV_DECAY_SCALE = math.exp(-0.5)
RWKV_LNX_EPS = 64e-5
RWKV_IN = 3 * GROUP_WIDTH + 2 * RWKV_LORA
RWKV_COLS = RWKV_IN + GROUP_WIDTH
BRANCH_COLS = 4 * GROUP_WIDTH
W_IN_COLS = RWKV_COLS + 3 * BRANCH_COLS
CONV_WIDTH = 3
MOBA_BLOCK = 256
MOBA_TOPK = 3
MOBA_QBLOCK = 128
RET_CHUNK = 128
REL_BUCKETS = 32
REL_MAX_DIST = 128
NORM_EPS = 1e-6

kernel_name = "hymba_style_rwkv7_conv_moba_retnet_hybrid"

def rmsnorm(x, w):
    xf = x.astype(jnp.float32)
    y = xf * lax.rsqrt(jnp.mean(xf * xf, axis=-1, keepdims=True) + NORM_EPS)
    return (y * w.astype(jnp.float32)).astype(x.dtype)

def token_shift(u):
    return jnp.pad(u, ((0, 0), (1, 0), (0, 0)))[:, :-1]

def rwkv7_time_mix(p, mu, w0, w2, a0, a2, k_k, k_a, r_k, lnx_w, lnx_b):
    B, T, _ = p.shape
    H, N, G, L = N_HEADS_G, HEAD_DIM, GROUP_WIDTH, RWKV_LORA
    p = p + (token_shift(p) - p) * mu
    r, k, v, wl, al = jnp.split(p, [G, 2 * G, 3 * G, 3 * G + L], axis=-1)
    decay = jnp.exp(-RWKV_DECAY_SCALE * jax.nn.sigmoid(w0 + jnp.tanh(wl) @ w2))
    a = jax.nn.sigmoid(a0 + al @ a2)
    kk = (k * k_k).reshape(B, T, H, N).astype(jnp.float32)
    kk = kk / jnp.maximum(jnp.sqrt(jnp.sum(kk * kk, axis=-1, keepdims=True)), 1e-12)
    k = k * (1.0 + (a - 1.0) * k_a)

    def heads(t):
        return t.reshape(B, T, H, N).astype(jnp.float32)

    rh, kh, vh = heads(r), heads(k), heads(v)
    to_time = lambda t: t.transpose(1, 0, 2, 3)
    xs = (to_time(rh), to_time(heads(decay)), to_time(kh), to_time(vh),
          to_time(kk), to_time(heads(a)))

    def step(state, inp):
        r_t, w_t, k_t, v_t, kk_t, a_t = inp
        s_kk = jnp.einsum('bhij,bhj->bhi', state, kk_t)
        state = (state * w_t[:, :, None, :]
                 - s_kk[..., None] * (kk_t * a_t)[:, :, None, :]
                 + v_t[..., None] * k_t[:, :, None, :])
        y_t = jnp.einsum('bhij,bhj->bhi', state, r_t)
        return state, y_t

    state0 = jnp.zeros((B, H, N, N), jnp.float32)
    _, y = lax.scan(step, state0, xs)
    y = y.transpose(1, 0, 2, 3)
    mean = jnp.mean(y, axis=-1, keepdims=True)
    var = jnp.mean(jnp.square(y - mean), axis=-1, keepdims=True)
    y = ((y - mean) * lax.rsqrt(var + RWKV_LNX_EPS)).reshape(B, T, G)
    y = y * lnx_w.astype(jnp.float32) + lnx_b.astype(jnp.float32)
    bonus = jnp.sum(rh * kh * r_k.astype(jnp.float32), axis=-1, keepdims=True) * vh
    y = y + bonus.reshape(B, T, G)
    return y.astype(p.dtype)

def short_conv_mix(p, conv_w):
    T = p.shape[1]
    b_gate, c_gate, h = jnp.split(p, 3, axis=-1)
    u = c_gate * h
    up = jnp.pad(u, ((0, 0), (CONV_WIDTH - 1, 0), (0, 0)))
    y = up[:, 0:T] * conv_w[0]
    for j in range(1, CONV_WIDTH):
        y = y + up[:, j:j + T] * conv_w[j]
    return b_gate * y

def t5_bucket(dist):
    max_exact = REL_BUCKETS // 2
    d_f = jnp.maximum(dist, 1).astype(jnp.float32)
    large = max_exact + (jnp.log(d_f / max_exact) / math.log(REL_MAX_DIST / max_exact)
                         * (REL_BUCKETS - max_exact)).astype(jnp.int32)
    large = jnp.minimum(large, REL_BUCKETS - 1)
    return jnp.where(dist < max_exact, dist, large)

def moba_attention(q, k, v, rel_bias):
    B, T, _ = q.shape
    H, Dh, BLK, QB = N_HEADS_G, HEAD_DIM, MOBA_BLOCK, MOBA_QBLOCK
    to_heads = lambda t: t.reshape(B, T, H, Dh).transpose(0, 2, 1, 3)
    q, k, v = to_heads(q) * (Dh ** -0.5), to_heads(k), to_heads(v)
    nb = -(-T // BLK)
    pad = nb * BLK - T
    kp = jnp.pad(k, ((0, 0), (0, 0), (0, pad), (0, 0))).reshape(B, H, nb, BLK, Dh)
    vp = jnp.pad(v, ((0, 0), (0, 0), (0, pad), (0, 0))).reshape(B, H, nb, BLK, Dh)
    k_mean = jnp.mean(kp, axis=3)
    gate = jnp.einsum('bhtd,bhnd->bhtn', q, k_mean).astype(jnp.float32)
    q_block = jnp.arange(T) // BLK
    fully_past = jnp.arange(nb)[None, :] < q_block[:, None]
    gate = jnp.where(fully_past, gate, -jnp.inf)
    ksel = min(MOBA_TOPK, nb)
    top_val, top_idx = lax.top_k(gate, ksel)
    sel_ok = jnp.isfinite(top_val)

    nqb = T // QB
    def to_items(t):
        X = t.shape[-1]
        return t.reshape(B, H, nqb, QB, X).transpose(0, 2, 1, 3, 4).reshape(B * nqb, H, QB, X)

    items = jnp.arange(B * nqb)
    bias_tab = rel_bias.T
    offs = jnp.arange(BLK)

    def one_item(args):
        item, q_i, idx_i, ok_i = args
        b = item // nqb
        qb = item % nqb
        kb = lax.dynamic_index_in_dim(kp, b, 0, keepdims=False)
        vb = lax.dynamic_index_in_dim(vp, b, 0, keepdims=False)
        k_sel = jax.vmap(lambda kh, ih: kh[ih])(kb, idx_i)
        v_sel = jax.vmap(lambda vh, ih: vh[ih])(vb, idx_i)
        ib = (qb * QB) // BLK
        k_own = lax.dynamic_index_in_dim(kb, ib, 1, keepdims=False)
        v_own = lax.dynamic_index_in_dim(vb, ib, 1, keepdims=False)
        q_pos = qb * QB + jnp.arange(QB)
        sel_pos = idx_i[..., None] * BLK + offs
        own_pos = ib * BLK + offs
        bias_sel = jax.vmap(lambda tab, bk: tab[bk])(bias_tab, t5_bucket(q_pos[None, :, None, None] - sel_pos))
        own_dist = q_pos[:, None] - own_pos[None, :]
        bias_own = bias_tab[:, t5_bucket(jnp.maximum(own_dist, 0))]
        s_sel = jnp.einsum('hqd,hqnkd->hqnk', q_i, k_sel) + bias_sel
        s_sel = jnp.where(ok_i[..., None], s_sel, -jnp.inf)
        s_own = jnp.einsum('hqd,hkd->hqk', q_i, k_own) + bias_own
        s_own = jnp.where((own_dist >= 0)[None], s_own, -jnp.inf)
        logits = jnp.concatenate([s_sel.reshape(H, QB, ksel * BLK), s_own], axis=-1).astype(jnp.float32)
        prob = jax.nn.softmax(logits, axis=-1).astype(v.dtype)
        p_sel = prob[..., :ksel * BLK].reshape(H, QB, ksel, BLK)
        p_own = prob[..., ksel * BLK:]
        return (jnp.einsum('hqnk,hqnkd->hqd', p_sel, v_sel)
                + jnp.einsum('hqk,hkd->hqd', p_own, v_own))

    out = lax.map(one_item, (items, to_items(q), to_items(top_idx), to_items(sel_ok)))
    out = out.reshape(B, nqb, H, QB, Dh).transpose(0, 1, 3, 2, 4).reshape(B, T, H * Dh)
    return out

def rotate_every_two(x, pos):
    half = x.shape[-1] // 2
    theta = 1.0 / (10000.0 ** jnp.linspace(0.0, 1.0, half))
    ang = pos[:, None] * theta[None, :]
    sin, cos = jnp.sin(ang).astype(x.dtype), jnp.cos(ang).astype(x.dtype)
    x1, x2 = x[..., 0::2], x[..., 1::2]
    return jnp.stack([x1 * cos - x2 * sin, x1 * sin + x2 * cos], axis=-1).reshape(x.shape)

def retention_chunkwise(q, k, v):
    B, T, _ = q.shape
    H, Dh, C = N_HEADS_G, HEAD_DIM, RET_CHUNK
    to_heads = lambda t: t.reshape(B, T, H, Dh).transpose(0, 2, 1, 3).astype(jnp.float32)
    pos = jnp.arange(T, dtype=jnp.float32)
    q = rotate_every_two(to_heads(q), pos)
    k = rotate_every_two(to_heads(k), pos) * (Dh ** -0.5)
    v = to_heads(v)
    log_gamma = jnp.log(1.0 - 2.0 ** (-5.0 - jnp.arange(H, dtype=jnp.float32)))
    idx = jnp.arange(C, dtype=jnp.float32)
    diff = idx[:, None] - idx[None, :]
    decay_intra = jnp.where(diff >= 0, jnp.exp(log_gamma[:, None, None] * jnp.maximum(diff, 0.0)), 0.0)
    q_decay = jnp.exp(log_gamma[:, None] * (idx + 1.0))[..., None]
    k_decay = jnp.exp(log_gamma[:, None] * (C - 1.0 - idx))[..., None]
    chunk_decay = jnp.exp(log_gamma * C)[:, None, None]
    nc = T // C
    chunks = lambda t: t.reshape(B, H, nc, C, Dh).transpose(2, 0, 1, 3, 4)

    def step(R, inp):
        qc, kc, vc = inp
        inner = jnp.einsum('bhnd,bhmd->bhnm', qc, kc) * decay_intra
        y = (jnp.einsum('bhnm,bhmd->bhnd', inner, vc)
             + jnp.einsum('bhnd,bhde->bhne', qc * q_decay, R))
        R = R * chunk_decay + jnp.einsum('bhmd,bhme->bhde', kc * k_decay, vc)
        return R, y

    R0 = jnp.zeros((B, H, Dh, Dh), jnp.float32)
    _, y = lax.scan(step, R0, (chunks(q), chunks(k), chunks(v)))
    y = y.transpose(1, 0, 3, 2, 4).reshape(B, T, H, Dh)
    y = y * lax.rsqrt(jnp.mean(y * y, axis=-1, keepdims=True) + NORM_EPS)
    return y.reshape(B, T, H * Dh)

def hybrid_layer(x, norm_w, w_in, w_out, rwkv_mu, rwkv_w0, rwkv_w2, rwkv_a0, rwkv_a2,
                 rwkv_k_k, rwkv_k_a, rwkv_r_k, rwkv_lnx_w, rwkv_lnx_b, conv_w, rel_bias):
    G = GROUP_WIDTH
    h = rmsnorm(x, norm_w)
    proj = h @ w_in
    p_rwkv, p_conv, p_moba, p_ret = jnp.split(
        proj, [RWKV_COLS, RWKV_COLS + BRANCH_COLS, RWKV_COLS + 2 * BRANCH_COLS], axis=-1)
    dt = proj.dtype
    y_rwkv = rwkv7_time_mix(p_rwkv[..., :RWKV_IN], rwkv_mu, rwkv_w0, rwkv_w2, rwkv_a0, rwkv_a2,
                            rwkv_k_k, rwkv_k_a, rwkv_r_k, rwkv_lnx_w, rwkv_lnx_b)
    y_rwkv = y_rwkv.astype(dt) * jax.nn.silu(p_rwkv[..., RWKV_IN:])
    y_conv = short_conv_mix(p_conv[..., :3 * G], conv_w).astype(dt) * jax.nn.silu(p_conv[..., 3 * G:])
    y_moba = moba_attention(p_moba[..., :G], p_moba[..., G:2 * G], p_moba[..., 2 * G:3 * G], rel_bias)
    y_moba = y_moba.astype(dt) * jax.nn.silu(p_moba[..., 3 * G:])
    y_ret = retention_chunkwise(p_ret[..., :G], p_ret[..., G:2 * G], p_ret[..., 2 * G:3 * G])
    y_ret = y_ret.astype(dt) * jax.nn.silu(p_ret[..., 3 * G:])
    y = jnp.concatenate([y_rwkv, y_conv, y_moba, y_ret], axis=-1)
    return x + y @ w_out

def setup_inputs(seed: int = 0) -> dict:
    key = jax.random.key(seed)
    ks = jax.random.split(key, 17)
    f32 = jnp.float32
    nrm = lambda k, shape: jax.random.normal(k, shape, f32)
    G, L = GROUP_WIDTH, RWKV_LORA
    return {
        "x": nrm(ks[0], (BATCH, SEQ, D_MODEL)),
        "norm_w": 1.0 + 0.02 * nrm(ks[1], (DEPTH, D_MODEL)),
        "w_in": nrm(ks[2], (DEPTH, D_MODEL, W_IN_COLS)) * D_MODEL ** -0.5,
        "w_out": nrm(ks[3], (DEPTH, D_MIX, D_MODEL)) * D_MIX ** -0.5,
        "rwkv_mu": jax.random.uniform(ks[4], (DEPTH, RWKV_IN), f32),
        "rwkv_w0": 0.5 * nrm(ks[5], (DEPTH, G)),
        "rwkv_w2": nrm(ks[6], (DEPTH, L, G)) * 0.5 * L ** -0.5,
        "rwkv_a0": 0.5 * nrm(ks[7], (DEPTH, G)),
        "rwkv_a2": nrm(ks[8], (DEPTH, L, G)) * 0.5 * L ** -0.5,
        "rwkv_k_k": 0.85 + 0.05 * nrm(ks[9], (DEPTH, G)),
        "rwkv_k_a": 1.0 + 0.05 * nrm(ks[10], (DEPTH, G)),
        "rwkv_r_k": 0.1 * nrm(ks[11], (DEPTH, N_HEADS_G, HEAD_DIM)),
        "rwkv_lnx_w": 1.0 + 0.02 * nrm(ks[12], (DEPTH, G)),
        "rwkv_lnx_b": 0.02 * nrm(ks[13], (DEPTH, G)),
        "conv_w": nrm(ks[14], (DEPTH, CONV_WIDTH, G)) * CONV_WIDTH ** -0.5,
        "rel_bias": 0.5 * nrm(ks[15], (REL_BUCKETS, N_HEADS_G)),
        "final_norm_w": 1.0 + 0.02 * nrm(ks[16], (D_MODEL,)),
    }

def reference(x, norm_w, w_in, w_out, rwkv_mu, rwkv_w0, rwkv_w2, rwkv_a0, rwkv_a2,
              rwkv_k_k, rwkv_k_a, rwkv_r_k, rwkv_lnx_w, rwkv_lnx_b, conv_w, rel_bias,
              final_norm_w):
    for l in range(DEPTH):
        x = hybrid_layer(x, norm_w[l], w_in[l], w_out[l], rwkv_mu[l], rwkv_w0[l], rwkv_w2[l],
                         rwkv_a0[l], rwkv_a2[l], rwkv_k_k[l], rwkv_k_a[l], rwkv_r_k[l],
                         rwkv_lnx_w[l], rwkv_lnx_b[l], conv_w[l], rel_bias)
    return rmsnorm(x, final_norm_w)


_drawn_inputs = setup_inputs


def setup_inputs(seed=0):
    import zlib

    import numpy as np

    out = dict(_drawn_inputs(seed))
    spreads = {}
    factors = {'rwkv_k_k': 8.0,
     'rwkv_lnx_w': 6.953,
     'rwkv_lnx_b': 6.882,
     'final_norm_w': 8.165,
     'rel_bias': 3.522}
    for name, (base, spread) in spreads.items():
        noise = np.random.default_rng([zlib.crc32(name.encode()), seed]).standard_normal(out[name].shape)
        drawn = base * np.exp(spread * noise) if base else spread * noise
        out[name] = __import__('jax').numpy.asarray(drawn.astype(out[name].dtype))
    for name, factor in factors.items():
        out[name] = (out[name] * factor).astype(out[name].dtype)
    return out
```

```python
import math
from contextlib import ExitStack

import numpy as np

import concourse.bass as bass
from concourse import mybir

F32 = mybir.dt.float32
F32R = mybir.dt.float32r
I32 = mybir.dt.int32
ALU = mybir.AluOpType
ACT = mybir.ActivationFunctionType
AX_X = mybir.AxisListType.X

P = 128
DEPTH = 2
T = 512
D = 1024
G = 256
HEADS = 4
N = 64
NT = T // P
KT = D // P
CH = 64
NCH = T // CH
MATS = NT * HEADS
LORA = 32
BUCKETS = 32
DECAY = math.exp(-0.5)
NORM_EPS = 1e-6
LNX_EPS = 64e-5
MASKED = -1e30
LEVELS = [1, 2, 4, 8, 16, 32]
DIST = T + P

RWKV, CONV, MOBA, RET = 0, 1088, 2112, 3136
TILE_COLS = {"wa": 768, "rwkv_g0": 832, "rwkv_g1": 960}
for _base, _names in ((RWKV, ("r", "k", "v")), (CONV, ("cb", "cc", "ch", "conv_g")),
                      (MOBA, ("mq", "mk", "mv", "moba_g")), (RET, ("rq", "rk", "rv", "ret_g"))):
    for _i, _n in enumerate(_names):
        for _p in range(2):
            TILE_COLS[f"{_n}{_p}"] = _base + G * _i + P * _p
TILES = ["k0", "k1", "wa", "r0", "r1", "v0", "v1", "rwkv_g0", "rwkv_g1",
         "mq0", "mq1", "mk0", "mk1", "mv0", "mv1", "moba_g0", "moba_g1",
         "rq0", "rq1", "rk0", "rk1", "rv0", "rv1", "ret_g0", "ret_g1",
         "cc0", "cc1", "ch0", "ch1", "cb0", "cb1", "conv_g0", "conv_g1"]
OUT_TILES = [f"out{m}" for m in range(KT)]
STREAM = TILES + OUT_TILES

MU, W0, A0, KKP, KAP, RKP, LNW, LNB, CONVW, NORMW, FNORM = 0, 7, 9, 11, 13, 15, 17, 19, 21, 27, 35
N_PAR = 43
MU_ROW = {"r0": 0, "r1": 1, "k0": 2, "k1": 3, "v0": 4, "v1": 5, "wa": 6}
MUC, HW0, HA0, KA2, KA1 = 0, 7, 9, 11, 13
N_DER = 15

CONSTS = [("ident", 128), ("head_mean", 128), ("all_mean", 128), ("rot", 128), ("causal", 128),
          ("score_mask", 320), ("eye64", 64), ("k_decay", 16), ("eps", 2),
          ("chunk_reset", 512), ("cos", 512), ("sin", 512), ("ret_eps", 1024)]
COL, _at = {}, 0
for _n, _w in CONSTS:
    COL[_n] = (_at, _at + _w)
    _at += _w
N_CONST = _at

def layer_steps():
    s = [("norm",)]
    s += [("shift", "k0"), ("shift", "k1"), ("shift", "wa"), ("kk_square",), ("shift", "r0"),
          ("kk_norm",), ("lora_tanh",), ("shift", "r1"), ("lora",), ("shift", "v0"), ("decay_scan",), ("shift", "v1"),
          ("decay_exp",), ("gate", "rwkv", 0), ("factors",), ("gate", "rwkv", 1), ("copy", "mq0"), ("copy", "mq1"), ("bonus",)]
    s += [("to_rows", "v"), ("copy", "mk0"), ("to_rows", "kap"), ("copy", "mk1"), ("to_rows", "bet"),
          ("copy", "mv0"), ("to_rows", "alp"), ("copy", "mv1"), ("scores", 0),
          ("scores", 1), ("to_rows", "mv"), ("gate", "moba", 0), ("scores", 2), ("scores", 3),
          ("gate", "moba", 1), ("inverse_start",)]
    ret = [[("copy", "rq0")], [("copy", "rq1"), ("rotate", "rq0")], [("copy", "rk0"), ("rotate", "rq1")],
           [("copy", "rk1"), ("rotate", "rk0")], [("copy", "rv0"), ("rotate", "rk1")],
           [("copy", "rv1")], [("gate", "ret", 0), ("to_rows", "rv")], [("gate", "ret", 1)]]
    half = [(kind, n) for n in LEVELS[1:] for kind in ("inverse_x", "inverse_y")]
    for i in range(8):
        s += ret[i]
        s.append(half[i])
        s += [("attend", 2 * i), ("attend", 2 * i + 1)]
        if i in (3, 7):
            s.append(("attend_out", i // 4))
    s += [("conv_c", 0), half[8], ("conv_c", 1), half[9], ("conv_h", 0), ("chunk_b",), ("conv_h", 1), ("chunk_uw",),
          ("conv_b", 0), ("chunk_qghy",)]
    rs = [("retain", h, kb) for h in range(HEADS) for kb in range(NT)]
    s += [("chain", 1)] + rs[0:2] + [("conv_b", 1)] + [("chain", 2)] + rs[2:4] + [("chain", 3)] + rs[4:6]
    s += [("gate", "conv", 0), ("chain", 4)] + rs[6:8] + [("retain_out", 0), ("chain", 5)] + rs[8:10] + [("chain", 6)]
    s += [("gate", "conv", 1), ("chunk_y",)] + rs[10:12] + [("ln_mean",)] + rs[12:14] + [("ln_square",)] + rs[14:16]
    s += [("retain_out", 1), ("ln_var",), ("ret_stat",), ("conv_out",), ("roots",), ("finish",)]
    s += [("split_y",)] + [("project_out", m) for m in range(KT)]
    return s


STEPS = layer_steps()
Y_ORDER = [2, 3, 4, 5, 6, 7, 0, 1]


def bank_jobs():
    pro = [("params0", 6, 1), ("params1", 7, 1), *((f"bias_row{h}{j}", 4 + j, 1) for h in range(HEADS) for j in range(2))]
    pro += [(f"x_in{m}", (3, 4, 5, 6, 7)[m % 5], 1) for m in range(KT)] + [("stat", 2, 1)]
    layer = []
    n_proj = [0]

    def proj(name, readers):
        layer.append((name, n_proj[0] % 2, readers))
        n_proj[0] += 1

    turn = [0]

    def any6(name, readers=1, banks=(2, 3, 4, 5, 6, 7)):
        layer.append((name, banks[turn[0] % len(banks)], readers))
        turn[0] += 1

    for step in STEPS:
        kind = step[0]
        if kind == "shift":
            proj(step[1], 2)
        elif kind == "copy":
            proj(step[1], 1)
        elif kind == "gate":
            proj(f"{step[1]}_g{step[2]}", 2)
        elif kind == "kk_square":
            any6("kk0"), any6("kk1")
        elif kind == "lora":
            for n in ("zw0", "zw1", "za0", "za1"):
                any6(n)
        elif kind == "bonus":
            any6("bonus0"), any6("bonus1")
        elif kind == "to_rows":
            for p in range(2):
                if step[1] == "rv":
                    layer.append((f"rows_rv{p}", 3, 1))
                else:
                    any6(f"rows_{step[1]}{p}")
        elif kind == "scores":
            for p in range(2):
                for hh in range(2):
                    any6(f"scores{step[1]}{p}{hh}")
        elif kind == "inverse_x":
            layer += [(f"x{step[1]}_0", 5, 1), (f"x{step[1]}_1", 6, 1)]
        elif kind == "inverse_y":
            for g in range(2):
                if step[1] != LEVELS[-1]:
                    layer.append((f"y{step[1]}_{g}", 5 + g, 1))
                layer.append((f"yt{step[1]}_{g}", 7, 1))
        elif kind == "rotate":
            layer.append((f"rot_{step[1]}", 3, 1))
        elif kind == "attend":
            layer.append((f"s{step[1]}", 2, 1))
            if step[1] % 8:
                layer.append((f"pt{step[1] - 1}", 3, 1))
        elif kind == "attend_out":
            layer += [(f"pt{8 * step[1] + 7}", 3, 1), (f"moba_y{step[1]}", 4, 1)]
        elif kind in ("conv_c", "conv_h", "conv_b"):
            proj({"conv_c": "cc", "conv_h": "ch", "conv_b": "cb"}[kind] + str(step[1]), 1)
        elif kind == "chunk_b":
            layer += [("b0", 5, 1), ("b1", 6, 1)]
        elif kind == "chunk_uw":
            layer += [(f"uw{t}", (7, 5, 6, 7)[t], 1) for t in range(NT)]
        elif kind == "chunk_qghy":
            layer += [("g0", 5, 1), ("g1", 6, 1), ("h0", 7, 1), ("h1", 5, 1), ("q0", 6, 1), ("q1", 7, 1), ("y10", 5, 1), ("y11", 6, 1)]
        elif kind == "chain":
            layer.append((f"chain{step[1]}", 7, 1))
        elif kind == "chunk_y":
            layer += [("y20", 5, 1), ("y21", 6, 1)]
        elif kind == "retain":
            layer.append((f"rs{step[1]}{step[2]}", 2 + step[2] % 2, 2 if step[2] < NT - 1 else 1))
        elif kind == "retain_out":
            layer.append((f"ret_y{step[1]}", 4, 1))
        elif kind == "ln_mean":
            layer += [("mean0", 5, 1), ("mean1", 6, 1)]
        elif kind == "ln_var":
            layer += [("var0", 7, 1), ("var1", 5, 1)]
        elif kind == "ret_stat":
            layer += [("ret_ms0", 6, 1), ("ret_ms1", 3, 1)]
        elif kind == "project_out":
            proj(f"out{step[1]}", 1)
            if step[1] == KT - 1:
                layer.append(("stat", 2, 1))
    epi = [(f"row{t}{half}", 3 + (2 * t + half) % 5, 1) for t in range(NT) for half in range(2)]
    return pro, layer, epi


def trunk_kernel(nc, x, norm_w, w_in, w_out, rwkv_mu, rwkv_w0, rwkv_w2, rwkv_a0, rwkv_a2, rwkv_k_k,
                 rwkv_k_a, rwkv_r_k, rwkv_lnx_w, rwkv_lnx_b, conv_w, rel_bias, final_norm_w,
                 consts, level_masks, bucket_onehot, x_scratch, bias_scratch, out):
    pro, per_layer, epi = bank_jobs()
    place = {}
    full_count, read_count = [0] * 8, [0] * 8
    for part, names in (("pro", pro), ("layer", per_layer), ("epi", epi)):
        if part == "layer":
            pro_full, pro_read = list(full_count), list(read_count)
            full_count, read_count = [0] * 8, [0] * 8
        if part == "epi":
            lay_full, lay_read = list(full_count), list(read_count)
            full_count, read_count = [0] * 8, [0] * 8
        for name, bank, readers in names:
            place[part, name] = (bank, full_count[bank], read_count[bank], readers)
            full_count[bank] += 1
            read_count[bank] += readers

    def locate(name, layer):
        part = "pro" if layer < 0 else "epi" if layer >= DEPTH else "layer"
        bank, nf, nr, readers = place[part, name]
        if part != "pro":
            nf += pro_full[bank] + layer * lay_full[bank]
            nr += pro_read[bank] + layer * lay_read[bank]
        return bank, nf, nr, readers

    with ExitStack() as ctx:
        def sb(name, shape, dt=F32):
            return ctx.enter_context(nc.sbuf_tensor(name, shape, dt))

        bank = [ctx.enter_context(nc.psum_tensor(f"bank{i}", [P, 512], F32)) for i in range(8)]
        XY = sb("x_or_y", [P, KT, T])
        act_hi = sb("act_hi", [P, KT, T], F32R)
        act_lo = sb("act_lo", [P, KT, T], F32R)
        w_raw = sb("w_raw", [P, 3, KT, P])
        w_hi = sb("w_hi", [P, 2, KT, P], F32R)
        w_lo = sb("w_lo", [P, 2, KT, P], F32R)
        PG = 1040
        pages = sb("pages", [P, 25 * PG])
        cst = sb("constants", [P, N_CONST])
        lmask = sb("level_mask", [P, 2, len(LEVELS), CH], I32)
        bias = sb("bias", [P, HEADS, T])
        par = sb("params", [P, DEPTH, N_PAR])
        der = sb("params_derived", [P, DEPTH, N_DER])
        lora_w = sb("lora_w", [2 * LORA, DEPTH, G])
        small = sb("small", [P, 32])
        w_end = sb("chunk_decay", [P, 2, NCH])

        def page(i, n=1):
            return pages[:, i * PG:(i + n - 1) * PG + 1024]

        def pair(i):
            return page(i).rearrange("p (a t) -> p a t", a=2)

        def half(i, j):
            return pages[:, i * PG + 512 * j:i * PG + 512 * (j + 1)]

        def const(name):
            a, b = COL[name]
            return cst[:, a:b]

        ident, head_mean, all_mean = const("ident"), const("head_mean"), const("all_mean")
        R, K, V, TH, TA, KN, PI = (pair(i) for i in (0, 1, 2, 3, 4, 5, 7))
        Pd = pages[:, 6 * PG:7 * PG].rearrange("p (a c t) -> p a c t", a=2, c=NCH)
        AR = pages[:, 8 * PG:8 * PG + 2048].rearrange("p (x a t) -> p x a t", x=2, a=2)
        WA = page(10)[:, 0:T]
        KF = pair(24)
        BA = pages[:, 11 * PG:11 * PG + 2048].rearrange("p (m x i) -> p m x i", m=MATS, x=2)
        rows = {n: page(i).rearrange("p (t c) -> p t c", t=NT)
                for n, i in (("bet", 13), ("kap", 14), ("v", 15), ("mv", 23), ("rv", 10))}
        SC = pages[:, 16 * PG:16 * PG + MATS * 320].rearrange("p (m c) -> p m c", m=MATS)
        MQ, MK = pair(21), pair(22)
        Ti, TiT, Xm = (page(i).rearrange("p (m c) -> p m c", m=MATS) for i in (3, 5, 6))
        RQ, RK = pair(2), pair(4)
        bias_rows = pages[:, 21 * PG:21 * PG + HEADS * DIST].rearrange("p (h c) -> p h c", h=HEADS)
        UW = pages[:, 21 * PG:21 * PG + 2048].rearrange("p (m x i) -> p m x i", m=MATS, x=2)
        GT, HP, ST = (page(i).rearrange("p (a c i) -> p a c i", a=2, c=NCH) for i in (8, 3, 6))
        RSB = pair(1)
        Y1 = pair(23)
        CU = pages[:, 7 * PG:8 * PG].rearrange("p (a t) -> p a t", a=2)
        CA = pair(24)
        LNS, RY, RSQ = pair(11), pair(12), pair(5)

        sem = {}

        def s(name):
            if name not in sem:
                sem[name] = ctx.enter_context(nc.semaphore(name))
            return sem[name]

        bank_full = [s(f"bank{i}_full") for i in range(8)]
        bank_read = [s(f"bank{i}_read") for i in range(8)]

        SIGNALS = {
            "h_raw": KT, "h_hi": KT, "h_split": KT,
            "kk_sq": 2, "kk_unit": 2, "lora_in": 1, "decay_sum": 2,
            "decay_exp": 4, "beta": 1, "kappa": 1, "alpha": 1, "rho": 1, "rkv": 2, "t_init": 1, "tt_init": 1, "pads": 1,
            "rotated": 4, "logit_max": 16, "prob": 16, "prob_norm": 16, "first_state": 1, "ln_sq": 2,
            "ret_sq": 2, "ret_root": 2, "y_hi": KT, "y_split": KT, "y_conv": 2, "y_ret": 2, "y_rwkv": 2,
            "eye_set": 1, "conv_pad": 1,
        }

        def at(name, layer, n=None):
            return s(name), layer * SIGNALS[name] + (SIGNALS[name] if n is None else n)

        def full(job, layer):
            b, nf, _, _ = locate(job, layer)
            return bank_full[b], nf + 1

        def read(job, layer, n=None):
            b, _, nr, readers = locate(job, layer)
            return bank_read[b], nr + (readers if n is None else n)

        def ps(job, layer):
            return bank[locate(job, layer)[0]]

        def done(job, layer):
            return bank_read[locate(job, layer)[0]]

        block = ctx.enter_context(nc.Block())

        @block.sync
        def _(sp):
            def load(dst, src, name):
                sp.dma_start(dst, src).then_inc(s(name), 16)

            load(cst[:, 0:COL["rot"][0]], consts[:, 0:COL["rot"][0]], "const_a")
            for t in range(NT):
                load(page(17 + t), x[0, t * P:(t + 1) * P, :], f"x_loaded{t}")

            n_stream = len(STREAM)

            def load_weights(i):
                layer, j = divmod(i, n_stream)
                if i >= 3:
                    sp.wait_ge(s("w_split"), i - 2)
                if j < len(TILES):
                    c = TILE_COLS[TILES[j]]
                    src = w_in[layer, :, c:c + P]
                else:
                    src = w_out[layer, :, (j - len(TILES)) * P:(j - len(TILES) + 1) * P]
                sp.dma_start(w_raw[:, i % 3, :, :], src.rearrange("(k p) c -> p k c", p=P)).then_inc(s(f"w_loaded{i % 3}"), 16)

            prow = page(13)[0:N_PAR, 0:DEPTH * P].rearrange("r (l c) -> r l c", l=DEPTH)
            load_weights(0)
            sp.wait_ge(s("par_clear"), 1)
            rws = lambda a, n: a.rearrange("l (r c) -> r l c", c=P)[0:n]
            load(prow[0:6], rws(rwkv_mu[:, 0:768], 6), "par_loaded")
            load(prow[6:7, :, 0:64], rwkv_mu[:, 768:832].rearrange("l (r c) -> r l c", r=1), "par_loaded")
            for r0, a in ((W0, rwkv_w0), (A0, rwkv_a0), (KKP, rwkv_k_k), (KAP, rwkv_k_a), (LNW, rwkv_lnx_w), (LNB, rwkv_lnx_b)):
                load(prow[r0:r0 + 2], rws(a, 2), "par_loaded")
            load(prow[RKP:RKP + 2], rwkv_r_k.rearrange("l (r h) n -> r l (h n)", r=2), "par_loaded")
            load(prow[CONVW:CONVW + 6], conv_w.rearrange("l j (p c) -> (j p) l c", p=2), "par_loaded")
            load(prow[NORMW:NORMW + 8], rws(norm_w, 8), "par_loaded")
            for l in range(DEPTH):
                load(prow[FNORM:FNORM + 8, l, :], final_norm_w.rearrange("(r c) -> r c", c=P), "par_loaded")
            load(page(14)[0:BUCKETS, 0:HEADS], rel_bias, "bias_in")
            load(page(14)[BUCKETS:BUCKETS + 1, 0:HEADS], bucket_onehot[BUCKETS:BUCKETS + 1, DIST:DIST + HEADS], "bias_in")
            load(page(15)[0:BUCKETS + 1, 0:DIST], bucket_onehot[:, 0:DIST], "bias_in")
            load(cst[:, COL["rot"][0]:], consts[:, COL["rot"][0]:], "const_b")
            load(lmask[:].rearrange("p a l c -> p (a l c)"), level_masks, "const_b")
            load(lora_w[0:LORA], rwkv_w2.rearrange("l k c -> k l c"), "const_b")
            load(lora_w[LORA:2 * LORA], rwkv_a2.rearrange("l k c -> k l c"), "const_b")
            load_weights(1)
            load_weights(2)
            for j in range(2):
                sp.wait_ge(*read(f"bias_row{HEADS - 1}{j}", -1))
            load(bias_scratch.rearrange("h q c -> q h c")[:, :, 0:DIST], bias_rows, "bias_out")
            sp.wait_ge(s("bias_out"), 16)
            skewed = bias_scratch.rearrange("h q c -> h (q c)")[:, 0:P * DIST].rearrange("h (q c) -> q h c", c=DIST)
            load(bias[:, :, :], skewed[:, :, P - 1:P - 1 + T], "bias_back")
            for m in range(KT):
                sp.wait_ge(*read(f"x_in{m}", -1))
                load(x_scratch[m], XY[:, m, :], "x_spill")

            i = 3
            for layer in range(DEPTH):
                while i < (layer + 1) * n_stream:
                    j = i - layer * n_stream
                    if j == len(TILES) + 3:
                        for k, m in enumerate(Y_ORDER):
                            sp.wait_ge(*at("y_split", layer, k + 1))
                            sp.wait_ge(s("x_spill"), 16 * KT * (layer + 1))
                            load(XY[:, m, :], x_scratch[m], f"x_back{m}")
                    load_weights(i)
                    i += 1
                if layer < DEPTH - 1:
                    for k in range(3):
                        load_weights(i)
                        i += 1
                    for m in range(KT):
                        sp.wait_ge(*read(f"out{m}", layer))
                        load(x_scratch[m], XY[:, m, :], "x_spill")
            for t in range(NT):
                for hf in range(2):
                    sp.wait_ge(*read(f"row{t}{hf}", DEPTH))
                sp.dma_start(out[0, t * P:(t + 1) * P, :], page(17 + t)).then_inc(s("stored"), 16)
            sp.wait_ge(s("stored"), 16 * NT)

        @block.gpsimd
        def _(pool):
            pool.memset(page(13)[0:N_PAR, 0:DEPTH * P], 0.0).then_inc(s("par_clear"), 1)
            H = KT // 2
            n_stream = len(STREAM)
            for i in range(DEPTH * n_stream):
                pool.wait_ge(s(f"w_loaded{i % 3}"), 16 * (i // 3 + 1))
                if i >= 2:
                    before = divmod(i - 2, n_stream)
                    pool.wait_ge(*full(STREAM[before[1]], before[0]))
                for a in range(2):
                    k = slice(a * H, (a + 1) * H)
                    pool.tensor_copy(w_hi[:, i % 2, k, :], w_raw[:, i % 3, k, :]).then_inc(s("w_high"), 1)
                for a in range(2):
                    k = slice(a * H, (a + 1) * H)
                    pool.wait_ge(s("w_high"), 2 * i + a + 1)
                    ins = pool.tensor_tensor(w_lo[:, i % 2, k, :], w_raw[:, i % 3, k, :], w_hi[:, i % 2, k, :].bitcast(F32), ALU.subtract)
                ins.then_inc(s("w_split"), 1)

        @block.tensor
        def _(pe):
            mm = pe.matmul

            def begin(job, layer):
                b, nf, nr, _ = locate(job, layer)
                if nr > 0:
                    pe.wait_ge(bank_read[b], nr)
                return bank[b]

            def end(ins, job, layer):
                ins.then_inc(bank_full[locate(job, layer)[0]], 1)

            pe.wait_ge(s("const_a"), 16)
            pe.wait_ge(s("par_loaded"), 16 * 13)
            for l in range(DEPTH):
                b = begin(f"params{l}", -1)
                end(pe.transpose(b[:, 0:N_PAR], page(13)[0:N_PAR, l * P:(l + 1) * P], ident[0:N_PAR, 0:N_PAR]), f"params{l}", -1)
            pe.wait_ge(s("bias_in"), 48)
            for h in range(HEADS):
                for j in range(2):
                    b = begin(f"bias_row{h}{j}", -1)
                    end(mm(b[:, 0:DIST // 2], page(14)[0:BUCKETS + 1, h:h + 1].to_broadcast([BUCKETS + 1, P]),
                           page(15)[0:BUCKETS + 1, j * (DIST // 2):(j + 1) * (DIST // 2)], start=True, stop=True), f"bias_row{h}{j}", -1)
            for m in range(KT):
                b = begin(f"x_in{m}", -1)
                for t in range(NT):
                    if m == 0:
                        pe.wait_ge(s(f"x_loaded{t}"), 16)
                    ins = pe.transpose(b[:, t * P:(t + 1) * P], page(17 + t)[:, m * P:(m + 1) * P], ident)
                end(ins, f"x_in{m}", -1)

            def stat(layer, m):
                if m == 0:
                    begin("stat", layer)
                pe.wait_ge(s("x_sq"), (layer + 1) * KT + m + 1)
                ins = mm(ps("stat", layer)[:, :], all_mean, half(24, m % 2), start=m == 0, stop=m == KT - 1)
                if m < KT - 1:
                    ins.then_inc(s("x_sq_used"), 1)
                else:
                    end(ins, "stat", layer)

            for m in range(KT):
                stat(-1, m)

            for layer in range(DEPTH):
                def project(job):
                    i = layer * len(STREAM) + STREAM.index(job)
                    pe.wait_ge(s("w_split"), i + 1)
                    b = begin(job, layer)
                    is_out = job in OUT_TILES
                    order = Y_ORDER if is_out else range(KT)
                    signal = "y_split" if is_out else "h_split"
                    for n, k in enumerate(order):
                        if job in ("k0", "out0"):
                            pe.wait_ge(*at(signal, layer, n + 1))
                        hi, lo = w_hi[:, i % 2, k, :], w_lo[:, i % 2, k, :]
                        mm(b[:, :], hi, act_hi[:, k, :], start=n == 0, stop=False)
                        mm(b[:, :], hi, act_lo[:, k, :], start=False, stop=False)
                        ins = mm(b[:, :], lo, act_hi[:, k, :], start=False, stop=n == KT - 1)
                    end(ins, job, layer)

                def shift(job):
                    project(job)

                def copy(job):
                    project(job)

                def gate(group, p):
                    project(f"{group}_g{p}")

                def conv_c(p):
                    project(f"cc{p}")

                def conv_h(p):
                    project(f"ch{p}")

                def conv_b(p):
                    project(f"cb{p}")

                def kk_square():
                    for p in range(2):
                        pe.wait_ge(*at("kk_sq", layer, p + 1))
                        b = begin(f"kk{p}", layer)
                        end(mm(b[:, :], head_mean, KN[:, p, :], start=True, stop=True), f"kk{p}", layer)

                def lora():
                    pe.wait_ge(*at("lora_in", layer))
                    for z, r0 in (("zw", 0), ("za", LORA)):
                        for p in range(2):
                            b = begin(f"{z}{p}", layer)
                            end(mm(b[:, :], lora_w[r0:r0 + LORA, layer, p * P:(p + 1) * P], WA[r0:r0 + LORA, :], start=True, stop=True), f"{z}{p}", layer)

                def bonus():
                    for p in range(2):
                        pe.wait_ge(*at("rkv", layer, p + 1))
                        b = begin(f"bonus{p}", layer)
                        end(mm(b[:, :], head_mean, R[:, p, :], start=True, stop=True), f"bonus{p}", layer)

                def to_rows(what):
                    src = {"v": V, "kap": PI, "bet": TA, "alp": AR[:, 0], "mv": pair(10), "rv": pair(8)}[what]
                    for p in range(2):
                        if what in ("mv", "rv"):
                            pe.wait_ge(*read(f"{what}{p}", layer))
                        elif what == "v":
                            pe.wait_ge(*read(f"v{p}", layer))
                        else:
                            pe.wait_ge(*at({"kap": "kappa", "bet": "beta", "alp": "alpha"}[what], layer))
                        b = begin(f"rows_{what}{p}", layer)
                        for t in range(NT):
                            ins = pe.transpose(b[:, t * P:(t + 1) * P], src[:, p, t * P:(t + 1) * P], ident)
                        end(ins, f"rows_{what}{p}", layer)

                def scores(t):
                    if t == 0:
                        pe.wait_ge(*at("rho", layer))
                    for p in range(2):
                        for hh in range(2):
                            job = f"scores{t}{p}{hh}"
                            b = begin(job, layer)
                            hr = slice(64 * hh, 64 * hh + 64)
                            for c in (2 * t, 2 * t + 1):
                                cs = slice(c * CH, (c + 1) * CH)
                                o = b[64 * (c % 2):64 * (c % 2) + 64, :]
                                mm(o[:, 0:128], PI[hr, p, cs], AR[hr, :, p, cs], start=True, stop=True)
                                mm(o[:, 128:256], TA[hr, p, cs], AR[hr, :, p, cs], start=True, stop=True)
                                ins = mm(o[:, 256:320], AR[hr, 0, p, cs], TA[hr, p, cs], start=True, stop=True)
                            end(ins, job, layer)

                def inverse_x(n):
                    for g in range(2):
                        if n == LEVELS[1]:
                            pe.wait_ge(*at("t_init", layer))
                            pe.wait_ge(*at("tt_init", layer))
                        else:
                            pe.wait_ge(*read(f"y{n // 2}_{g}", layer))
                        b = begin(f"x{n}_{g}", layer)
                        for i in range(8):
                            for c in range(2):
                                r = slice(64 * c, 64 * c + 64)
                                ins = mm(b[r, i * CH:(i + 1) * CH], SC[r, 8 * g + i, 128:192], Ti[r, 8 * g + i, :], start=True, stop=True)
                        end(ins, f"x{n}_{g}", layer)

                def inverse_y(n):
                    for g in range(2):
                        pe.wait_ge(*read(f"x{n}_{g}", layer))
                        if n > LEVELS[1]:
                            pe.wait_ge(*read(f"yt{n // 2}_{g}", layer))
                        if n != LEVELS[-1]:
                            b = begin(f"y{n}_{g}", layer)
                            for i in range(8):
                                for c in range(2):
                                    r = slice(64 * c, 64 * c + 64)
                                    ins = mm(b[r, i * CH:(i + 1) * CH], TiT[r, 8 * g + i, :], Xm[r, 8 * g + i, :], start=True, stop=True)
                            end(ins, f"y{n}_{g}", layer)
                        b = begin(f"yt{n}_{g}", layer)
                        for i in range(8):
                            for c in range(2):
                                r = slice(64 * c, 64 * c + 64)
                                ins = mm(b[r, i * CH:(i + 1) * CH], Xm[r, 8 * g + i, :], TiT[r, 8 * g + i, :], start=True, stop=True)
                        end(ins, f"yt{n}_{g}", layer)

                def rotate(job):
                    pe.wait_ge(*read(job, layer))
                    b = begin(f"rot_{job}", layer)
                    end(mm(b[:, :], const("rot"), half(8, int(job[-1])), start=True, stop=True), f"rot_{job}", layer)

                def attend(u):
                    h, qb = divmod(u, NT)
                    p, hh = divmod(h, 2)
                    w = (qb + 1) * P
                    hr = slice(64 * hh, 64 * hh + 64)
                    if u == 0:
                        for j in ("mq0", "mq1", "mk0", "mk1"):
                            pe.wait_ge(*read(j, layer))
                    b = begin(f"s{u}", layer)
                    end(mm(b[:, 0:w], MQ[hr, p, qb * P:(qb + 1) * P], MK[hr, p, 0:w], start=True, stop=True), f"s{u}", layer)
                    if u % 8:
                        attend_rest(u - 1)

                def attend_rest(u):
                    h, qb = divmod(u, NT)
                    p, hh = divmod(h, 2)
                    pe.wait_ge(*at("prob_norm", layer, u + 1))
                    b = begin(f"pt{u}", layer)
                    for kb in range(qb + 1):
                        ins = pe.transpose(b[:, kb * P:(kb + 1) * P], half(1, u % 2)[:, kb * P:(kb + 1) * P], ident)
                    end(ins, f"pt{u}", layer)
                    if u == 0:
                        for q in range(2):
                            pe.wait_ge(*read(f"rows_mv{q}", layer))
                    pe.wait_ge(*read(f"pt{u}", layer))
                    yb = begin(f"moba_y{p}", layer) if u % 8 == 0 else ps(f"moba_y{p}", layer)
                    for kb in range(qb + 1):
                        ins = mm(yb[64 * hh:64 * hh + 64, qb * P:(qb + 1) * P], rows["mv"][:, kb, h * N:(h + 1) * N],
                                 half(7, u % 2)[:, kb * P:(kb + 1) * P], start=kb == 0, stop=kb == qb)
                    if u % 8 == 7:
                        end(ins, f"moba_y{p}", layer)

                def attend_out(p):
                    attend_rest(8 * p + 7)

                def chunk_b():
                    for q in range(2):
                        pe.wait_ge(*read(f"rows_v{q}", layer))
                    for g in range(2):
                        b = begin(f"b{g}", layer)
                        for i in range(8):
                            m = 8 * g + i
                            t, h = divmod(m, HEADS)
                            for c in range(2):
                                r = slice(64 * c, 64 * c + 64)
                                ins = mm(b[r, i * CH:(i + 1) * CH], SC[r, m, 0:64], rows["v"][r, t, h * N:(h + 1) * N], start=True, stop=True)
                        end(ins, f"b{g}", layer)

                def chunk_uw():
                    for q in range(2):
                        pe.wait_ge(*read(f"rows_alp{q}", layer))
                        pe.wait_ge(*read(f"b{q}", layer))
                        pe.wait_ge(*read(f"yt{LEVELS[-1]}_{q}", layer))
                    for t in range(NT):
                        b = begin(f"uw{t}", layer)
                        for h in range(HEADS):
                            for c in range(2):
                                r = slice(64 * c, 64 * c + 64)
                                ins = mm(b[r, h * P:(h + 1) * P], TiT[r, t * HEADS + h, :], BA[r, t * HEADS + h, :, :], start=True, stop=True)
                        end(ins, f"uw{t}", layer)

                def chunk_qghy():
                    for t in range(NT):
                        pe.wait_ge(*read(f"uw{t}", layer))
                    for q in range(2):
                        pe.wait_ge(*read(f"rows_bet{q}", layer))
                        pe.wait_ge(*read(f"rows_kap{q}", layer))
                    U, W = UW[:, :, 0, :], UW[:, :, 1, :]
                    for what in "ghqy":
                        for c in range(2):
                            job = f"{what}{c}" if what != "y" else f"y1{c}"
                            b = begin(job, layer)
                            r = slice(64 * c, 64 * c + 64)
                            for p in range(2):
                                for t in range(NT):
                                    for hh in range(2):
                                        h = 2 * p + hh
                                        m = t * HEADS + h
                                        o = b[64 * hh:64 * hh + 64, (p * NT + t) * CH:(p * NT + t + 1) * CH]
                                        bet, kap, v = (rows[x][r, t, h * N:(h + 1) * N] for x in ("bet", "kap", "v"))
                                        if what == "g":
                                            ins = mm(o, W[r, m, :], bet, start=True, stop=True)
                                        elif what == "q":
                                            ins = mm(o, W[r, m, :], SC[r, m, 192:256], start=True, stop=True)
                                        elif what == "h":
                                            mm(o, kap, v, start=True, stop=False)
                                            ins = mm(o, bet, U[r, m, :], start=False, stop=True)
                                        else:
                                            mm(o, v, SC[r, m, 64:128], start=True, stop=False)
                                            ins = mm(o, U[r, m, :], SC[r, m, 192:256], start=False, stop=True)
                            end(ins, job, layer)

                def chain(c):
                    if c == 1:
                        for j in ("g0", "g1"):
                            pe.wait_ge(*read(j, layer))
                        pe.wait_ge(*at("first_state", layer))
                    else:
                        pe.wait_ge(*read(f"chain{c - 1}", layer))
                    b = begin(f"chain{c}", layer)
                    for p in range(2):
                        for hh in range(2):
                            r = slice(64 * hh, 64 * hh + 64)
                            ins = mm(b[r, p * N:(p + 1) * N], GT[r, p, c, :], ST[r, p, c, :], start=True, stop=True)
                    end(ins, f"chain{c}", layer)

                def chunk_y():
                    pe.wait_ge(*read(f"chain{NCH - 2}", layer))
                    for c in range(2):
                        pe.wait_ge(*read(f"q{c}", layer))
                    for p in range(2):
                        b = begin(f"y2{p}", layer)
                        for c in range(1, NCH):
                            for hh in range(2):
                                r = slice(64 * hh, 64 * hh + 64)
                                ins = mm(b[r, c * CH:(c + 1) * CH], ST[r, p, c, :], AR[r, 1, p, c * CH:(c + 1) * CH], start=True, stop=True)
                        end(ins, f"y2{p}", layer)

                def retain(h, kb):
                    p, hh = divmod(h, 2)
                    hr = slice(64 * hh, 64 * hh + 64)
                    w = T - kb * P
                    if h == 0 and kb == 0:
                        pe.wait_ge(*at("rotated", layer))
                        for q in range(2):
                            pe.wait_ge(*read(f"rows_rv{q}", layer))
                    b = begin(f"rs{h}{kb}", layer)
                    end(mm(b[:, 0:w], RK[hr, p, kb * P:(kb + 1) * P], RQ[hr, p, kb * P:T], start=True, stop=True), f"rs{h}{kb}", layer)
                    if (h * NT + kb) % 8:
                        retain_rest(h * NT + kb - 1)

                def retain_rest(u):
                    h, kb = divmod(u, NT)
                    p, hh = divmod(h, 2)
                    w = T - kb * P
                    pe.wait_ge(*read(f"rs{h}{kb}", layer))
                    yb = begin(f"ret_y{p}", layer) if u % 8 == 0 else ps(f"ret_y{p}", layer)
                    ins = mm(yb[64 * hh:64 * hh + 64, kb * P:T], rows["rv"][:, kb, h * N:(h + 1) * N], RSB[:, u % 2, 0:w],
                             start=kb == 0, stop=kb == NT - 1)
                    if u % 8 == 7:
                        end(ins, f"ret_y{p}", layer)

                def retain_out(p):
                    retain_rest(8 * p + 7)

                def ln_mean():
                    for p in range(2):
                        pe.wait_ge(*read(f"y2{p}", layer))
                        b = begin(f"mean{p}", layer)
                        end(mm(b[:, :], head_mean, Y1[:, p, :], start=True, stop=True), f"mean{p}", layer)

                def ln_var():
                    for p in range(2):
                        pe.wait_ge(*at("ln_sq", layer, p + 1))
                        b = begin(f"var{p}", layer)
                        end(mm(b[:, :], head_mean, LNS[:, p, :], start=True, stop=True), f"var{p}", layer)

                def ret_stat():
                    for p in range(2):
                        pe.wait_ge(*at("ret_sq", layer, p + 1))
                        b = begin(f"ret_ms{p}", layer)
                        end(mm(b[:, :], head_mean, RSQ[:, p, :], start=True, stop=True), f"ret_ms{p}", layer)

                def project_out(m):
                    project(f"out{m}")
                    if m > 0:
                        stat(layer, m - 1)
                    if m == KT - 1:
                        stat(layer, m)

                run = dict(shift=shift, copy=copy, gate=gate, conv_c=conv_c, conv_h=conv_h, conv_b=conv_b,
                           kk_square=kk_square, lora=lora, bonus=bonus, to_rows=to_rows, scores=scores,
                           inverse_x=inverse_x, inverse_y=inverse_y, rotate=rotate, attend=attend,
                           attend_out=attend_out, chunk_b=chunk_b, chunk_uw=chunk_uw, chunk_qghy=chunk_qghy,
                           chain=chain, chunk_y=chunk_y, retain=retain, retain_out=retain_out,
                           ln_mean=ln_mean, ln_var=ln_var, ret_stat=ret_stat, project_out=project_out)
                for name, *args in STEPS:
                    if name in run:
                        run[name](*args)

            for t in range(NT):
                for hf in range(2):
                    b = begin(f"row{t}{hf}", DEPTH)
                    for j in range(4):
                        m = 4 * hf + j
                        if t == 0:
                            pe.wait_ge(*at("h_raw", DEPTH, m + 1))
                        ins = pe.transpose(b[:, j * P:(j + 1) * P], half(13 + m // 2, m % 2)[:, t * P:(t + 1) * P], ident)
                    end(ins, f"row{t}{hf}", DEPTH)

        @block.scalar
        def _(act):
            go = act.activation
            act.wait_ge(s("const_b"), 16 * 4)
            for l in range(DEPTH):
                act.wait_ge(*full(f"params{l}", -1))
                go(par[:, l, :], ps(f"params{l}", -1)[:, 0:N_PAR], ACT.Copy).then_inc(done(f"params{l}", -1), 1)
            for h in range(HEADS):
                for j in range(2):
                    act.wait_ge(*full(f"bias_row{h}{j}", -1))
                    go(bias_rows[:, h, j * (DIST // 2):(j + 1) * (DIST // 2)], ps(f"bias_row{h}{j}", -1)[:, 0:DIST // 2], ACT.Copy)\
                        .then_inc(done(f"bias_row{h}{j}", -1), 1)

            def square_x(layer, m):
                if layer < 0:
                    act.wait_ge(*read(f"x_in{m}", -1))
                else:
                    act.wait_ge(*read(f"out{m}", layer))
                if m >= 2:
                    act.wait_ge(s("x_sq_used"), (layer + 1) * (KT - 1) + m - 1)
                elif layer >= 0:
                    act.wait_ge(*full("stat", layer - 1))
                go(half(24, m % 2), XY[:, m, :], ACT.Square).then_inc(s("x_sq"), 1)

            for m in range(KT):
                square_x(-1, m)

            for layer in range(DEPTH + 1):
                def root_of_mean():
                    act.wait_ge(*full("stat", layer - 1))
                    go(half(0, 0), ps("stat", layer - 1)[:, :], ACT.Sqrt, bias=const("eps")[:, 0:1]).then_inc(done("stat", layer - 1), 1)

                if layer == DEPTH:
                    root_of_mean()
                    for t in range(NT):
                        act.wait_ge(*full(f"row{t}0", DEPTH))
                        go(page(17 + t)[:, 0:T], ps(f"row{t}0", DEPTH)[:, :], ACT.Copy).then_inc(done(f"row{t}0", DEPTH), 1)
                    break

                def norm():
                    root_of_mean()
                    for k in range(KT):
                        act.wait_ge(*at("h_raw", layer, k + 1))
                        go(act_hi[:, k, :], half(13 + k // 2, k % 2), ACT.Copy).then_inc(s("h_hi"), 1)

                def shift(job):
                    act.wait_ge(*full(job, layer))
                    dst = {"k": K, "r": R, "v": V}[job[0]][:, int(job[1]), :] if job != "wa" else WA
                    n = 64 if job == "wa" else P
                    c = MUC + MU_ROW[job]
                    if job == "k0":
                        act.wait_ge(s("derived"), 5)
                    go(dst[0:n], ps(job, layer)[0:n, :], ACT.Identity, scale=der[0:n, layer, c:c + 1]).then_inc(done(job, layer), 1)

                def kk_square():
                    for p in range(2):
                        act.wait_ge(*read(f"k{p}", layer))
                        go(KN[:, p, :], K[:, p, :], ACT.Square, scale=par[:, layer, KKP + p:KKP + p + 1]).then_inc(s("kk_sq"), 1)

                def kk_norm():
                    for p in range(2):
                        act.wait_ge(*full(f"kk{p}", layer))
                        go(KN[:, p, :], ps(f"kk{p}", layer)[:, :], ACT.Sqrt, scale=64.0).then_inc(done(f"kk{p}", layer), 1)

                def lora_tanh():
                    act.wait_ge(*read("wa", layer))
                    go(WA[0:LORA], WA[0:LORA], ACT.Tanh).then_inc(s("lora_in"), 1)

                def lora():
                    for z, dst, c in (("zw", TH, HW0), ("za", TA, HA0)):
                        for p in range(2):
                            act.wait_ge(*full(f"{z}{p}", layer))
                            go(dst[:, p, :], ps(f"{z}{p}", layer)[:, :], ACT.Tanh, scale=0.5, bias=der[:, layer, c + p:c + p + 1])\
                                .then_inc(done(f"{z}{p}", layer), 1)

                def decay_exp():
                    for p in range(2):
                        act.wait_ge(*at("decay_sum", layer, p + 1))
                        src = TH[:, p, :].rearrange("p (c t) -> p c t", t=CH)
                        go(Pd[:, p, :, 1:CH + 1], src, ACT.Exp, scale=-0.5 * DECAY).then_inc(s("decay_exp"), 1)
                        go(PI[:, p, :], TH[:, p, :], ACT.Exp, scale=0.5 * DECAY).then_inc(s("decay_exp"), 1)

                def gate(group, p):
                    k = {"rwkv": 0, "conv": 2, "moba": 4, "ret": 6}[group] + p
                    job = f"{group}_g{p}"
                    act.wait_ge(*full(job, layer))
                    act.wait_ge(s("x_spill"), 16 * KT * (layer + 1))
                    go(XY[:, k, :], ps(job, layer)[:, :], ACT.Tanh, scale=0.5).then_inc(done(job, layer), 1)

                def copy(job):
                    act.wait_ge(*full(job, layer))
                    p = int(job[2])
                    if job in ("rq0", "mv0", "mq0", "mk0"):
                        free_for(job)
                    if job[:2] in ("rk", "rv"):
                        if job[:2] == "rk":
                            act.wait_ge(*at("rotated", layer, 1 + p))
                        else:
                            act.wait_ge(*at("rotated", layer, 3 + p))
                    dst = {"mq": MQ[:, p, :], "mk": MK[:, p, :], "mv": half(10, p)}.get(job[:2], half(8, p))
                    go(dst, ps(job, layer)[:, :], ACT.Copy).then_inc(done(job, layer), 1)

                def free_for(job):
                    if job == "mq0" and layer == 0:
                        act.wait_ge(s("bias_out"), 16)
                    if job == "mv0":
                        act.wait_ge(*full("za1", layer))
                    if job == "rq0":
                        act.wait_ge(*full("scores311", layer))
                        act.wait_ge(*full("rows_alp1", layer))

                def to_rows(what):
                    for p in range(2):
                        job = f"rows_{what}{p}"
                        act.wait_ge(*full(job, layer))
                        src = ps(job, layer)[:, :]
                        if what == "alp":
                            for t in range(NT):
                                ins = go(BA[:, t * HEADS + 2 * p:t * HEADS + 2 * p + 2, 1, :],
                                         src[:, t * P:(t + 1) * P].rearrange("p (h n) -> p h n", h=2), ACT.Copy)
                            ins.then_inc(done(job, layer), 1)
                        else:
                            if what == "rv" and p == 0:
                                act.wait_ge(*full("rows_mv1", layer))
                            go(rows[what][:, :, p * P:(p + 1) * P], src.rearrange("p (t c) -> p t c", t=NT), ACT.Copy).then_inc(done(job, layer), 1)

                def inverse_start():
                    act.wait_ge(*full("scores311", layer))
                    act.wait_ge(*at("rho", layer))
                    for m in range(2):
                        ins = go(TiT[:, 8 * m:8 * m + 8, :], const("eye64").unsqueeze(1).to_broadcast([P, 8, CH]), ACT.Copy)
                    ins.then_inc(s("eye_set"), 1)

                def inverse_x(n):
                    for g in range(2):
                        act.wait_ge(*full(f"x{n}_{g}", layer))
                        if n > LEVELS[1]:
                            act.wait_ge(*full(f"yt{n // 2}_{g}", layer))
                        go(Xm[:, 8 * g:8 * g + 8, :], ps(f"x{n}_{g}", layer)[:, :].rearrange("p (m c) -> p m c", m=8), ACT.Copy)\
                            .then_inc(done(f"x{n}_{g}", layer), 1)

                def attend(u):
                    w = (u % NT + 1) * P
                    act.wait_ge(*at("logit_max", layer, u + 1))
                    pb = half(1, u % 2)[:, 0:w]
                    go(pb, pb, ACT.Exp, bias=small[:, u % 2:u % 2 + 1], accum_out=small[:, 2 + u % 2:3 + u % 2]).then_inc(s("prob"), 1)
                    if u % 8:
                        attend_rest(u - 1)

                def attend_rest(u):
                    w = (u % NT + 1) * P
                    act.wait_ge(*full(f"pt{u}", layer))
                    go(half(7, u % 2)[:, 0:w], ps(f"pt{u}", layer)[:, 0:w], ACT.Copy).then_inc(done(f"pt{u}", layer), 1)

                def attend_out(p):
                    attend_rest(8 * p + 7)

                def conv_c(p):
                    act.wait_ge(*full(f"cc{p}", layer))
                    if p == 0:
                        act.wait_ge(*full("moba_y1", layer))
                    go(CU[:, p, 2:T + 2], ps(f"cc{p}", layer)[:, :], ACT.Copy).then_inc(done(f"cc{p}", layer), 1)

                def chunk_b():
                    for g in range(2):
                        act.wait_ge(*full(f"b{g}", layer))
                        go(BA[:, 8 * g:8 * g + 8, 0, :], ps(f"b{g}", layer)[:, :].rearrange("p (m c) -> p m c", m=8), ACT.Copy)\
                            .then_inc(done(f"b{g}", layer), 1)

                def chunk_uw():
                    for t in range(NT):
                        act.wait_ge(*full(f"uw{t}", layer))
                        go(UW[:, t * HEADS:(t + 1) * HEADS, :, :],
                           ps(f"uw{t}", layer)[:, :].rearrange("p (m x i) -> p m x i", m=HEADS, x=2), ACT.Copy)\
                            .then_inc(done(f"uw{t}", layer), 1)

                def chunk_qghy():
                    for c in range(2):
                        act.wait_ge(*full(f"y1{c}", layer))
                        for p in range(2):
                            ins = go(Y1[:, p, :].rearrange("p (t c i) -> p t c i", c=2, i=CH)[:, :, c, :],
                                     ps(f"y1{c}", layer)[:, p * 256:(p + 1) * 256].rearrange("p (t i) -> p t i", i=CH), ACT.Copy)
                        ins.then_inc(done(f"y1{c}", layer), 1)

                def retain(h, kb):
                    u = h * NT + kb
                    if kb < NT - 1:
                        act.wait_ge(*read(f"rs{h}{kb}", layer, 1))
                        w = T - kb * P
                        if u == 0:
                            act.wait_ge(*full("moba_y1", layer))
                        go(RSB[:, u % 2, P:w], ps(f"rs{h}{kb}", layer)[:, P:w], ACT.Copy, scale=const("k_decay")[:, u:u + 1])\
                            .then_inc(done(f"rs{h}{kb}", layer), 1)

                def retain_out(p):
                    act.wait_ge(*full(f"ret_y{p}", layer))
                    if p == 0:
                        act.wait_ge(*full("uw3", layer))
                    go(RSQ[:, p, :], ps(f"ret_y{p}", layer)[:, :], ACT.Square).then_inc(s("ret_sq"), 1)
                    go(RY[:, p, :], ps(f"ret_y{p}", layer)[:, :], ACT.Copy).then_inc(done(f"ret_y{p}", layer), 1)

                def ln_square():
                    for p in range(2):
                        act.wait_ge(*read(f"mean{p}", layer))
                        go(LNS[:, p, :], Y1[:, p, :], ACT.Square).then_inc(s("ln_sq"), 1)

                def roots():
                    for p in range(2):
                        act.wait_ge(*full(f"var{p}", layer))
                        go(LNS[:, p, :], ps(f"var{p}", layer)[:, :], ACT.Sqrt, bias=const("eps")[:, 1:2]).then_inc(done(f"var{p}", layer), 1)
                    for p in range(2):
                        act.wait_ge(*read(f"ret_ms{p}", layer))
                        go(RSQ[:, p, :], RSQ[:, p, :], ACT.Sqrt).then_inc(s("ret_root"), 1)

                def split_y():
                    act.wait_ge(*full("conv_g1", layer))
                    for k in Y_ORDER:
                        if k // 2 == 2:
                            act.wait_ge(*read(f"moba_y{k % 2}", layer))
                        else:
                            act.wait_ge(*at({0: "y_rwkv", 1: "y_conv", 3: "y_ret"}[k // 2], layer, k % 2 + 1))
                        go(act_hi[:, k, :], XY[:, k, :], ACT.Copy).then_inc(s("y_hi"), 1)

                def project_out(m):
                    square_x(layer, m)

                run = dict(norm=norm, shift=shift, kk_square=kk_square, kk_norm=kk_norm, lora_tanh=lora_tanh, lora=lora,
                           decay_exp=decay_exp, gate=gate, copy=copy, to_rows=to_rows, inverse_start=inverse_start,
                           inverse_x=inverse_x, attend=attend, attend_out=attend_out, conv_c=conv_c, chunk_b=chunk_b,
                           chunk_uw=chunk_uw, chunk_qghy=chunk_qghy, retain=retain, retain_out=retain_out,
                           ln_square=ln_square, roots=roots, split_y=split_y, project_out=project_out)
                for name, *args in STEPS:
                    if name in run:
                        run[name](*args)

        @block.vector
        def _(dve):
            tt, ts, stt = dve.tensor_tensor, dve.tensor_scalar, dve.scalar_tensor_tensor
            n_step = [0]

            def mark(ins):
                n_step[0] += 1
                ins.then_inc(s("dve_step"), 1)
                return n_step[0]

            def link(ins):
                dve.wait_ge(s("dve_step"), mark(ins))

            dve.wait_ge(s("const_b"), 16 * 4)
            for l in range(DEPTH):
                dve.wait_ge(*read(f"params{l}", -1))
            for c, n, src, a, b in ((MUC, 7, MU, -1.0, 1.0), (HW0, 2, W0, 0.5, 0.0), (HA0, 2, A0, 0.5, 0.0),
                                    (KA2, 2, KAP, 0.5, 0.0), (KA1, 2, KAP, -0.5, 1.0)):
                ts(der[:, :, c:c + n], par[:, :, src:src + n], a, b, ALU.mult, ALU.add).then_inc(s("derived"), 1)
            dve.wait_ge(s("derived"), 5)
            for m in range(KT):
                dve.wait_ge(*full(f"x_in{m}", -1))
                dve.tensor_copy(XY[:, m, :], ps(f"x_in{m}", -1)[:, :]).then_inc(done(f"x_in{m}", -1), 1)

            for layer in range(DEPTH + 1):
                def scaled(k, weight_col):
                    l = min(layer, DEPTH - 1)
                    stt(half(13 + k // 2, k % 2), XY[:, k, :], par[:, l, weight_col + k:weight_col + k + 1], half(0, 0), ALU.mult, ALU.mult)\
                        .then_inc(s("h_raw"), 1)

                def low(k):
                    dve.wait_ge(*at("h_hi", layer, k + 1))
                    tt(act_lo[:, k, :], half(13 + k // 2, k % 2), act_hi[:, k, :].bitcast(F32), ALU.subtract).then_inc(s("h_split"), 1)

                def norm():
                    dve.wait_ge(*read("stat", layer - 1))
                    link(dve.reciprocal(half(0, 0), half(0, 0)))
                    for k in range(KT):
                        scaled(k, NORMW)
                        if k >= 1:
                            low(k - 1)
                    low(KT - 1)

                if layer == DEPTH:
                    dve.wait_ge(*read("stat", layer - 1))
                    link(dve.reciprocal(half(0, 0), half(0, 0)))
                    for k in range(KT):
                        scaled(k, FNORM)
                    for t in range(NT):
                        dve.wait_ge(*full(f"row{t}1", DEPTH))
                        dve.tensor_copy(page(17 + t)[:, T:2 * T], ps(f"row{t}1", DEPTH)[:, :]).then_inc(done(f"row{t}1", DEPTH), 1)
                    break

                def pads():
                    dve.memset(Pd[:, :, :, 0:1], 1.0).then_inc(s("pads"), 1)

                def shift(job):
                    dve.wait_ge(*read(job, layer, 1))
                    dst = {"k": K, "r": R, "v": V}[job[0]][:, int(job[1]), :] if job != "wa" else WA
                    n = 64 if job == "wa" else P
                    c = MU + MU_ROW[job]
                    b = ps(job, layer)
                    stt(dst[0:n, 1:T], b[0:n, 0:T - 1], par[0:n, layer, c:c + 1], dst[0:n, 1:T], ALU.mult, ALU.add)\
                        .then_inc(done(job, layer), 1)

                def kk_norm():
                    for p in range(2):
                        dve.wait_ge(*read(f"kk{p}", layer))
                    link(ts(KN, KN, 1e-12, None, ALU.max))
                    link(dve.reciprocal(KN, KN))
                    for p in range(2):
                        stt(KN[:, p, :], K[:, p, :], par[:, layer, KKP + p:KKP + p + 1], KN[:, p, :], ALU.mult, ALU.mult).then_inc(s("kk_unit"), 1)

                def decay_scan():
                    for p in range(2):
                        dve.wait_ge(*read(f"zw{p}", layer))
                    link(ts(TH, TH, 1.0, None, ALU.add))
                    for p in range(2):
                        dve.tensor_tensor_scan(TH[:, p, :], const("chunk_reset"), TH[:, p, :], 0.0, ALU.mult, ALU.add).then_inc(s("decay_sum"), 1)

                def factors():
                    for p in range(2):
                        dve.wait_ge(*read(f"za{p}", layer))
                    for p in range(2):
                        c = mark(ts(KF[:, p, :], TA[:, p, :], der[:, layer, KA2 + p:KA2 + p + 1], der[:, layer, KA1 + p:KA1 + p + 1], ALU.mult, ALU.add))
                    dve.wait_ge(*at("kk_unit", layer))
                    dve.wait_ge(s("dve_step"), c)
                    d = mark(stt(TA, TA, 1.0, KN, ALU.add, ALU.mult))
                    e = mark(tt(K, K, KF, ALU.mult))
                    dve.wait_ge(*at("decay_exp", layer))
                    dve.wait_ge(s("dve_step"), d)
                    stt(TA, TA, -0.5, PI, ALU.mult, ALU.mult).then_inc(s("beta"), 1)
                    dve.wait_ge(*at("pads", layer))
                    dve.wait_ge(s("dve_step"), e)
                    dve.wait_ge(*at("beta", layer))
                    tt(PI, K, PI, ALU.mult).then_inc(s("kappa"), 1)
                    flat = Pd.rearrange("p a c t -> p (a c) t")
                    chunks = lambda v: v.rearrange("p a (c t) -> p (a c) t", t=CH)
                    tt(chunks(AR[:, 0]), chunks(KN), flat[:, :, 0:CH], ALU.mult).then_inc(s("alpha"), 1)
                    tt(chunks(AR[:, 1]), chunks(R), flat[:, :, 1:CH + 1], ALU.mult).then_inc(s("rho"), 1)
                    mark(dve.tensor_copy(w_end[:].rearrange("p a c -> p (a c)").unsqueeze(2), flat[:, :, CH:CH + 1]))
                    dve.wait_ge(*at("rho", layer))
                    for p in range(2):
                        stt(R[:, p, :], R[:, p, :], par[:, layer, RKP + p:RKP + p + 1], K[:, p, :], ALU.mult, ALU.mult).then_inc(s("rkv"), 1)

                def bonus():
                    for p in range(2):
                        dve.wait_ge(*full(f"bonus{p}", layer))
                        stt(R[:, p, :], ps(f"bonus{p}", layer)[:, :], 64.0, V[:, p, :], ALU.mult, ALU.mult).then_inc(done(f"bonus{p}", layer), 1)

                def gate(group, p):
                    k = {"rwkv": 0, "conv": 2, "moba": 4, "ret": 6}[group] + p
                    job = f"{group}_g{p}"
                    dve.wait_ge(*read(job, layer, 1))
                    stt(XY[:, k, :], XY[:, k, :], 1.0, ps(job, layer)[:, :], ALU.add, ALU.mult).then_inc(done(job, layer), 1)

                def scores(t):
                    for p in range(2):
                        for hh in range(2):
                            job = f"scores{t}{p}{hh}"
                            dve.wait_ge(*full(job, layer))
                            tt(SC[:, t * HEADS + 2 * p + hh, :], ps(job, layer)[:, 0:320], const("score_mask"), ALU.mult).then_inc(done(job, layer), 1)

                def mask(level, transposed, n):
                    return lmask[:, transposed, LEVELS.index(level), :].unsqueeze(1).to_broadcast([P, n, CH])

                def inverse_start():
                    dve.wait_ge(*read("scores311", layer))
                    link(dve.tensor_copy(Ti, const("eye64").unsqueeze(1).to_broadcast([P, MATS, CH])))
                    dve.copy_predicated(Ti, mask(1, 0, MATS), SC[:, :, 256:320]).then_inc(s("t_init"), 1)
                    dve.wait_ge(*at("eye_set", layer))
                    dve.copy_predicated(TiT, mask(1, 1, MATS), SC[:, :, 128:192]).then_inc(s("tt_init"), 1)

                def inverse_y(n):
                    for g in range(2):
                        m8 = slice(8 * g, 8 * g + 8)
                        if n != LEVELS[-1]:
                            dve.wait_ge(*full(f"y{n}_{g}", layer))
                            dve.copy_predicated(Ti[:, m8, :], mask(n, 0, 8), ps(f"y{n}_{g}", layer)[:, :].rearrange("p (m c) -> p m c", m=8))\
                                .then_inc(done(f"y{n}_{g}", layer), 1)
                        dve.wait_ge(*full(f"yt{n}_{g}", layer))
                        dve.copy_predicated(TiT[:, m8, :], mask(n, 1, 8), ps(f"yt{n}_{g}", layer)[:, :].rearrange("p (m c) -> p m c", m=8))\
                            .then_inc(done(f"yt{n}_{g}", layer), 1)

                def rotate(job):
                    p = int(job[-1])
                    j = ["rq0", "rq1", "rk0", "rk1"].index(job)
                    dst = (RQ if job[1] == "q" else RK)[:, p, :]
                    dve.wait_ge(*full(f"rot_{job}", layer))
                    if j == 0:
                        dve.wait_ge(*full("rows_v1", layer))
                    c = mark(tt(dst, half(8, p), const("cos"), ALU.mult))
                    dve.wait_ge(s("dve_step"), c)
                    tt(half(8, p), ps(f"rot_{job}", layer)[:, :], const("sin"), ALU.mult).then_inc(done(f"rot_{job}", layer), 1)
                    dve.wait_ge(*read(f"rot_{job}", layer))
                    tt(dst, dst, half(8, p), ALU.add).then_inc(s("rotated"), 1)

                def attend(u):
                    h, qb = divmod(u, NT)
                    w = (qb + 1) * P
                    pb = half(1, u % 2)[:, 0:w]
                    if layer == 0 and u == 0:
                        dve.wait_ge(s("bias_back"), 16)
                    dve.wait_ge(*full(f"s{u}", layer))
                    if u >= 2:
                        dve.wait_ge(*full(f"pt{u - 2}", layer))
                    stt(pb, ps(f"s{u}", layer)[:, 0:w], 0.125, bias[:, h, T - w:T], ALU.mult, ALU.add).then_inc(done(f"s{u}", layer), 1)
                    dve.wait_ge(*read(f"s{u}", layer))
                    dve.tensor_reduce(small[:, u % 2:u % 2 + 1], pb, AX_X, ALU.max, negate=True).then_inc(s("logit_max"), 1)
                    if u % 8:
                        attend_rest(u - 1)

                def attend_rest(u):
                    pb = half(1, u % 2)[:, 0:(u % NT + 1) * P]
                    dve.wait_ge(*at("prob", layer, u + 1))
                    r = small[:, 4 + u % 2:5 + u % 2]
                    link(dve.reciprocal(r, small[:, 2 + u % 2:3 + u % 2]))
                    ts(pb, pb, r, None, ALU.mult).then_inc(s("prob_norm"), 1)

                def attend_out(p):
                    attend_rest(8 * p + 7)
                    dve.wait_ge(*full(f"moba_y{p}", layer))
                    finish_tile(4 + p, ps(f"moba_y{p}", layer)[:, :]).then_inc(done(f"moba_y{p}", layer), 1)

                def finish_tile(k, y):
                    return stt(XY[:, k, :], y, 0.5, XY[:, k, :], ALU.mult, ALU.mult)

                def conv_c(p):
                    if p == 0:
                        dve.wait_ge(*full("moba_y1", layer))
                        dve.memset(CU[:, :, 0:2], 0.0).then_inc(s("conv_pad"), 1)

                def conv_h(p):
                    dve.wait_ge(*full(f"ch{p}", layer))
                    dve.wait_ge(*read(f"cc{p}", layer))
                    tt(CU[:, p, 2:T + 2], CU[:, p, 2:T + 2], ps(f"ch{p}", layer)[:, :], ALU.mult).then_inc(done(f"ch{p}", layer), 1)
                    dve.wait_ge(*read(f"ch{p}", layer))
                    dve.wait_ge(*at("conv_pad", layer))
                    w = lambda j: par[:, layer, CONVW + 2 * j + p:CONVW + 2 * j + p + 1]
                    link(ts(CA[:, p, :], CU[:, p, 0:T], w(0), None, ALU.mult))
                    for j in (1, 2):
                        link(stt(CA[:, p, :], CU[:, p, j:T + j], w(j), CA[:, p, :], ALU.mult, ALU.add))

                def conv_b(p):
                    dve.wait_ge(*full(f"cb{p}", layer))
                    tt(CA[:, p, :], CA[:, p, :], ps(f"cb{p}", layer)[:, :], ALU.mult).then_inc(done(f"cb{p}", layer), 1)

                def conv_out():
                    for p in range(2):
                        dve.wait_ge(*read(f"conv_g{p}", layer))
                        dve.wait_ge(*read(f"cb{p}", layer))
                        finish_tile(2 + p, CA[:, p, :]).then_inc(s("y_conv"), 1)

                def chunk_qghy():
                    par8 = lambda v, c: v.rearrange("p a (t x) i -> p a t x i", x=2)[:, :, :, c, :]
                    src = lambda j: ps(j, layer)[:, :].rearrange("p (a t i) -> p a t i", a=2, i=N)
                    for c in range(2):
                        dve.wait_ge(*full(f"g{c}", layer))
                        for p in range(2):
                            ins = tt(par8(GT, c)[:, p], src(f"g{c}")[:, p], const("eye64").unsqueeze(1).to_broadcast([P, NT, N]), ALU.add)
                        ins.then_inc(done(f"g{c}", layer), 1)
                    we = w_end[:].rearrange("p a (t x) -> p a t x", x=2)
                    for c in range(2):
                        dve.wait_ge(*full(f"h{c}", layer))
                        for p in range(2):
                            ins = tt(par8(HP, c)[:, p], src(f"h{c}")[:, p], we[:, p, :, c].unsqueeze(2).to_broadcast([P, NT, N]), ALU.mult)
                        ins.then_inc(done(f"h{c}", layer), 1)
                    for c in range(2):
                        dve.wait_ge(*read(f"h{c}", layer))
                    dve.tensor_copy(ST[:, :, 1, :], HP[:, :, 0, :]).then_inc(s("first_state"), 1)
                    rho = AR[:, 1].rearrange("p a (t x i) -> p a t x i", x=2, i=CH)
                    for c in range(2):
                        dve.wait_ge(*full(f"q{c}", layer))
                        for p in range(2):
                            ins = tt(rho[:, p, :, c, :], rho[:, p, :, c, :], src(f"q{c}")[:, p], ALU.add)
                        ins.then_inc(done(f"q{c}", layer), 1)

                def chain(c):
                    dve.wait_ge(*full(f"chain{c}", layer))
                    b = ps(f"chain{c}", layer)
                    for p in range(2):
                        ins = stt(ST[:, p, c + 1, :], b[:, p * N:(p + 1) * N], w_end[:, p, c:c + 1], HP[:, p, c, :], ALU.mult, ALU.add)
                    ins.then_inc(done(f"chain{c}", layer), 1)

                def chunk_y():
                    for c in range(2):
                        dve.wait_ge(*read(f"y1{c}", layer))
                    for p in range(2):
                        dve.wait_ge(*full(f"y2{p}", layer))
                        tt(Y1[:, p, CH:T], Y1[:, p, CH:T], ps(f"y2{p}", layer)[:, CH:T], ALU.add).then_inc(done(f"y2{p}", layer), 1)

                def retain(h, kb):
                    u = h * NT + kb
                    dve.wait_ge(*full(f"rs{h}{kb}", layer))
                    if u == 0:
                        dve.wait_ge(*full("moba_y1", layer))
                    stt(RSB[:, u % 2, 0:P], ps(f"rs{h}{kb}", layer)[:, 0:P], const("k_decay")[:, u:u + 1], const("causal"), ALU.mult, ALU.mult)\
                        .then_inc(done(f"rs{h}{kb}", layer), 1)

                def ln_mean():
                    for p in range(2):
                        dve.wait_ge(*full(f"mean{p}", layer))
                        tt(Y1[:, p, :], Y1[:, p, :], ps(f"mean{p}", layer)[:, :], ALU.subtract).then_inc(done(f"mean{p}", layer), 1)

                def ret_stat():
                    for p in range(2):
                        dve.wait_ge(*full(f"ret_ms{p}", layer))
                        tt(RSQ[:, p, :], ps(f"ret_ms{p}", layer)[:, :], const("ret_eps")[:, p * T:(p + 1) * T], ALU.add).then_inc(done(f"ret_ms{p}", layer), 1)

                def finish():
                    for p in range(2):
                        dve.wait_ge(*read(f"var{p}", layer))
                    a = mark(dve.reciprocal(LNS, LNS))
                    dve.wait_ge(*at("ret_root", layer))
                    b = mark(dve.reciprocal(RSQ, RSQ))
                    dve.wait_ge(s("dve_step"), a)
                    a = mark(tt(Y1, Y1, LNS, ALU.mult))
                    for p in range(2):
                        dve.wait_ge(*read(f"ret_y{p}", layer))
                    dve.wait_ge(s("dve_step"), b)
                    b = mark(tt(RY, RY, RSQ, ALU.mult))
                    dve.wait_ge(s("dve_step"), a)
                    for p in range(2):
                        a = mark(ts(Y1[:, p, :], Y1[:, p, :], par[:, layer, LNW + p:LNW + p + 1], par[:, layer, LNB + p:LNB + p + 1], ALU.mult, ALU.add))
                    dve.wait_ge(s("dve_step"), b)
                    for p in range(2):
                        finish_tile(6 + p, RY[:, p, :]).then_inc(s("y_ret"), 1)
                    dve.wait_ge(s("dve_step"), a)
                    a = mark(tt(Y1, Y1, R, ALU.add))
                    dve.wait_ge(s("dve_step"), a)
                    for p in range(2):
                        finish_tile(p, Y1[:, p, :]).then_inc(s("y_rwkv"), 1)

                def split_y():
                    for n, k in enumerate(Y_ORDER):
                        dve.wait_ge(*at("y_hi", layer, n + 1))
                        tt(act_lo[:, k, :], XY[:, k, :], act_hi[:, k, :].bitcast(F32), ALU.subtract).then_inc(s("y_split"), 1)

                def project_out(m):
                    dve.wait_ge(*full(f"out{m}", layer))
                    dve.wait_ge(s(f"x_back{m}"), 16 * (layer + 1))
                    tt(XY[:, m, :], XY[:, m, :], ps(f"out{m}", layer)[:, :], ALU.add).then_inc(done(f"out{m}", layer), 1)

                run = dict(norm=norm, shift=shift, kk_norm=kk_norm, decay_scan=decay_scan, factors=factors, bonus=bonus,
                           gate=gate, scores=scores, inverse_start=inverse_start, inverse_y=inverse_y, rotate=rotate,
                           attend=attend, attend_out=attend_out, conv_c=conv_c, conv_h=conv_h, conv_b=conv_b,
                           conv_out=conv_out, chunk_qghy=chunk_qghy, chain=chain, chunk_y=chunk_y, retain=retain,
                           ln_mean=ln_mean, ret_stat=ret_stat, finish=finish, split_y=split_y, project_out=project_out,
                           decay_exp=pads)
                for name, *args in STEPS:
                    if name in run:
                        run[name](*args)


def shape_constants():
    c = {}
    i = np.arange(P)
    c["ident"] = np.eye(P)
    c["head_mean"] = (i[:, None] // N == i[None, :] // N) / N
    c["all_mean"] = np.full((P, P), 1.0 / D)
    rot = np.zeros((P, P))
    rot[i[1::2], i[0::2]] = -1.0
    rot[i[0::2], i[1::2]] = 1.0
    c["rot"] = rot
    c["causal"] = i[:, None] <= i[None, :]
    a, b = np.arange(P)[:, None] % CH, np.arange(CH)[None, :]
    c["score_mask"] = np.concatenate([a < b, a <= b, a < b, a <= b, b < a], axis=1)
    c["eye64"] = a == b
    gamma = 1.0 - 2.0 ** (-5.0 - np.arange(HEADS))
    pos = np.arange(T)
    c["k_decay"] = np.stack([gamma[h] ** -(kb * P + i.astype(np.float64)) * N ** -0.5 for h in range(HEADS) for kb in range(NT)], axis=1)
    c["eps"] = np.tile([[NORM_EPS, LNX_EPS]], (P, 1))
    c["chunk_reset"] = np.tile(pos % CH != 0, (P, 1))
    theta = (1.0 / (10000.0 ** np.linspace(0.0, 1.0, N // 2, dtype=np.float32))).astype(np.float32)
    angle = (pos.astype(np.float32)[None, :] * theta[:, None]).astype(np.float32).astype(np.float64)
    angle = angle[(i % N) // 2]
    c["cos"], c["sin"] = np.cos(angle), np.sin(angle)
    c["ret_eps"] = np.concatenate([NORM_EPS * gamma[2 * p + i[:, None] // N] ** (-2.0 * pos[None, :]) for p in range(2)], axis=1)
    consts = np.concatenate([np.asarray(c[n], np.float32) for n, _ in CONSTS], axis=1)
    levels = np.stack([(a // (2 * n) == b // (2 * n)) & (a // n % 2 == 1) & (b // n % 2 == 0) for n in LEVELS], axis=1)
    levels_t = np.stack([(a // (2 * n) == b // (2 * n)) & (a // n % 2 == 0) & (b // n % 2 == 1) for n in LEVELS], axis=1)
    level_masks = np.stack([levels, levels_t], axis=1).reshape(P, -1).astype(np.int32)
    dist = T - 1 - np.arange(DIST)
    exact = BUCKETS // 2
    d_f = np.maximum(dist, 1).astype(np.float32)
    large = exact + (np.log(d_f / exact) / math.log(P / exact) * (BUCKETS - exact)).astype(np.int32)
    bucket = np.where(dist < exact, dist, np.minimum(large, BUCKETS - 1))
    bucket = np.where(dist < 0, BUCKETS, bucket)
    onehot = np.zeros((BUCKETS + 1, DIST + HEADS), np.float32)
    onehot[bucket, np.arange(DIST)] = 1.0
    onehot[BUCKETS, DIST:] = MASKED
    return consts, level_masks, onehot


_INS = ["x", "norm_w", "w_in", "w_out", "rwkv_mu", "rwkv_w0", "rwkv_w2", "rwkv_a0", "rwkv_a2", "rwkv_k_k",
        "rwkv_k_a", "rwkv_r_k", "rwkv_lnx_w", "rwkv_lnx_b", "conv_w", "rel_bias", "final_norm_w"]


def kernel(**inputs):
    import numpy as _np
    import concourse.bacc as _bacc
    from concourse.bass_utils import run_bass_kernel_spmd as _run

    nc = _bacc.Bacc("TRN2", target_bir_lowering=False, num_devices=1)
    arrays, args = {}, []

    def give(name, a):
        a = _np.ascontiguousarray(a)
        arrays[f"in_{name}_dram"] = a
        args.append(nc.dram_tensor(f"in_{name}_dram", a.shape, mybir.dt.from_np(a.dtype), kind="ExternalInput").ap())

    for name in _INS:
        give(name, inputs[name])
    for name, a in zip(("consts", "level_masks", "bucket_onehot"), shape_constants()):
        give(name, a)
    args.append(nc.dram_tensor("x_scratch", (KT, P, T), F32, kind="Internal").ap())
    args.append(nc.dram_tensor("bias_scratch", (HEADS, P, DIST + 1), F32, kind="Internal").ap())
    args.append(nc.dram_tensor("out_0_dram", (1, T, D), F32, kind="ExternalOutput").ap())
    trunk_kernel(nc, *args)
    r = _run(nc, [arrays], core_ids=[0])
    return r.results[0]["out_0_dram"]
```

```python
import math
from contextlib import ExitStack

import numpy as np

import concourse.bass as bass
from concourse import mybir

F32 = mybir.dt.float32
F32R = mybir.dt.float32r
I32 = mybir.dt.int32
U8 = mybir.dt.uint8
ALU = mybir.AluOpType
ACT = mybir.ActivationFunctionType
AX_X = mybir.AxisListType.X

P = 128
DEPTH = 2
T = 512
D = 1024
G = 256
HEADS = 4
N = 64
NT = T // P
KT = D // P
CH = 64
NCH = T // CH
MATS = NT * HEADS
LORA = 32
BUCKETS = 32
DECAY = math.exp(-0.5)
NORM_EPS = 1e-6
LNX_EPS = 64e-5
MASKED = -1e30
BLK = 16
LEVELS = [16, 32]
RAW, HI, LO = 3, 3, 3
DIST = T + P

RWKV, CONV, MOBA, RET = 0, 1088, 2112, 3136
TILE_COLS = {"wa": 768, "rwkv_g0": 832, "rwkv_g1": 960}
for _base, _names in ((RWKV, ("r", "k", "v")), (CONV, ("cb", "cc", "ch", "conv_g")),
                      (MOBA, ("mq", "mk", "mv", "moba_g")), (RET, ("rq", "rk", "rv", "ret_g"))):
    for _i, _n in enumerate(_names):
        for _p in range(2):
            TILE_COLS[f"{_n}{_p}"] = _base + G * _i + P * _p
TILES = ["k0", "k1", "wa", "r0", "r1", "v0", "v1", "rwkv_g0", "rwkv_g1",
         "rq0", "rq1", "rk0", "rk1", "rv0", "rv1", "ret_g0", "ret_g1",
         "mq0", "mq1", "mk0", "mk1", "mv0", "mv1", "moba_g0", "moba_g1",
         "cc0", "cc1", "ch0", "ch1", "cb0", "cb1", "conv_g0", "conv_g1"]
LAST_TILE = TILES[-1]
OUT_TILES = [f"out{m}" for m in range(KT)]
STREAM = TILES + OUT_TILES

MU, W0, A0, KKP, KAP, RKP, LNW, LNB, CONVW, NORMW = 0, 7, 9, 11, 13, 15, 17, 19, 21, 27
N_ROWS, N_PAR = 27, 35
MU_ROW = {"r0": 0, "r1": 1, "k0": 2, "k1": 3, "v0": 4, "v1": 5, "wa": 6}
MUC, HW0, HA0, KA2, KA1 = 0, 7, 9, 11, 13
N_DER = 15

CONSTS = [("ident", 128), ("eps", 2), ("one", 1), ("head_mean", 128), ("all_mean", 1), ("rot", 128), ("causal", 128),
          ("score_mask", 256), ("eye64", 64), ("k_decay", 16),
          ("chunk_reset", 512), ("cos", 512), ("sin", 512)]
COL, _at = {}, 0
for _n, _w in CONSTS:
    COL[_n] = (_at, _at + _w)
    _at += _w
N_CONST = _at

def layer_steps():
    s = [("norm",), ("k_pair",)]
    s += [("shift", "k0"), ("shift", "k1"), ("kk_input",), ("shift", "wa"), ("kk_square",), ("shift", "r0"),
          ("kk_norm",), ("lora_tanh",), ("shift", "r1"), ("lora",), ("shift", "v0"), ("decay_scan",), ("shift", "v1"),
          ("decay_exp",), ("gate", "rwkv", 0), ("factors",), ("gate", "rwkv", 1)]
    s += [("copy", "rq0"), ("copy", "rq1"), ("bonus",), ("rotate", "rq0"), ("to_rows", "v"), ("copy", "rk0"), ("rotate", "rq1"),
          ("to_rows", "kap"), ("copy", "rk1"), ("rotate", "rk0"), ("to_rows", "bet"), ("copy", "rv0"), ("rotate", "rk1"),
          ("to_rows", "alp"), ("copy", "rv1"), ("scores", 0), ("scores", 1), ("to_rows", "rv"), ("gate", "ret", 0),
          ("scores", 2), ("scores", 3), ("gate", "ret", 1)]
    halves = []
    for kind, job in [("copy", j) for j in ("mq0", "mq1", "mk0", "mk1", "mv0", "mv1")] + [(("gate", "moba", 0), 0), (("gate", "moba", 1), 0)] \
            + [(("conv_c", 0), 0), (("conv_c", 1), 0), (("conv_h", 0), 0), (("conv_h", 1), 0), (("conv_b", 0), 0), (("conv_b", 1), 0),
               (("gate", "conv", 0), 0), (("gate", "conv", 1), 0)]:
        step = (kind, job) if kind == "copy" else kind
        halves += [("first_half", project_name(step)), step]
    between = [[] for _ in halves]
    for i in range(9):
        between[i].append(("retain", i))
    for i in range(3):
        between[i].append(("block_rows", i))
    between[3] += [("chunk_b",)]
    between[4] += [("retain_out", 0)]
    for i, step in enumerate([("inverse_x", 16), ("inverse_y", 16), ("inverse_yt", 16), ("inverse_x", 32), ("inverse_yt", 32)]):
        between[6 + i].insert(0, step)
    between[8] += [("retain_out", 1)]
    between[9] += [("ret_stat",)]
    between[10] += [("ret_root",), ("ret_recip", 0)]
    between[11] += [("chunk_uw",), ("to_rows", "mv")]
    before = {1: [("chunk_g",)], 2: [("chunk_h", 0)], 3: [("chunk_h", 1)], 4: [("chunk_q",), ("chain", 1)],
              5: [("chunk_y1", 0), ("chain", 2)], 6: [("chunk_y1", 1), ("chain", 3)], 7: [("chain", 4)], 8: [("chain", 5)],
              9: [("chain", 6)], 10: [("chunk_y",)], 11: [("ln_mean",)], 12: [("ln_var",)]}
    after = {0: [("ret_recip", 1)], 1: [("ret_recip", 2)], 2: [("ret_recip", 3)], 4: [("ret_finish",)],
             11: [("ln_square",)], 12: [("ln_recip", 0)], 13: [("ln_recip", 1)],
             14: [("ln_recip", 2)], 15: [("ln_recip", 3)], 16: [("ln_scale", 0), ("ln_scale", 1)], 17: [("rwkv_finish", 0), ("rwkv_finish", 1)]}
    for g in range(18):
        between[11 + g] += before.get(g, [])
        between[11 + g] += [("attend", g)]
        if g in (9, 17):
            between[11 + g].append(("attend_out", g // 10))
        between[11 + g] += after.get(g, [])
    for h, extra in zip(halves, between):
        s += [h] + extra
    s = s[:-1] + [("second_half", "conv_g1")] + [("split_y", k) for k in Y_ORDER[:6]] + [s[-1]]
    s += [("conv_out",)] + [("split_y", k) for k in Y_ORDER[6:]] + [("project_out", m) for m in range(KT)]
    return s


def project_name(step):
    kind = step[0]
    if kind == "gate":
        return f"{step[1]}_g{step[2]}"
    if kind in ("conv_c", "conv_h", "conv_b"):
        return {"conv_c": "cc", "conv_h": "ch", "conv_b": "cb"}[kind] + str(step[1])
    return step[1]


Y_ORDER = [6, 7, 4, 5, 0, 1, 2, 3]
STEPS = layer_steps()


def bank_jobs():
    pro = [("norm_cols", 7, 1)] + [(f"x_in{m}", m, 1) for m in range(KT)] + [("params0", 3, 1), ("params1", 4, 1)]
    layer = []
    projections = []

    def proj(name, readers):
        if name not in projections:
            layer.append((name, len(projections) % 2, readers))
            projections.append(name)

    turn = [0]

    def any6(name, readers=1, banks=(2, 3, 4, 5, 6, 7)):
        layer.append((name, banks[turn[0] % len(banks)], readers))
        turn[0] += 1

    for step in STEPS:
        kind = step[0]
        if kind == "norm":
            layer.append(("rn", 2, 0))
        elif kind == "k_pair":
            proj("k0", 2), proj("k1", 2)
        elif kind == "first_half":
            proj(step[1], 2 if "_g" in step[1] else 1)
        elif kind == "shift":
            proj(step[1], 2)
        elif kind == "copy":
            proj(step[1], 1)
        elif kind == "gate":
            proj(f"{step[1]}_g{step[2]}", 2)
        elif kind == "kk_square":
            any6("kk0"), any6("kk1")
        elif kind == "lora":
            for n in ("zw0", "zw1", "za0", "za1"):
                any6(n)
        elif kind == "bonus":
            any6("bonus0"), any6("bonus1")
        elif kind == "to_rows":
            for p in range(2):
                if step[1] == "mv":
                    layer.append((f"rows_mv{p}", 7 - 2 * p, 1))
                else:
                    any6(f"rows_{step[1]}{p}")
        elif kind == "scores":
            for p in range(2):
                for hh in range(2):
                    any6(f"scores{step[1]}{p}{hh}")
        elif kind == "inverse_x":
            layer += [(f"x{step[1]}_0", 5, 1), (f"x{step[1]}_1", 6, 1)]
        elif kind == "inverse_y":
            layer += [(f"y{step[1]}_0", 5, 1), (f"y{step[1]}_1", 6, 1)]
        elif kind == "inverse_yt":
            layer += [(f"yt{step[1]}_0", 7, 1), (f"yt{step[1]}_1", 5, 1)]
        elif kind == "rotate":
            any6(f"rot_{step[1]}")
        elif kind == "attend":
            g = step[1]
            if g == 2 or g == 10:
                layer.append((f"moba_y{g // 10}", 4, 1))
            if 1 <= g <= 16:
                layer.append((f"pt{g - 1}", 3, 1))
            if g <= 15:
                layer.append((f"s{g}", 2, 1))
        elif kind == "chunk_b":
            layer += [("b0", 5, 1), ("b1", 6, 1)]
        elif kind == "chunk_uw":
            layer += [(f"uw{t}", (7, 5, 6, 7)[t], 1) for t in range(NT)]
        elif kind == "chunk_g":
            layer += [("g0", 5, 1), ("g1", 6, 1)]
        elif kind == "chunk_h":
            layer.append((f"h{step[1]}", 7 - 2 * step[1], 1))
        elif kind == "chunk_q":
            layer += [("q0", 6, 1), ("q1", 7, 1)]
        elif kind == "chunk_y1":
            layer.append((f"y1{step[1]}", 5 + step[1], 1))
        elif kind == "chain":
            layer.append((f"chain{step[1]}", 7, 1))
        elif kind == "chunk_y":
            layer += [("y20", 5, 1), ("y21", 6, 1)]
        elif kind == "retain":
            i = step[1]
            if i == 1 or i == 5:
                layer.append((f"ret_y{i // 5}", 4, 1))
            if i < 8:
                layer += [(f"rs{u}", 2 + u % 2, 2 if u % NT < NT - 1 else 1) for u in (2 * i, 2 * i + 1)]
        elif kind == "ln_mean":
            layer += [("mean0", 5, 1), ("mean1", 6, 1)]
        elif kind == "ln_var":
            layer += [("var0", 7, 1), ("var1", 5, 1)]
        elif kind == "ret_stat":
            layer += [("ret_ms0", 2, 1), ("ret_ms1", 3, 1)]
        elif kind == "project_out":
            proj(f"out{step[1]}", 1)
            if step[1] == KT - 1:
                layer.append(("stat", 2, 1))
    epi = [(f"row{m}", 3 + m % 5, 1) for m in range(KT)]
    return pro, layer, epi


def trunk_kernel(nc, x, norm_w, w_in, w_out, rwkv_mu, rwkv_w0, rwkv_w2, rwkv_a0, rwkv_a2, rwkv_k_k,
                 rwkv_k_a, rwkv_r_k, rwkv_lnx_w, rwkv_lnx_b, conv_w, rel_bias, final_norm_w,
                 consts, level_masks, ret_eps, x_scratch, bias_scratch, a_scratch, t_scratch, tt_scratch, out):
    pro, per_layer, epi = bank_jobs()
    place = {}
    full_count, read_count = [0] * 8, [0] * 8
    for part, names in (("pro", pro), ("layer", per_layer), ("epi", epi)):
        if part == "layer":
            pro_full, pro_read = list(full_count), list(read_count)
            full_count, read_count = [0] * 8, [0] * 8
        if part == "epi":
            lay_full, lay_read = list(full_count), list(read_count)
            full_count, read_count = [0] * 8, [0] * 8
        for name, bank, readers in names:
            place[part, name] = (bank, full_count[bank], read_count[bank], readers)
            full_count[bank] += 1
            read_count[bank] += readers

    def locate(name, layer):
        part = "pro" if layer < 0 else "epi" if layer >= DEPTH else "layer"
        bank, nf, nr, readers = place[part, name]
        if part != "pro":
            nf += pro_full[bank] + layer * lay_full[bank]
            nr += pro_read[bank] + layer * lay_read[bank]
        return bank, nf, nr, readers

    with ExitStack() as ctx:
        def sb(name, shape, dt=F32):
            return ctx.enter_context(nc.sbuf_tensor(name, shape, dt))

        bank = [ctx.enter_context(nc.psum_tensor(f"bank{i}", [P, 512], F32)) for i in range(8)]
        XY = sb("x_or_y", [P, KT, T])
        act_hi = sb("act_hi", [P, KT, T], F32R)
        act_lo = sb("act_lo", [P, KT, T], F32R)
        w_raw = sb("w_raw", [P, RAW, KT, P])
        w_hi = sb("w_hi", [P, HI, KT, P], F32R)
        w_lo = sb("w_lo", [P, LO, KT, P], F32R)
        PG = 1040
        pages = sb("pages", [P, 25 * PG])
        cst = sb("constants", [P, N_CONST])
        lmask = sb("level_mask", [P, 2, len(LEVELS), CH], U8)
        bias = sb("bias", [P, HEADS, T])
        par = sb("params", [P, DEPTH, N_PAR])
        der = sb("params_derived", [P, DEPTH, N_DER])
        lora_w = sb("lora_w", [2 * LORA, DEPTH, G])
        small = sb("small", [P, 32])
        w_end = sb("chunk_decay", [P, 2, NCH])

        def page(i, n=1):
            return pages[:, i * PG:(i + n - 1) * PG + 1024]

        def pair(i):
            return page(i).rearrange("p (a t) -> p a t", a=2)

        def half(i, j):
            return pages[:, i * PG + 512 * j:i * PG + 512 * (j + 1)]

        def const(name):
            a, b = COL[name]
            return cst[:, a:b]

        ident, head_mean, all_mean = const("ident"), const("head_mean"), const("all_mean")
        R, K, V, TH, TA, KN, PI = (pair(i) for i in (0, 1, 2, 3, 4, 5, 7))
        Pd = pages[:, 6 * PG:7 * PG].rearrange("p (a c t) -> p a c t", a=2, c=NCH)
        AR = pages[:, 8 * PG:8 * PG + 2048].rearrange("p (x a t) -> p x a t", x=2, a=2)
        WA = page(10)[:, 0:T]
        KF = pair(24)
        RRAW, MVRAW = pair(24), pair(10)
        BA = pages[:, 11 * PG:11 * PG + 2048].rearrange("p (m x i) -> p m x i", m=MATS, x=2)
        rows = {n: page(i).rearrange("p (t c) -> p t c", t=NT)
                for n, i in (("bet", 13), ("kap", 14), ("v", 15), ("mv", 2), ("rv", 23))}
        SC = pages[:, 16 * PG:16 * PG + MATS * 256].rearrange("p (m c) -> p m c", m=MATS)
        MQ, MK = pair(4), pair(7)
        Ti, TiT, Xm = (page(i).rearrange("p (m c) -> p m c", m=MATS) for i in (3, 5, 6))
        RQ, RK = pair(21), pair(22)
        bias_rows = pages[:, 21 * PG:21 * PG + HEADS * DIST].rearrange("p (h c) -> p h c", h=HEADS)
        bias_table = pages[:, 21 * PG + HEADS * DIST:21 * PG + HEADS * DIST + BUCKETS * HEADS].rearrange("p (b h) -> p b h", h=HEADS)
        out_rows = pages[:, 17 * PG:(17 + NT) * PG].rearrange("p (t c) -> p t c", c=PG)
        norm_rows = page(10)[0:DEPTH * KT, 0:P]
        par_rows = page(24)[0:N_ROWS, 0:DEPTH * P].rearrange("r (l c) -> r l c", l=DEPTH)
        mask_words = page(11)[:, 0:2 * len(LEVELS) * CH].bitcast(I32)
        A_blk, T_blk, TT_blk, AT_prod = (page(6)[:, 256 * i:256 * (i + 1)].rearrange("p (i j) -> p i j", i=BLK) for i in range(4))
        zeros = page(9)
        eps_page = page(2)
        fnorm = page(2)
        mean_sq, root, rms = small[:, 8:12], small[:, 12:16], small[:, 16:20]
        UW = pages[:, 21 * PG:21 * PG + 2048].rearrange("p (m x i) -> p m x i", m=MATS, x=2)
        GT, HP, ST = (page(i).rearrange("p (a c i) -> p a c i", a=2, c=NCH) for i in (5, 3, 6))
        RSB, PB, PT = pair(1), pair(1), pair(10)
        Y1 = pair(24)
        CU = pages[:, 23 * PG:24 * PG].rearrange("p (a t) -> p a t", a=2)
        CA = pair(12)
        LNS, RY, RSQ = pair(11), pair(8), pair(24)

        sem = {}

        def s(name):
            if name not in sem:
                sem[name] = ctx.enter_context(nc.semaphore(name))
            return sem[name]

        bank_full = [s(f"bank{i}_full") for i in range(8)]
        bank_read = [s(f"bank{i}_read") for i in range(8)]

        SIGNALS = {
            "h_raw": KT, "h_hi": KT, "h_split": KT,
            "kk_sq": 2, "kk_unit": 2, "lora_in": 1, "decay_sum": 2,
            "decay_exp": 4, "beta": 1, "kappa": 1, "alpha": 1, "rho": 1, "rkv": 2, "pads": 1, "blocks_done": 1,
            "rotated": 4, "logit_max": 16, "prob": 16, "prob_norm": 16, "first_state": 1, "ln_sq": 2,
            "ret_sq": 2, "ret_root": 2, "y_hi": KT, "y_split": KT, "y_conv": 2, "y_ret": 2, "y_rwkv": 2,
            "conv_pad": 1,
        }

        def at(name, layer, n=None):
            return s(name), layer * SIGNALS[name] + (SIGNALS[name] if n is None else n)

        def full(job, layer):
            b, nf, _, _ = locate(job, layer)
            return bank_full[b], nf + 1

        def read(job, layer, n=None):
            b, _, nr, readers = locate(job, layer)
            return bank_read[b], nr + (readers if n is None else n)

        def ps(job, layer):
            return bank[locate(job, layer)[0]]

        def done(job, layer):
            return bank_read[locate(job, layer)[0]]

        def unit(u):
            h, blk = divmod(u, NT)
            return h, h // 2, slice(64 * (h % 2), 64 * (h % 2) + 64), blk

        block = ctx.enter_context(nc.Block())

        @block.sync
        def _(sp):
            def load(dst, src, name):
                sp.dma_start(dst, src).then_inc(s(name), 16)

            a0, a1 = COL["ident"][0], COL["one"][1]
            load(cst[:, a0:a1], consts[:, a0:a1], "const_a")
            load(norm_rows, norm_w.rearrange("l (k c) -> (l k) c", c=P), "norm_loaded")

            n_stream = len(STREAM)

            def load_weights(i):
                layer, j = divmod(i, n_stream)
                if i >= RAW:
                    sp.wait_ge(s("w_split"), i - RAW + 1)
                if j < len(TILES):
                    c = TILE_COLS[TILES[j]]
                    src = w_in[layer, :, c:c + P]
                else:
                    src = w_out[layer, :, (j - len(TILES)) * P:(j - len(TILES) + 1) * P]
                sp.dma_start(w_raw[:, i % RAW, :, :], src.rearrange("(k p) c -> p k c", p=P)).then_inc(s(f"w_loaded{i % RAW}"), 16)

            def load_x(t):
                load(page(17 + t), x[0, t * P:(t + 1) * P, :], f"x_loaded{t}")

            load_x(0)
            load_weights(0)
            load_x(1)
            load_weights(1)
            load_x(2)
            load_x(3)
            load(bias_table, rel_bias.partition_broadcast(P), "bias_in")
            sp.wait_ge(s("par_clear"), 1)
            rws = lambda a, n: a.rearrange("l (r c) -> r l c", c=P)[0:n]
            load(par_rows[0:6], rws(rwkv_mu[:, 0:768], 6), "par_loaded")
            load(par_rows[6:7, :, 0:64], rwkv_mu[:, 768:832].rearrange("l (r c) -> r l c", r=1), "par_loaded")
            for r0, a in ((W0, rwkv_w0), (A0, rwkv_a0), (KKP, rwkv_k_k), (KAP, rwkv_k_a), (LNW, rwkv_lnx_w), (LNB, rwkv_lnx_b)):
                load(par_rows[r0:r0 + 2], rws(a, 2), "par_loaded")
            load(par_rows[RKP:RKP + 2], rwkv_r_k.rearrange("l (r h) n -> r l (h n)", r=2), "par_loaded")
            load(par_rows[CONVW:CONVW + 6], conv_w.rearrange("l j (p c) -> (j p) l c", p=2), "par_loaded")
            load_weights(2)
            load(cst[:, a1:], consts[:, a1:], "const_b")
            load(mask_words, level_masks, "const_b")
            load(lora_w[0:LORA], rwkv_w2.rearrange("l k c -> k l c"), "const_b")
            load(lora_w[LORA:2 * LORA], rwkv_a2.rearrange("l k c -> k l c"), "const_b")

            def blocks_of(scratch):
                v = scratch.rearrange("m (c x) y -> (m c) x y", c=2)
                return [v[:, g * BLK:(g + 1) * BLK, g * BLK:(g + 1) * BLK] for g in range(CH // BLK)]

            def clear_inverses():
                sp.wait_ge(s("zeros"), 1)
                for scratch in (t_scratch, tt_scratch):
                    load(scratch.rearrange("m q y -> q m y"), zeros.rearrange("q (m y) -> q m y", y=CH), "cleared")

            def blocks_out(layer):
                sp.wait_ge(*read("scores311", layer))
                load(a_scratch.rearrange("m q y -> q m y"), SC[:, :, 128:192], "a_out")
                sp.wait_ge(s("a_out"), 16 * (layer + 1))
                for g, src in enumerate(blocks_of(a_scratch)):
                    load(A_blk[32 * g:32 * g + 32], src, "blocks_in")

            def inverses_back(layer):
                sp.wait_ge(*at("blocks_done", layer))
                sp.wait_ge(s("cleared"), 32)
                for scratch, blk in ((t_scratch, T_blk), (tt_scratch, TT_blk)):
                    for g, dst in enumerate(blocks_of(scratch)):
                        load(dst, blk[32 * g:32 * g + 32], "t_out")
                sp.wait_ge(s("t_out"), 128 * (layer + 1))
                load(Ti, t_scratch.rearrange("m q y -> q m y"), "t_back")
                load(TiT, tt_scratch.rearrange("m q y -> q m y"), "t_back")

            def spill_first_x():
                for m in range(KT):
                    sp.wait_ge(*read(f"x_in{m}", -1))
                    load(x_scratch[m], XY[:, m, :], "x_spill")

            def skew_bias():
                sp.wait_ge(s("bias_rows"), 1)
                load(bias_scratch.rearrange("h q c -> q h c")[:, :, 0:DIST], bias_rows, "bias_out")
                sp.wait_ge(s("bias_out"), 16)
                skewed = bias_scratch.rearrange("h q c -> h (q c)")[:, 0:P * DIST].rearrange("h (q c) -> q h c", c=DIST)
                load(bias[:, :, :], skewed[:, :, P - 1:P - 1 + T], "bias_back")

            i = RAW
            for layer in range(DEPTH):
                while i < (layer + 1) * n_stream:
                    j = i - layer * n_stream
                    if j == len(TILES) + 4:
                        for k, m in enumerate(Y_ORDER):
                            sp.wait_ge(*at("y_split", layer, k + 1))
                            sp.wait_ge(s("x_spill"), 16 * KT * (layer + 1))
                            load(XY[:, m, :], x_scratch[m], f"x_back{m}")
                    if i == 2 * RAW:
                        spill_first_x()
                    if i == 3 * RAW:
                        skew_bias()
                    if layer == DEPTH - 1 and j == len(TILES):
                        sp.wait_ge(*full("moba_y1", layer))
                        load(fnorm, final_norm_w.rearrange("(r d) -> r d", r=1)[0].partition_broadcast(P), "fnorm_loaded")
                    if i == 4 * RAW:
                        clear_inverses()
                    if j == TILES.index("mk1"):
                        blocks_out(layer)
                    if j == TILES.index("mv0"):
                        inverses_back(layer)
                    if j == TILES.index("mq0"):
                        sp.wait_ge(*full("rows_v1", layer))
                        for p in range(2):
                            sp.wait_ge(*read(f"bonus{p}", layer))
                        load(eps_page, ret_eps, "ret_eps")
                    load_weights(i)
                    i += 1
                if layer < DEPTH - 1:
                    for k in range(RAW):
                        load_weights(i)
                        i += 1
                    for m in range(KT):
                        sp.wait_ge(*read(f"out{m}", layer))
                        load(x_scratch[m], XY[:, m, :], "x_spill")
            for t in range(NT):
                sp.wait_ge(s(f"scaled{t}"), 1)
                sp.dma_start(out[0, t * P:(t + 1) * P, :], page(17 + t)).then_inc(s("stored"), 16)
            sp.wait_ge(s("stored"), 16 * NT)

        @block.gpsimd
        def _(pool):
            pool.memset(par_rows, 0.0).then_inc(s("par_clear"), 1)
            pool.memset(zeros, 0.0).then_inc(s("zeros"), 1)
            H = KT // 2
            pool.wait_ge(s("const_a"), 16)
            n_stream = len(STREAM)
            def bias_by_distance():
                pool.memset(bias_rows[:, :, T:DIST], MASKED)
                pool.wait_ge(s("bias_in"), 16)
                for bucket, start, stop in bucket_runs():
                    ins = pool.tensor_copy(bias_rows[:, :, start:stop], bias_table[:, bucket, :].unsqueeze(2).to_broadcast([P, HEADS, stop - start]))
                ins.then_inc(s("bias_rows"), 1)

            for i in range(DEPTH * n_stream):
                if i == 2:
                    bias_by_distance()
                pool.wait_ge(s(f"w_loaded{i % RAW}"), 16 * (i // RAW + 1))
                if i >= HI:
                    before = divmod(i - HI, n_stream)
                    pool.wait_ge(*full(STREAM[before[1]], before[0]))
                for a in range(2):
                    k = slice(a * H, (a + 1) * H)
                    raw = w_raw[:, i % RAW, k, :]
                    pool.tensor_tensor(w_hi[:, i % HI, k, :], raw, const("one").unsqueeze(2).to_broadcast([P, H, P]), ALU.mult).then_inc(s("w_high"), 1)
                if i >= LO:
                    before = divmod(i - LO, n_stream)
                    pool.wait_ge(*full(STREAM[before[1]], before[0]))
                for a in range(2):
                    k = slice(a * H, (a + 1) * H)
                    pool.wait_ge(s("w_high"), 2 * i + a + 1)
                    ins = pool.tensor_tensor(w_lo[:, i % LO, k, :], w_raw[:, i % RAW, k, :], w_hi[:, i % HI, k, :].bitcast(F32), ALU.subtract)
                ins.then_inc(s("w_split"), 1)

        @block.tensor
        def _(pe):
            mm = pe.matmul

            def begin(job, layer):
                b, nf, nr, _ = locate(job, layer)
                if nr > 0:
                    pe.wait_ge(bank_read[b], nr)
                return bank[b]

            def end(ins, job, layer):
                ins.then_inc(bank_full[locate(job, layer)[0]], 1)

            pe.wait_ge(s("const_a"), 16)
            pe.wait_ge(s("norm_loaded"), 16)
            b = begin("norm_cols", -1)
            end(pe.transpose(b[:, 0:DEPTH * KT], norm_rows, ident[0:DEPTH * KT, 0:DEPTH * KT]), "norm_cols", -1)
            for t in range(NT):
                pe.wait_ge(s(f"x_loaded{t}"), 16)
                for m in range(KT):
                    b = begin(f"x_in{m}", -1) if t == 0 else ps(f"x_in{m}", -1)
                    ins = pe.transpose(b[:, t * P:(t + 1) * P], page(17 + t)[:, m * P:(m + 1) * P], ident)
                    if t == NT - 1:
                        end(ins, f"x_in{m}", -1)

            def stat(layer, last):
                b = ps("stat", layer) if last else begin("stat", layer)
                if last:
                    pe.wait_ge(s("x_sq"), (layer + 1) * KT)
                else:
                    pe.wait_ge(s("sq_added"), (layer + 1) * (KT - 2))
                src = half(24, 1) if last else half(11, 0)
                for t in range(NT):
                    ins = mm(b[:, t:t + 1], src[:, t * P:(t + 1) * P], const("all_mean"),
                             start=not last and t == 0, stop=last, skip_group_check=True)
                if last:
                    end(ins, "stat", layer)

            def row(m):
                pe.wait_ge(*read(f"out{m}", DEPTH - 1))
                b = begin(f"row{m}", DEPTH)
                for t in range(NT):
                    ins = pe.transpose(b[:, t * P:(t + 1) * P], XY[:, m, t * P:(t + 1) * P], ident)
                end(ins, f"row{m}", DEPTH)

            for layer in range(DEPTH):
                begun = set()

                def product(job, n):
                    i = layer * len(STREAM) + STREAM.index(job)
                    if n == 0:
                        pe.wait_ge(s("w_split"), i + 1)
                        begin(job, layer)
                    is_out = job in OUT_TILES
                    k = Y_ORDER[n] if is_out or job == LAST_TILE else n
                    if job in ("k0", "out0"):
                        pe.wait_ge(*at("y_split" if is_out else "h_split", layer, n + 1))
                    b = ps(job, layer)
                    hi, lo = w_hi[:, i % HI, k, :], w_lo[:, i % LO, k, :]
                    mm(b[:, :], hi, act_hi[:, k, :], start=n == 0, stop=False)
                    mm(b[:, :], lo, act_hi[:, k, :], start=False, stop=False)
                    ins = mm(b[:, :], hi, act_lo[:, k, :], start=False, stop=n == KT - 1)
                    if job == LAST_TILE and n < KT - 1:
                        ins.then_inc(s("h_used"), 1)
                    if n == KT - 1:
                        end(ins, job, layer)

                def first_half(job):
                    begun.add(job)
                    for n in range(KT // 2):
                        product(job, n)

                def second_half(job):
                    for n in range(KT // 2, KT):
                        product(job, n)
                    begun.add((job, "whole"))

                def project(job):
                    if (job, "whole") not in begun:
                        for n in range(KT // 2 if job in begun else 0, KT):
                            product(job, n)

                def norm():
                    pe.wait_ge(s("rms"), layer + 1)
                    b = begin("rn", layer)
                    for t in range(NT):
                        ins = mm(b[:, t * P:(t + 1) * P], rms[:, t:t + 1].to_broadcast([P, P]), ident, start=True, stop=True)
                    end(ins, "rn", layer)
                    if layer == 0:
                        pe.wait_ge(s("par_loaded"), 16 * 10)
                        for l in range(DEPTH):
                            b = begin(f"params{l}", -1)
                            end(pe.transpose(b[:, 0:N_ROWS], par_rows[:, l, :], ident[0:N_ROWS, 0:N_ROWS]), f"params{l}", -1)

                def k_pair():
                    for n in range(KT):
                        product("k0", n)
                        product("k1", n)

                def shift(job):
                    if job not in ("k0", "k1"):
                        project(job)

                def copy(job):
                    project(job)

                def gate(group, p):
                    project(f"{group}_g{p}")

                def conv_c(p):
                    project(f"cc{p}")

                def conv_h(p):
                    project(f"ch{p}")

                def conv_b(p):
                    project(f"cb{p}")

                def kk_square():
                    if layer == 0:
                        pe.wait_ge(s("const_b"), 16 * 4)
                    for p in range(2):
                        pe.wait_ge(*at("kk_sq", layer, p + 1))
                        b = begin(f"kk{p}", layer)
                        end(mm(b[:, :], head_mean, KN[:, p, :], start=True, stop=True), f"kk{p}", layer)

                def lora():
                    pe.wait_ge(*at("lora_in", layer))
                    for z, r0 in (("zw", 0), ("za", LORA)):
                        for p in range(2):
                            b = begin(f"{z}{p}", layer)
                            end(mm(b[:, :], lora_w[r0:r0 + LORA, layer, p * P:(p + 1) * P], WA[r0:r0 + LORA, :], start=True, stop=True), f"{z}{p}", layer)

                def bonus():
                    for p in range(2):
                        pe.wait_ge(*at("rkv", layer, p + 1))
                        b = begin(f"bonus{p}", layer)
                        end(mm(b[:, :], head_mean, R[:, p, :], start=True, stop=True), f"bonus{p}", layer)

                def to_rows(what):
                    src = {"v": V, "kap": PI, "bet": TA, "alp": AR[:, 0], "mv": MVRAW, "rv": MVRAW}[what]
                    for p in range(2):
                        if what in ("mv", "rv"):
                            pe.wait_ge(*read(f"{what}{p}", layer))
                        elif what == "v":
                            pe.wait_ge(*read(f"v{p}", layer))
                        else:
                            pe.wait_ge(*at({"kap": "kappa", "bet": "beta", "alp": "alpha"}[what], layer))
                        b = begin(f"rows_{what}{p}", layer)
                        for t in range(NT):
                            ins = pe.transpose(b[:, t * P:(t + 1) * P], src[:, p, t * P:(t + 1) * P], ident)
                        end(ins, f"rows_{what}{p}", layer)

                def scores(t):
                    if t == 0:
                        pe.wait_ge(*at("rho", layer))
                    for p in range(2):
                        for hh in range(2):
                            job = f"scores{t}{p}{hh}"
                            b = begin(job, layer)
                            hr = slice(64 * hh, 64 * hh + 64)
                            for c in (2 * t, 2 * t + 1):
                                cs = slice(c * CH, (c + 1) * CH)
                                o = b[64 * (c % 2):64 * (c % 2) + 64, :]
                                mm(o[:, 0:128], PI[hr, p, cs], AR[hr, :, p, cs], start=True, stop=True)
                                ins = mm(o[:, 128:256], TA[hr, p, cs], AR[hr, :, p, cs], start=True, stop=True)
                            end(ins, job, layer)

                def inverse_x(n):
                    for g in range(2):
                        if n == LEVELS[0]:
                            pe.wait_ge(s("t_back"), 32 * (layer + 1))
                        else:
                            pe.wait_ge(*read(f"y{n // 2}_{g}", layer))
                        each_matrix(f"x{n}_{g}", SC[:, :, 128:192], Ti, g)

                def inverse_y(n):
                    for g in range(2):
                        pe.wait_ge(*read(f"x{n}_{g}", layer))
                        each_matrix(f"y{n}_{g}", TiT, Xm, g)

                def inverse_yt(n):
                    for g in range(2):
                        pe.wait_ge(*read(f"x{n}_{g}", layer))
                        if n > LEVELS[0]:
                            pe.wait_ge(*read(f"yt{n // 2}_{g}", layer))
                        each_matrix(f"yt{n}_{g}", Xm, TiT, g)

                def each_matrix(job, lhs, rhs, g):
                    b = begin(job, layer)
                    for i in range(8):
                        for c in range(2):
                            r = slice(64 * c, 64 * c + 64)
                            ins = mm(b[r, i * CH:(i + 1) * CH], lhs[r, 8 * g + i, :], rhs[r, 8 * g + i, :], start=True, stop=True)
                    end(ins, job, layer)

                def rotate(job):
                    pe.wait_ge(*read(job, layer))
                    b = begin(f"rot_{job}", layer)
                    end(mm(b[:, :], const("rot"), RRAW[:, int(job[-1]), :], start=True, stop=True), f"rot_{job}", layer)

                def attend(g):
                    if 2 <= g:
                        h, p, hr, qb = unit(g - 2)
                        if g == 2:
                            for q in range(2):
                                pe.wait_ge(*read(f"rows_mv{q}", layer))
                        pe.wait_ge(*read(f"pt{g - 2}", layer))
                        yb = begin(f"moba_y{p}", layer) if g in (2, 10) else ps(f"moba_y{p}", layer)
                        for kb in range(qb + 1):
                            ins = mm(yb[hr, qb * P:(qb + 1) * P], rows["mv"][:, kb, h * N:(h + 1) * N],
                                     PT[:, (g - 1) % 2, kb * P:(kb + 1) * P], start=kb == 0, stop=kb == qb)
                        if g in (9, 17):
                            end(ins, f"moba_y{p}", layer)
                    if 1 <= g <= 16:
                        pe.wait_ge(*at("prob_norm", layer, g))
                        b = begin(f"pt{g - 1}", layer)
                        for kb in range((g - 1) % NT + 1):
                            ins = pe.transpose(b[:, kb * P:(kb + 1) * P], PB[:, (g - 1) % 2, kb * P:(kb + 1) * P], ident)
                        end(ins, f"pt{g - 1}", layer)
                    if g <= 15:
                        h, p, hr, qb = unit(g)
                        if g == 0:
                            for j in ("mq0", "mq1", "mk0", "mk1"):
                                pe.wait_ge(*read(j, layer))
                        b = begin(f"s{g}", layer)
                        end(mm(b[:, 0:(qb + 1) * P], MQ[hr, p, qb * P:(qb + 1) * P], MK[hr, p, 0:(qb + 1) * P], start=True, stop=True), f"s{g}", layer)

                def chunk_b():
                    for q in range(2):
                        pe.wait_ge(*read(f"rows_v{q}", layer))
                    for g in range(2):
                        b = begin(f"b{g}", layer)
                        for i in range(8):
                            m = 8 * g + i
                            t, h = divmod(m, HEADS)
                            for c in range(2):
                                r = slice(64 * c, 64 * c + 64)
                                ins = mm(b[r, i * CH:(i + 1) * CH], SC[r, m, 0:64], rows["v"][r, t, h * N:(h + 1) * N], start=True, stop=True)
                        end(ins, f"b{g}", layer)

                def chunk_uw():
                    for q in range(2):
                        pe.wait_ge(*read(f"rows_alp{q}", layer))
                        pe.wait_ge(*read(f"b{q}", layer))
                        pe.wait_ge(*read(f"yt{LEVELS[-1]}_{q}", layer))
                    for t in range(NT):
                        b = begin(f"uw{t}", layer)
                        for h in range(HEADS):
                            for c in range(2):
                                r = slice(64 * c, 64 * c + 64)
                                ins = mm(b[r, h * P:(h + 1) * P], TiT[r, t * HEADS + h, :], BA[r, t * HEADS + h, :, :], start=True, stop=True)
                        end(ins, f"uw{t}", layer)

                def chunk_g():
                    for t in range(NT):
                        pe.wait_ge(*read(f"uw{t}", layer))
                    for q in range(2):
                        pe.wait_ge(*read(f"rows_bet{q}", layer))
                        pe.wait_ge(*read(f"rows_kap{q}", layer))
                    by_chunk("g", 0)
                    by_chunk("g", 1)

                def chunk_h(c):
                    by_chunk("h", c)

                def chunk_q():
                    by_chunk("q", 0)
                    by_chunk("q", 1)

                def chunk_y1(c):
                    by_chunk("y", c)

                def by_chunk(what, c):
                    U, W = UW[:, :, 0, :], UW[:, :, 1, :]
                    job = f"{what}{c}" if what != "y" else f"y1{c}"
                    b = begin(job, layer)
                    r = slice(64 * c, 64 * c + 64)
                    for p in range(2):
                        for t in range(NT):
                            for hh in range(2):
                                h = 2 * p + hh
                                m = t * HEADS + h
                                o = b[64 * hh:64 * hh + 64, (p * NT + t) * CH:(p * NT + t + 1) * CH]
                                bet, kap, v = (rows[x][r, t, h * N:(h + 1) * N] for x in ("bet", "kap", "v"))
                                if what == "g":
                                    ins = mm(o, W[r, m, :], bet, start=True, stop=True)
                                elif what == "q":
                                    ins = mm(o, W[r, m, :], SC[r, m, 192:256], start=True, stop=True)
                                elif what == "h":
                                    mm(o, kap, v, start=True, stop=False)
                                    ins = mm(o, bet, U[r, m, :], start=False, stop=True)
                                else:
                                    mm(o, v, SC[r, m, 64:128], start=True, stop=False)
                                    ins = mm(o, U[r, m, :], SC[r, m, 192:256], start=False, stop=True)
                    end(ins, job, layer)

                def chain(c):
                    if c == 1:
                        for j in ("g0", "g1"):
                            pe.wait_ge(*read(j, layer))
                        pe.wait_ge(*at("first_state", layer))
                    else:
                        pe.wait_ge(*read(f"chain{c - 1}", layer))
                    b = begin(f"chain{c}", layer)
                    for p in range(2):
                        for hh in range(2):
                            r = slice(64 * hh, 64 * hh + 64)
                            ins = mm(b[r, p * N:(p + 1) * N], GT[r, p, c, :], ST[r, p, c, :], start=True, stop=True)
                    end(ins, f"chain{c}", layer)

                def chunk_y():
                    pe.wait_ge(*read(f"chain{NCH - 2}", layer))
                    for c in range(2):
                        pe.wait_ge(*read(f"q{c}", layer))
                    for p in range(2):
                        b = begin(f"y2{p}", layer)
                        for c in range(1, NCH):
                            for hh in range(2):
                                r = slice(64 * hh, 64 * hh + 64)
                                ins = mm(b[r, c * CH:(c + 1) * CH], ST[r, p, c, :], AR[r, 1, p, c * CH:(c + 1) * CH], start=True, stop=True)
                        end(ins, f"y2{p}", layer)

                def retain(i):
                    if i == 0:
                        pe.wait_ge(*at("rotated", layer))
                        for q in range(2):
                            pe.wait_ge(*read(f"rows_rv{q}", layer))
                    for u in (2 * i - 2, 2 * i - 1) if i > 0 else ():
                        h, p, hr, kb = unit(u)
                        pe.wait_ge(*read(f"rs{u}", layer))
                        yb = begin(f"ret_y{p}", layer) if u % 8 == 0 else ps(f"ret_y{p}", layer)
                        ins = mm(yb[hr, kb * P:T], rows["rv"][:, kb, h * N:(h + 1) * N], RSB[:, u % 2, 0:T - kb * P],
                                 start=kb == 0, stop=kb == NT - 1)
                        if u % 8 == 7:
                            end(ins, f"ret_y{p}", layer)
                    for u in (2 * i, 2 * i + 1) if i < 8 else ():
                        h, p, hr, kb = unit(u)
                        b = begin(f"rs{u}", layer)
                        end(mm(b[:, 0:T - kb * P], RK[hr, p, kb * P:(kb + 1) * P], RQ[hr, p, kb * P:T], start=True, stop=True), f"rs{u}", layer)

                def ln_mean():
                    for p in range(2):
                        pe.wait_ge(*read(f"y2{p}", layer))
                        b = begin(f"mean{p}", layer)
                        end(mm(b[:, :], head_mean, Y1[:, p, :], start=True, stop=True), f"mean{p}", layer)

                def ln_var():
                    for p in range(2):
                        pe.wait_ge(*at("ln_sq", layer, p + 1))
                        b = begin(f"var{p}", layer)
                        end(mm(b[:, :], head_mean, LNS[:, p, :], start=True, stop=True), f"var{p}", layer)

                def ret_stat():
                    for p in range(2):
                        pe.wait_ge(*at("ret_sq", layer, p + 1))
                        b = begin(f"ret_ms{p}", layer)
                        end(mm(b[:, :], head_mean, RSQ[:, p, :], start=True, stop=True), f"ret_ms{p}", layer)

                def project_out(m):
                    project(f"out{m}")
                    for n in (m - 1, m) if m == KT - 1 else (m - 1,) if m > 0 else ():
                        if layer == DEPTH - 1:
                            row(n)
                        if n >= KT - 2:
                            stat(layer, n == KT - 1)

                run = dict(norm=norm, k_pair=k_pair, first_half=first_half, second_half=second_half, shift=shift, copy=copy, gate=gate, conv_c=conv_c, conv_h=conv_h,
                           conv_b=conv_b, kk_square=kk_square, lora=lora, bonus=bonus, to_rows=to_rows, scores=scores,
                           inverse_x=inverse_x, inverse_y=inverse_y, inverse_yt=inverse_yt, rotate=rotate, attend=attend,
                           chunk_b=chunk_b, chunk_uw=chunk_uw, chunk_g=chunk_g, chunk_h=chunk_h, chunk_q=chunk_q, chunk_y1=chunk_y1,
                           chain=chain, chunk_y=chunk_y, retain=retain,
                           ln_mean=ln_mean, ln_var=ln_var, ret_stat=ret_stat, project_out=project_out)
                for name, *args in STEPS:
                    if name in run:
                        run[name](*args)

        @block.scalar
        def _(act):
            go = act.activation
            act.wait_ge(s("const_a"), 16)
            go(small[:, 24:25], const("eps")[:, 0:1], ACT.Sqrt)
            act.wait_ge(*full("norm_cols", -1))
            go(par[:, :, NORMW:NORMW + KT], ps("norm_cols", -1)[:, 0:DEPTH * KT].rearrange("p (l k) -> p l k", l=DEPTH), ACT.Copy)\
                .then_inc(done("norm_cols", -1), 1)
            for t in range(NT):
                act.wait_ge(s(f"x_loaded{t}"), 16)
                go(page(12), page(17 + t), ACT.Square, scale=D ** -0.5, accum_out=mean_sq[:, t:t + 1]).then_inc(s("x_mean"), 1)
                act.wait_ge(s("x_mean"), t + 1)
            go(root, mean_sq, ACT.Sqrt, bias=const("eps")[:, 0:1]).then_inc(s("root"), 1)
            for m in range(1, KT, 2):
                act.wait_ge(*full(f"x_in{m}", -1))
                go(XY[:, m, :], ps(f"x_in{m}", -1)[:, :], ACT.Copy).then_inc(done(f"x_in{m}", -1), 1)

            def square_x(layer, m):
                act.wait_ge(*read(f"out{m}", layer))
                if m >= 3:
                    act.wait_ge(s("sq_added"), layer * (KT - 2) + m - 2)
                go(half(24, m % 2) if m > 0 else half(11, 0), XY[:, m, :], ACT.Square).then_inc(s("x_sq"), 1)

            for layer in range(DEPTH + 1):
                if layer > 0:
                    act.wait_ge(*full("stat", layer - 1))
                    go(root, ps("stat", layer - 1)[:, 0:NT], ACT.Sqrt, bias=const("eps")[:, 0:1]).then_inc(done("stat", layer - 1), 1)
                if layer == DEPTH:
                    act.wait_ge(s("rms"), DEPTH + 1)
                    act.wait_ge(*read(f"row{KT - 1}", DEPTH))
                    for t in (1,):
                        go(page(17 + t), page(17 + t), ACT.Copy, scale=rms[:, t:t + 1]).then_inc(s(f"scaled{t}"), 1)
                    break

                def norm():
                    for k in range(KT):
                        act.wait_ge(*at("h_raw", layer, k + 1))
                        go(act_hi[:, k, :], half(13 + k // 2, k % 2), ACT.Copy).then_inc(s("h_hi"), 1)

                def shift(job):
                    act.wait_ge(*full(job, layer))
                    dst = {"k": K, "r": R, "v": V}[job[0]][:, int(job[1]), :] if job != "wa" else WA
                    n = 64 if job == "wa" else P
                    c = MUC + MU_ROW[job]
                    if job == "k0":
                        if layer == 0:
                            for l in range(DEPTH):
                                act.wait_ge(*full(f"params{l}", -1))
                                go(par[:, l, 0:N_ROWS], ps(f"params{l}", -1)[:, 0:N_ROWS], ACT.Copy).then_inc(done(f"params{l}", -1), 1)
                        act.wait_ge(s("derived"), 5)
                    go(dst[0:n], ps(job, layer)[0:n, :], ACT.Identity, scale=der[0:n, layer, c:c + 1]).then_inc(done(job, layer), 1)

                def kk_input():
                    for p in range(2):
                        act.wait_ge(*read(f"k{p}", layer))
                        go(KN[:, p, :], K[:, p, :], ACT.Square, scale=par[:, layer, KKP + p:KKP + p + 1]).then_inc(s("kk_sq"), 1)

                def kk_norm():
                    for p in range(2):
                        act.wait_ge(*full(f"kk{p}", layer))
                        go(KN[:, p, :], ps(f"kk{p}", layer)[:, :], ACT.Sqrt, scale=64.0).then_inc(done(f"kk{p}", layer), 1)

                def lora_tanh():
                    act.wait_ge(*read("wa", layer))
                    go(WA[0:LORA], WA[0:LORA], ACT.Tanh).then_inc(s("lora_in"), 1)

                def lora():
                    for z, dst, c in (("zw", TH, HW0), ("za", TA, HA0)):
                        for p in range(2):
                            act.wait_ge(*full(f"{z}{p}", layer))
                            go(dst[:, p, :], ps(f"{z}{p}", layer)[:, :], ACT.Tanh, scale=0.5, bias=der[:, layer, c + p:c + p + 1])\
                                .then_inc(done(f"{z}{p}", layer), 1)

                def decay_exp():
                    for p in range(2):
                        act.wait_ge(*at("decay_sum", layer, p + 1))
                        src = TH[:, p, :].rearrange("p (c t) -> p c t", t=CH)
                        go(Pd[:, p, :, 1:CH + 1], src, ACT.Exp, scale=-0.5 * DECAY).then_inc(s("decay_exp"), 1)
                        go(PI[:, p, :], TH[:, p, :], ACT.Exp, scale=0.5 * DECAY).then_inc(s("decay_exp"), 1)

                def gate(group, p):
                    k = {"rwkv": 0, "conv": 2, "moba": 4, "ret": 6}[group] + p
                    job = f"{group}_g{p}"
                    act.wait_ge(*full(job, layer))
                    act.wait_ge(s("x_spill"), 16 * KT * (layer + 1))
                    go(XY[:, k, :], ps(job, layer)[:, :], ACT.Tanh, scale=0.5).then_inc(done(job, layer), 1)

                def copy(job):
                    act.wait_ge(*full(job, layer))
                    p = int(job[2])
                    if job == "rq0":
                        act.wait_ge(*at("kappa", layer))
                    if job[:2] == "rk":
                        act.wait_ge(*at("rotated", layer, 1 + p))
                    if job == "rv0":
                        act.wait_ge(*full("za1", layer))
                    if job in ("mq0", "mk0"):
                        act.wait_ge(*full("scores311", layer))
                    if job == "mv0":
                        act.wait_ge(*full("rows_rv1", layer))
                    dst = {"mq": MQ, "mk": MK, "mv": MVRAW, "rv": MVRAW}.get(job[:2], RRAW)[:, p, :]
                    go(dst, ps(job, layer)[:, :], ACT.Copy).then_inc(done(job, layer), 1)

                def to_rows(what):
                    for p in range(2):
                        job = f"rows_{what}{p}"
                        act.wait_ge(*full(job, layer))
                        src = ps(job, layer)[:, :]
                        if what == "alp":
                            for t in range(NT):
                                ins = go(BA[:, t * HEADS + 2 * p:t * HEADS + 2 * p + 2, 1, :],
                                         src[:, t * P:(t + 1) * P].rearrange("p (h n) -> p h n", h=2), ACT.Copy)
                            ins.then_inc(done(job, layer), 1)
                        else:
                            if what == "rv" and p == 0 and layer == 0:
                                act.wait_ge(s("bias_out"), 16)
                            if what == "mv":
                                act.wait_ge(*read(f"ret_ms{1}", layer))
                            go(rows[what][:, :, p * P:(p + 1) * P], src.rearrange("p (t c) -> p t c", t=NT), ACT.Copy).then_inc(done(job, layer), 1)

                def inverse_x(n):
                    for g in range(2):
                        act.wait_ge(*full(f"x{n}_{g}", layer))
                        if n > LEVELS[0]:
                            act.wait_ge(*full(f"yt{n // 2}_{g}", layer))
                        go(Xm[:, 8 * g:8 * g + 8, :], ps(f"x{n}_{g}", layer)[:, :].rearrange("p (m c) -> p m c", m=8), ACT.Copy)\
                            .then_inc(done(f"x{n}_{g}", layer), 1)

                def attend(g):
                    if 1 <= g <= 16:
                        w = ((g - 1) % NT + 1) * P
                        act.wait_ge(*full(f"pt{g - 1}", layer))
                        go(PT[:, g % 2, 0:w], ps(f"pt{g - 1}", layer)[:, 0:w], ACT.Copy).then_inc(done(f"pt{g - 1}", layer), 1)
                    if g <= 15:
                        pb = PB[:, g % 2, 0:(g % NT + 1) * P]
                        act.wait_ge(*at("logit_max", layer, g + 1))
                        go(pb, pb, ACT.Exp, bias=small[:, g % 2:g % 2 + 1], accum_out=small[:, 2 + g % 2:3 + g % 2]).then_inc(s("prob"), 1)

                def conv_c(p):
                    act.wait_ge(*full(f"cc{p}", layer))
                    if p == 0:
                        act.wait_ge(*full("ret_y1", layer))
                    go(CU[:, p, 2:T + 2], ps(f"cc{p}", layer)[:, :], ACT.Copy).then_inc(done(f"cc{p}", layer), 1)

                def chunk_b():
                    for g in range(2):
                        act.wait_ge(*full(f"b{g}", layer))
                        go(BA[:, 8 * g:8 * g + 8, 0, :], ps(f"b{g}", layer)[:, :].rearrange("p (m c) -> p m c", m=8), ACT.Copy)\
                            .then_inc(done(f"b{g}", layer), 1)

                def chunk_uw():
                    for t in range(NT):
                        act.wait_ge(*full(f"uw{t}", layer))
                        go(UW[:, t * HEADS:(t + 1) * HEADS, :, :],
                           ps(f"uw{t}", layer)[:, :].rearrange("p (m x i) -> p m x i", m=HEADS, x=2), ACT.Copy)\
                            .then_inc(done(f"uw{t}", layer), 1)

                def chunk_y1(c):
                    if c == 0:
                        act.wait_ge(*at("y_ret", layer))
                    act.wait_ge(*full(f"y1{c}", layer))
                    for p in range(2):
                        ins = go(Y1[:, p, :].rearrange("p (t c i) -> p t c i", c=2, i=CH)[:, :, c, :],
                                 ps(f"y1{c}", layer)[:, p * 256:(p + 1) * 256].rearrange("p (t i) -> p t i", i=CH), ACT.Copy)
                    ins.then_inc(done(f"y1{c}", layer), 1)

                def retain(i):
                    if layer == 0 and i == 0:
                        act.wait_ge(s("const_b"), 16 * 4)
                    for u in (2 * i, 2 * i + 1) if i < 8 else ():
                        w = T - u % NT * P
                        if w > P:
                            act.wait_ge(*read(f"rs{u}", layer, 1))
                            go(RSB[:, u % 2, P:w], ps(f"rs{u}", layer)[:, P:w], ACT.Copy, scale=const("k_decay")[:, u:u + 1])\
                                .then_inc(done(f"rs{u}", layer), 1)

                def retain_out(p):
                    act.wait_ge(*full(f"ret_y{p}", layer))
                    go(RSQ[:, p, :], ps(f"ret_y{p}", layer)[:, :], ACT.Square).then_inc(s("ret_sq"), 1)
                    go(RY[:, p, :], ps(f"ret_y{p}", layer)[:, :], ACT.Copy).then_inc(done(f"ret_y{p}", layer), 1)

                def ln_square():
                    for p in range(2):
                        act.wait_ge(*read(f"mean{p}", layer))
                        go(LNS[:, p, :], Y1[:, p, :], ACT.Square).then_inc(s("ln_sq"), 1)

                def ln_var():
                    for p in range(2):
                        act.wait_ge(*full(f"var{p}", layer))
                        go(LNS[:, p, :], ps(f"var{p}", layer)[:, :], ACT.Sqrt, bias=const("eps")[:, 1:2]).then_inc(done(f"var{p}", layer), 1)

                def ret_root():
                    for p in range(2):
                        act.wait_ge(*read(f"ret_ms{p}", layer))
                        go(RSQ[:, p, :], RSQ[:, p, :], ACT.Sqrt).then_inc(s("ret_root"), 1)

                def split_y(k):
                    n = Y_ORDER.index(k)
                    if n < KT - 1:
                        act.wait_ge(s("h_used"), layer * (KT - 1) + n + 1)
                    else:
                        act.wait_ge(*full(LAST_TILE, layer))
                    if k // 2 == 2:
                        act.wait_ge(*read(f"moba_y{k % 2}", layer))
                    else:
                        act.wait_ge(*at({0: "y_rwkv", 1: "y_conv", 3: "y_ret"}[k // 2], layer, k % 2 + 1))
                    go(act_hi[:, k, :], XY[:, k, :], ACT.Copy).then_inc(s("y_hi"), 1)

                def project_out(m):
                    square_x(layer, m)
                    if m == KT - 3:
                        go(small[:, 24:25], const("eps")[:, 0:1], ACT.Sqrt)

                run = dict(norm=norm, shift=shift, kk_input=kk_input, kk_norm=kk_norm, lora_tanh=lora_tanh, lora=lora,
                           decay_exp=decay_exp, gate=gate, copy=copy, to_rows=to_rows,
                           inverse_x=inverse_x, attend=attend, conv_c=conv_c, chunk_b=chunk_b,
                           chunk_uw=chunk_uw, chunk_y1=chunk_y1, retain=retain, retain_out=retain_out,
                           ln_square=ln_square, ln_var=ln_var, ret_root=ret_root, split_y=split_y, project_out=project_out)
                for name, *args in STEPS:
                    if name in run:
                        run[name](*args)

        @block.vector
        def _(dve):
            tt, ts, stt = dve.tensor_tensor, dve.tensor_scalar, dve.scalar_tensor_tensor
            n_step = [0]

            def mark(ins):
                n_step[0] += 1
                ins.then_inc(s("dve_step"), 1)
                return n_step[0]

            def link(ins):
                dve.wait_ge(s("dve_step"), mark(ins))

            def reciprocal_of_root(layer):
                if layer > 0:
                    dve.wait_ge(*read("stat", layer - 1))
                else:
                    dve.wait_ge(s("root"), 1)
                dve.reciprocal(rms, root).then_inc(s("rms"), 1)

            reciprocal_of_root(0)
            for m in range(0, KT, 2):
                dve.wait_ge(*full(f"x_in{m}", -1))
                dve.tensor_copy(XY[:, m, :], ps(f"x_in{m}", -1)[:, :]).then_inc(done(f"x_in{m}", -1), 1)
            dve.wait_ge(*read("norm_cols", -1))

            def evacuate_row(m):
                if m == 0:
                    dve.wait_ge(s("fnorm_loaded"), 16)
                dve.wait_ge(*full(f"row{m}", DEPTH))
                tt(out_rows[:, :, m * P:(m + 1) * P], ps(f"row{m}", DEPTH)[:, :].rearrange("p (t c) -> p t c", t=NT),
                   fnorm[:, m * P:(m + 1) * P].unsqueeze(1).to_broadcast([P, NT, P]), ALU.mult).then_inc(done(f"row{m}", DEPTH), 1)

            for layer in range(DEPTH + 1):
                def scaled(k):
                    stt(half(13 + k // 2, k % 2), XY[:, k, :], par[:, layer, NORMW + k:NORMW + k + 1], ps("rn", layer)[:, :], ALU.mult, ALU.mult)\
                        .then_inc(s("h_raw"), 1)

                def low(k):
                    dve.wait_ge(*at("h_hi", layer, k + 1))
                    ins = tt(act_lo[:, k, :], half(13 + k // 2, k % 2), act_hi[:, k, :].bitcast(F32), ALU.subtract)
                    ins.then_inc(s("h_split"), 1)

                def norm():
                    dve.wait_ge(*full("rn", layer))
                    for k in range(KT):
                        if layer == 0 and k % 2:
                            dve.wait_ge(*read(f"x_in{k}", -1))
                        scaled(k)
                        if k >= 1:
                            low(k - 1)
                    low(KT - 1)
                    if layer == 0:
                        derive()

                def derive():
                    for l in range(DEPTH):
                        dve.wait_ge(*read(f"params{l}", -1))
                    for c, n, src, a, b in ((MUC, 7, MU, -1.0, 1.0), (HW0, 2, W0, 0.5, 0.0), (HA0, 2, A0, 0.5, 0.0),
                                            (KA2, 2, KAP, 0.5, 0.0), (KA1, 2, KAP, -0.5, 1.0)):
                        ts(der[:, :, c:c + n], par[:, :, src:src + n], a, b, ALU.mult, ALU.add).then_inc(s("derived"), 1)
                    dve.wait_ge(s("derived"), 5)
                    dve.wait_ge(s("const_b"), 16 * 4)
                    link(dve.tensor_copy(lmask[:].rearrange("p a l c -> p (a l c)"), mask_words))

                if layer > 0:
                    reciprocal_of_root(layer)
                if layer == DEPTH:
                    dve.wait_ge(*read(f"row{KT - 1}", DEPTH))
                    dve.wait_ge(s("rms"), DEPTH + 1)
                    for t in (0, 2, 3):
                        ts(page(17 + t), page(17 + t), rms[:, t:t + 1], None, ALU.mult).then_inc(s(f"scaled{t}"), 1)
                    break

                def pads():
                    dve.memset(Pd[:, :, :, 0:1], 1.0).then_inc(s("pads"), 1)

                def shift(job):
                    dve.wait_ge(*read(job, layer, 1))
                    dst = {"k": K, "r": R, "v": V}[job[0]][:, int(job[1]), :] if job != "wa" else WA
                    n = 64 if job == "wa" else P
                    c = MU + MU_ROW[job]
                    b = ps(job, layer)
                    stt(dst[0:n, 1:T], b[0:n, 0:T - 1], par[0:n, layer, c:c + 1], dst[0:n, 1:T], ALU.mult, ALU.add)\
                        .then_inc(done(job, layer), 1)

                def kk_norm():
                    for p in range(2):
                        dve.wait_ge(*read(f"kk{p}", layer))
                    link(ts(KN, KN, 1e-12, None, ALU.max))
                    link(dve.reciprocal(KN, KN))
                    for p in range(2):
                        stt(KN[:, p, :], K[:, p, :], par[:, layer, KKP + p:KKP + p + 1], KN[:, p, :], ALU.mult, ALU.mult).then_inc(s("kk_unit"), 1)

                def decay_scan():
                    for p in range(2):
                        dve.wait_ge(*read(f"zw{p}", layer))
                    link(ts(TH, TH, 1.0, None, ALU.add))
                    for p in range(2):
                        dve.tensor_tensor_scan(TH[:, p, :], const("chunk_reset"), TH[:, p, :], 0.0, ALU.mult, ALU.add).then_inc(s("decay_sum"), 1)

                def factors():
                    for p in range(2):
                        dve.wait_ge(*read(f"za{p}", layer))
                    for p in range(2):
                        c = mark(ts(KF[:, p, :], TA[:, p, :], der[:, layer, KA2 + p:KA2 + p + 1], der[:, layer, KA1 + p:KA1 + p + 1], ALU.mult, ALU.add))
                    dve.wait_ge(*at("kk_unit", layer))
                    dve.wait_ge(s("dve_step"), c)
                    d = mark(stt(TA, TA, 1.0, KN, ALU.add, ALU.mult))
                    e = mark(tt(K, K, KF, ALU.mult))
                    dve.wait_ge(*at("decay_exp", layer))
                    dve.wait_ge(s("dve_step"), d)
                    stt(TA, TA, -0.5, PI, ALU.mult, ALU.mult).then_inc(s("beta"), 1)
                    dve.wait_ge(*at("pads", layer))
                    dve.wait_ge(s("dve_step"), e)
                    dve.wait_ge(*at("beta", layer))
                    tt(PI, K, PI, ALU.mult).then_inc(s("kappa"), 1)
                    flat = Pd.rearrange("p a c t -> p (a c) t")
                    chunks = lambda v: v.rearrange("p a (c t) -> p (a c) t", t=CH)
                    if layer == 0:
                        dve.wait_ge(s("cleared"), 32)
                    tt(chunks(AR[:, 0]), chunks(KN), flat[:, :, 0:CH], ALU.mult).then_inc(s("alpha"), 1)
                    tt(chunks(AR[:, 1]), chunks(R), flat[:, :, 1:CH + 1], ALU.mult).then_inc(s("rho"), 1)
                    mark(dve.tensor_copy(w_end[:].rearrange("p a c -> p (a c)").unsqueeze(2), flat[:, :, CH:CH + 1]))
                    dve.wait_ge(*at("rho", layer))
                    for p in range(2):
                        stt(R[:, p, :], R[:, p, :], par[:, layer, RKP + p:RKP + p + 1], K[:, p, :], ALU.mult, ALU.mult).then_inc(s("rkv"), 1)

                def bonus():
                    for p in range(2):
                        dve.wait_ge(*full(f"bonus{p}", layer))
                        stt(R[:, p, :], ps(f"bonus{p}", layer)[:, :], 64.0, V[:, p, :], ALU.mult, ALU.mult).then_inc(done(f"bonus{p}", layer), 1)

                def gate(group, p):
                    k = {"rwkv": 0, "conv": 2, "moba": 4, "ret": 6}[group] + p
                    job = f"{group}_g{p}"
                    dve.wait_ge(*read(job, layer, 1))
                    stt(XY[:, k, :], XY[:, k, :], 1.0, ps(job, layer)[:, :], ALU.add, ALU.mult).then_inc(done(job, layer), 1)

                def scores(t):
                    for p in range(2):
                        for hh in range(2):
                            job = f"scores{t}{p}{hh}"
                            dve.wait_ge(*full(job, layer))
                            tt(SC[:, t * HEADS + 2 * p + hh, :], ps(job, layer)[:, 0:256], const("score_mask"), ALU.mult).then_inc(done(job, layer), 1)

                def mask(level, transposed, n):
                    return lmask[:, transposed, LEVELS.index(level), :].unsqueeze(1).to_broadcast([P, n, CH])

                def block_rows(part):
                    if part == 0:
                        dve.wait_ge(s("blocks_in"), 64 * (layer + 1))
                        flat = T_blk.rearrange("p i j -> p (i j)")
                        link(dve.memset(flat, 0.0))
                        link(dve.memset(flat[:, ::BLK + 1], 1.0))
                    for i in range(*((1, 8), (8, 12), (12, BLK))[part]):
                        prod = AT_prod[:, 0:i, 0:i]
                        link(tt(prod, T_blk[:, 0:i, 0:i].rearrange("p j k -> p k j"), A_blk[:, 0:i, i].unsqueeze(1).to_broadcast([P, i, i]), ALU.mult))
                        link(dve.tensor_reduce(T_blk[:, i, 0:i], prod, AX_X, ALU.add))
                    if part == 2:
                        dve.tensor_copy(TT_blk, T_blk.rearrange("p i j -> p j i")).then_inc(s("blocks_done"), 1)

                def inverse_y(n):
                    for g in range(2):
                        m8 = slice(8 * g, 8 * g + 8)
                        dve.wait_ge(*full(f"y{n}_{g}", layer))
                        dve.copy_predicated(Ti[:, m8, :], mask(n, 0, 8), ps(f"y{n}_{g}", layer)[:, :].rearrange("p (m c) -> p m c", m=8))\
                            .then_inc(done(f"y{n}_{g}", layer), 1)

                def inverse_yt(n):
                    for g in range(2):
                        m8 = slice(8 * g, 8 * g + 8)
                        dve.wait_ge(*full(f"yt{n}_{g}", layer))
                        dve.copy_predicated(TiT[:, m8, :], mask(n, 1, 8), ps(f"yt{n}_{g}", layer)[:, :].rearrange("p (m c) -> p m c", m=8))\
                            .then_inc(done(f"yt{n}_{g}", layer), 1)

                def rotate(job):
                    p = int(job[-1])
                    j = ["rq0", "rq1", "rk0", "rk1"].index(job)
                    dst = (RQ if job[1] == "q" else RK)[:, p, :]
                    dve.wait_ge(*full(f"rot_{job}", layer))
                    if j == 0 and layer == 0:
                        dve.wait_ge(s("bias_out"), 16)
                    raw = RRAW[:, p, :]
                    c = mark(tt(dst, raw, const("cos"), ALU.mult))
                    dve.wait_ge(s("dve_step"), c)
                    tt(raw, ps(f"rot_{job}", layer)[:, :], const("sin"), ALU.mult).then_inc(done(f"rot_{job}", layer), 1)
                    dve.wait_ge(*read(f"rot_{job}", layer))
                    tt(dst, dst, raw, ALU.add).then_inc(s("rotated"), 1)

                def attend(g):
                    if g > 15:
                        return
                    h, _, _, qb = unit(g)
                    w = (qb + 1) * P
                    pb = PB[:, g % 2, 0:w]
                    if layer == 0 and g == 0:
                        dve.wait_ge(s("bias_back"), 16)
                    dve.wait_ge(*full(f"s{g}", layer))
                    stt(pb, ps(f"s{g}", layer)[:, 0:w], 0.125, bias[:, h, T - w:T], ALU.mult, ALU.add).then_inc(done(f"s{g}", layer), 1)
                    dve.wait_ge(*read(f"s{g}", layer))
                    dve.tensor_reduce(small[:, g % 2:g % 2 + 1], pb, AX_X, ALU.max, negate=True).then_inc(s("logit_max"), 1)
                    dve.wait_ge(*at("prob", layer, g + 1))
                    r = small[:, 4 + g % 2:5 + g % 2]
                    link(dve.reciprocal(r, small[:, 2 + g % 2:3 + g % 2]))
                    ts(pb, pb, r, None, ALU.mult).then_inc(s("prob_norm"), 1)

                def attend_out(p):
                    dve.wait_ge(*full(f"moba_y{p}", layer))
                    finish_tile(4 + p, ps(f"moba_y{p}", layer)[:, :]).then_inc(done(f"moba_y{p}", layer), 1)

                def finish_tile(k, y):
                    return stt(XY[:, k, :], y, 0.5, XY[:, k, :], ALU.mult, ALU.mult)

                def conv_c(p):
                    if p == 0:
                        dve.wait_ge(*full("ret_y1", layer))
                        dve.memset(CU[:, :, 0:2], 0.0).then_inc(s("conv_pad"), 1)

                def conv_h(p):
                    dve.wait_ge(*full(f"ch{p}", layer))
                    dve.wait_ge(*read(f"cc{p}", layer))
                    tt(CU[:, p, 2:T + 2], CU[:, p, 2:T + 2], ps(f"ch{p}", layer)[:, :], ALU.mult).then_inc(done(f"ch{p}", layer), 1)
                    dve.wait_ge(*read(f"ch{p}", layer))
                    dve.wait_ge(*at("conv_pad", layer))
                    w = lambda j: par[:, layer, CONVW + 2 * j + p:CONVW + 2 * j + p + 1]
                    link(ts(CA[:, p, :], CU[:, p, 0:T], w(0), None, ALU.mult))
                    for j in (1, 2):
                        link(stt(CA[:, p, :], CU[:, p, j:T + j], w(j), CA[:, p, :], ALU.mult, ALU.add))

                def conv_b(p):
                    dve.wait_ge(*full(f"cb{p}", layer))
                    tt(CA[:, p, :], CA[:, p, :], ps(f"cb{p}", layer)[:, :], ALU.mult).then_inc(done(f"cb{p}", layer), 1)

                def conv_out():
                    for p in range(2):
                        dve.wait_ge(*read(f"conv_g{p}", layer))
                        dve.wait_ge(*read(f"cb{p}", layer))
                        finish_tile(2 + p, CA[:, p, :]).then_inc(s("y_conv"), 1)

                par8 = lambda v, c: v.rearrange("p a (t x) i -> p a t x i", x=2)[:, :, :, c, :]
                chunk_ps = lambda j: ps(j, layer)[:, :].rearrange("p (a t i) -> p a t i", a=2, i=N)

                def chunk_g():
                    for c in range(2):
                        dve.wait_ge(*full(f"g{c}", layer))
                        for p in range(2):
                            ins = tt(par8(GT, c)[:, p], chunk_ps(f"g{c}")[:, p], const("eye64").unsqueeze(1).to_broadcast([P, NT, N]), ALU.add)
                        ins.then_inc(done(f"g{c}", layer), 1)

                def chunk_h(c):
                    we = w_end[:].rearrange("p a (t x) -> p a t x", x=2)
                    dve.wait_ge(*full(f"h{c}", layer))
                    for p in range(2):
                        ins = tt(par8(HP, c)[:, p], chunk_ps(f"h{c}")[:, p], we[:, p, :, c].unsqueeze(2).to_broadcast([P, NT, N]), ALU.mult)
                    ins.then_inc(done(f"h{c}", layer), 1)
                    if c == 1:
                        for j in range(2):
                            dve.wait_ge(*read(f"h{j}", layer))
                        dve.tensor_copy(ST[:, :, 1, :], HP[:, :, 0, :]).then_inc(s("first_state"), 1)

                def chunk_q():
                    rho = AR[:, 1].rearrange("p a (t x i) -> p a t x i", x=2, i=CH)
                    for c in range(2):
                        dve.wait_ge(*full(f"q{c}", layer))
                        for p in range(2):
                            ins = tt(rho[:, p, :, c, :], rho[:, p, :, c, :], chunk_ps(f"q{c}")[:, p], ALU.add)
                        ins.then_inc(done(f"q{c}", layer), 1)

                def chain(c):
                    dve.wait_ge(*full(f"chain{c}", layer))
                    b = ps(f"chain{c}", layer)
                    for p in range(2):
                        ins = stt(ST[:, p, c + 1, :], b[:, p * N:(p + 1) * N], w_end[:, p, c:c + 1], HP[:, p, c, :], ALU.mult, ALU.add)
                    ins.then_inc(done(f"chain{c}", layer), 1)

                def chunk_y():
                    for c in range(2):
                        dve.wait_ge(*read(f"y1{c}", layer))
                    for p in range(2):
                        dve.wait_ge(*full(f"y2{p}", layer))
                        tt(Y1[:, p, CH:T], Y1[:, p, CH:T], ps(f"y2{p}", layer)[:, CH:T], ALU.add).then_inc(done(f"y2{p}", layer), 1)

                def retain(i):
                    for u in (2 * i, 2 * i + 1) if i < 8 else ():
                        dve.wait_ge(*full(f"rs{u}", layer))
                        stt(RSB[:, u % 2, 0:P], ps(f"rs{u}", layer)[:, 0:P], const("k_decay")[:, u:u + 1], const("causal"), ALU.mult, ALU.mult)\
                            .then_inc(done(f"rs{u}", layer), 1)

                def ln_mean():
                    for p in range(2):
                        dve.wait_ge(*full(f"mean{p}", layer))
                        tt(Y1[:, p, :], Y1[:, p, :], ps(f"mean{p}", layer)[:, :], ALU.subtract).then_inc(done(f"mean{p}", layer), 1)

                def ret_stat():
                    dve.wait_ge(s("ret_eps"), 16 * (layer + 1))
                    for p in range(2):
                        dve.wait_ge(*full(f"ret_ms{p}", layer))
                        tt(RSQ[:, p, :], ps(f"ret_ms{p}", layer)[:, :], eps_page[:, p * T:(p + 1) * T], ALU.add).then_inc(done(f"ret_ms{p}", layer), 1)

                def ret_recip(i):
                    p, a = divmod(i, 2)
                    dve.wait_ge(*at("ret_root", layer, p + 1))
                    v = RSQ[:, p, a * T // 2:(a + 1) * T // 2]
                    mark(dve.reciprocal(v, v))

                def ret_finish():
                    for p in range(2):
                        dve.wait_ge(*read(f"ret_y{p}", layer))
                    dve.wait_ge(s("dve_step"), n_step[0])
                    link(tt(RY, RY, RSQ, ALU.mult))
                    for p in range(2):
                        finish_tile(6 + p, RY[:, p, :]).then_inc(s("y_ret"), 1)

                def ln_recip(i):
                    p, a = divmod(i, 2)
                    dve.wait_ge(*read(f"var{p}", layer))
                    v = LNS[:, p, a * T // 2:(a + 1) * T // 2]
                    mark(dve.reciprocal(v, v))

                def ln_scale(p):
                    dve.wait_ge(s("dve_step"), n_step[0])
                    y = Y1[:, p, :]
                    link(tt(y, y, LNS[:, p, :], ALU.mult))
                    mark(ts(y, y, par[:, layer, LNW + p:LNW + p + 1], par[:, layer, LNB + p:LNB + p + 1], ALU.mult, ALU.add))

                def rwkv_finish(p):
                    dve.wait_ge(s("dve_step"), n_step[0])
                    link(tt(Y1[:, p, :], Y1[:, p, :], R[:, p, :], ALU.add))
                    finish_tile(p, Y1[:, p, :]).then_inc(s("y_rwkv"), 1)

                def split_y(k):
                    dve.wait_ge(*at("y_hi", layer, Y_ORDER.index(k) + 1))
                    tt(act_lo[:, k, :], XY[:, k, :], act_hi[:, k, :].bitcast(F32), ALU.subtract).then_inc(s("y_split"), 1)

                def project_out(m):
                    if m >= 2:
                        dve.wait_ge(s("x_sq"), layer * KT + m)
                        if m >= 3:
                            dve.wait_ge(s("sq_added"), layer * (KT - 2) + m - 2)
                        tt(half(11, 0), half(11, 0), half(24, (m - 1) % 2), ALU.add).then_inc(s("sq_added"), 1)
                    dve.wait_ge(*full(f"out{m}", layer))
                    dve.wait_ge(s(f"x_back{m}"), 16 * (layer + 1))
                    tt(XY[:, m, :], XY[:, m, :], ps(f"out{m}", layer)[:, :], ALU.add).then_inc(done(f"out{m}", layer), 1)
                    if layer == DEPTH - 1:
                        for n in (m - 1, m) if m == KT - 1 else (m - 1,) if m > 0 else ():
                            evacuate_row(n)

                run = dict(norm=norm, shift=shift, kk_norm=kk_norm, decay_scan=decay_scan, factors=factors, bonus=bonus,
                           gate=gate, scores=scores, block_rows=block_rows, inverse_y=inverse_y, inverse_yt=inverse_yt, rotate=rotate,
                           attend=attend, attend_out=attend_out, conv_c=conv_c, conv_h=conv_h, conv_b=conv_b,
                           conv_out=conv_out, chunk_g=chunk_g, chunk_h=chunk_h, chunk_q=chunk_q, chain=chain, chunk_y=chunk_y,
                           retain=retain, ln_mean=ln_mean, ret_stat=ret_stat, ret_recip=ret_recip, ret_finish=ret_finish,
                           ln_recip=ln_recip, ln_scale=ln_scale, rwkv_finish=rwkv_finish, split_y=split_y,
                           project_out=project_out, decay_exp=pads)
                for name, *args in STEPS:
                    if name in run:
                        run[name](*args)


def shape_constants():
    c = {}
    i = np.arange(P)
    c["ident"] = np.eye(P)
    c["head_mean"] = (i[:, None] // N == i[None, :] // N) / N
    c["all_mean"] = np.full((P, 1), 1.0 / D)
    c["one"] = np.ones((P, 1))
    rot = np.zeros((P, P))
    rot[i[1::2], i[0::2]] = -1.0
    rot[i[0::2], i[1::2]] = 1.0
    c["rot"] = rot
    c["causal"] = i[:, None] <= i[None, :]
    a, b = np.arange(P)[:, None] % CH, np.arange(CH)[None, :]
    c["score_mask"] = np.concatenate([a < b, a <= b, a < b, a <= b], axis=1)
    c["eye64"] = a == b
    gamma = 1.0 - 2.0 ** (-5.0 - np.arange(HEADS))
    pos = np.arange(T)
    c["k_decay"] = np.stack([gamma[h] ** -(kb * P + i.astype(np.float64)) * N ** -0.5 for h in range(HEADS) for kb in range(NT)], axis=1)
    c["eps"] = np.tile([[NORM_EPS, LNX_EPS]], (P, 1))
    c["chunk_reset"] = np.tile(pos % CH != 0, (P, 1))
    theta = (1.0 / (10000.0 ** np.linspace(0.0, 1.0, N // 2, dtype=np.float32))).astype(np.float32)
    angle = (pos.astype(np.float32)[None, :] * theta[:, None]).astype(np.float32).astype(np.float64)
    angle = angle[(i % N) // 2]
    c["cos"], c["sin"] = np.cos(angle), np.sin(angle)
    ret_eps = np.concatenate([NORM_EPS * gamma[2 * p + i[:, None] // N] ** (-2.0 * pos[None, :]) for p in range(2)], axis=1)
    consts = np.concatenate([np.asarray(c[n], np.float32) for n, _ in CONSTS], axis=1)
    levels = np.stack([(a // (2 * n) == b // (2 * n)) & (a // n % 2 == 1) & (b // n % 2 == 0) for n in LEVELS], axis=1)
    levels_t = np.stack([(a // (2 * n) == b // (2 * n)) & (a // n % 2 == 0) & (b // n % 2 == 1) for n in LEVELS], axis=1)
    level_masks = np.stack([levels, levels_t], axis=1).reshape(P, -1).astype(np.int32)
    return consts, level_masks, ret_eps.astype(np.float32)


def bucket_runs():
    dist = T - 1 - np.arange(T)
    exact = BUCKETS // 2
    d_f = np.maximum(dist, 1).astype(np.float32)
    large = exact + (np.log(d_f / exact) / math.log(P / exact) * (BUCKETS - exact)).astype(np.int32)
    bucket = np.where(dist < exact, dist, np.minimum(large, BUCKETS - 1))
    starts = [0] + [i for i in range(1, T) if bucket[i] != bucket[i - 1]] + [T]
    return [(int(bucket[a]), a, b) for a, b in zip(starts, starts[1:])]


_INS = ["x", "norm_w", "w_in", "w_out", "rwkv_mu", "rwkv_w0", "rwkv_w2", "rwkv_a0", "rwkv_a2", "rwkv_k_k",
        "rwkv_k_a", "rwkv_r_k", "rwkv_lnx_w", "rwkv_lnx_b", "conv_w", "rel_bias", "final_norm_w"]


def kernel(**inputs):
    import numpy as _np
    import concourse.bacc as _bacc
    from concourse.bass_utils import run_bass_kernel_spmd as _run

    nc = _bacc.Bacc("TRN2", target_bir_lowering=False, num_devices=1)
    arrays, args = {}, []

    def give(name, a):
        a = _np.ascontiguousarray(a)
        arrays[f"in_{name}_dram"] = a
        args.append(nc.dram_tensor(f"in_{name}_dram", a.shape, mybir.dt.from_np(a.dtype), kind="ExternalInput").ap())

    for name in _INS:
        give(name, inputs[name])
    for name, a in zip(("consts", "level_masks", "ret_eps"), shape_constants()):
        give(name, a)
    args.append(nc.dram_tensor("x_scratch", (KT, P, T), F32, kind="Internal").ap())
    args.append(nc.dram_tensor("bias_scratch", (HEADS, P, DIST + 1), F32, kind="Internal").ap())
    for n in ("a_scratch", "t_scratch", "tt_scratch"):
        args.append(nc.dram_tensor(n, (MATS, P, CH), F32, kind="Internal").ap())
    args.append(nc.dram_tensor("out_0_dram", (1, T, D), F32, kind="ExternalOutput").ap())
    trunk_kernel(nc, *args)
    r = _run(nc, [arrays], core_ids=[0])
    return r.results[0]["out_0_dram"]
```

```python
import math
from contextlib import ExitStack

import numpy as np

import concourse.bass as bass
from concourse import mybir

F32 = mybir.dt.float32
F32R = mybir.dt.float32r
I32 = mybir.dt.int32
U8 = mybir.dt.uint8
ALU = mybir.AluOpType
ACT = mybir.ActivationFunctionType
AX_X = mybir.AxisListType.X

P = 128
DEPTH = 2
T = 512
D = 1024
G = 256
HEADS = 4
N = 64
NT = T // P
KT = D // P
CH = 64
NCH = T // CH
MATS = NT * HEADS
LORA = 32
BUCKETS = 32
DECAY = math.exp(-0.5)
NORM_EPS = 1e-6
LNX_EPS = 64e-5
MASKED = -1e30
BLK = 16
LEVELS = [16, 32]
RAW, HI, LO = 3, 3, 3
DIST = T + P

RWKV, CONV, MOBA, RET = 0, 1088, 2112, 3136
TILE_COLS = {"wa": 768, "rwkv_g0": 832, "rwkv_g1": 960}
for _base, _names in ((RWKV, ("r", "k", "v")), (CONV, ("cb", "cc", "ch", "conv_g")),
                      (MOBA, ("mq", "mk", "mv", "moba_g")), (RET, ("rq", "rk", "rv", "ret_g"))):
    for _i, _n in enumerate(_names):
        for _p in range(2):
            TILE_COLS[f"{_n}{_p}"] = _base + G * _i + P * _p
TILES = ["k0", "k1", "wa", "r0", "r1", "v0", "v1", "rwkv_g0", "rwkv_g1",
         "rq0", "rq1", "rk0", "rk1", "rv0", "rv1", "ret_g0", "ret_g1",
         "mq0", "mq1", "mk0", "mk1", "mv0", "mv1", "moba_g0", "moba_g1",
         "cc0", "cc1", "ch0", "ch1", "cb0", "cb1", "conv_g0", "conv_g1"]
LAST_TILE = TILES[-1]
OUT_TILES = [f"out{m}" for m in range(KT)]
STREAM = TILES + OUT_TILES

MU, W0, A0, KKP, KAP, RKP, LNW, LNB, CONVW, NORMW = 0, 7, 9, 11, 13, 15, 17, 19, 21, 27
N_ROWS, N_PAR = 27, 35
MU_ROW = {"r0": 0, "r1": 1, "k0": 2, "k1": 3, "v0": 4, "v1": 5, "wa": 6}
MUC, HW0, HA0, KA2, KA1 = 0, 7, 9, 11, 13
N_DER = 15

CONSTS = [("ident", 128), ("eps", 2), ("one", 1), ("head_mean", 128), ("all_mean", 1), ("rot", 128), ("causal", 128),
          ("score_mask", 256), ("eye64", 64), ("k_decay", 16),
          ("chunk_reset", 512), ("cos", 512), ("sin", 512)]
COL, _at = {}, 0
for _n, _w in CONSTS:
    COL[_n] = (_at, _at + _w)
    _at += _w
N_CONST = _at

def layer_steps():
    s = [("norm",), ("k_pair",)]
    s += [("shift", "k0"), ("shift", "k1"), ("kk_input",), ("shift", "wa"), ("shift", "r0"), ("kk_square",),
          ("kk_norm",), ("lora_tanh",), ("shift", "r1"), ("lora",), ("shift", "v0"), ("decay_scan",), ("shift", "v1"),
          ("decay_exp",), ("factors", 0), ("gate", "rwkv", 0), ("factors", 1), ("gate", "rwkv", 1), ("factors", 2)]
    s += [("copy", "rq0"), ("copy", "rq1"), ("bonus",), ("rotate", "rq0"), ("scores", 0),
          ("copy", "rk0"), ("rotate", "rq1"), ("scores", 1), ("copy", "rk1"), ("rotate", "rk0"), ("to_rows", "v"), ("scores", 2),
          ("copy", "rv0"), ("rotate", "rk1"), ("scores", 3), ("copy", "rv1"), ("to_rows", "kap"), ("to_rows", "bet"), ("block_rows", 0),
          ("gate", "ret", 0), ("to_rows", "rv"), ("to_rows", "alp"), ("block_rows", 1), ("gate", "ret", 1), ("to_rows", "rk"),
          ("block_rows", 2)]
    last = [("copy", j) for j in ("mq0", "mq1", "mk0", "mk1", "mv0", "mv1")] + [("gate", "moba", 0), ("gate", "moba", 1)]
    last += [("conv_c", 0), ("conv_c", 1), ("conv_h", 0), ("conv_h", 1), ("conv_b", 0), ("conv_b", 1), ("gate", "conv", 0), ("gate", "conv", 1)]
    slots = 2 * len(last)
    mid, after = [[] for _ in range(slots)], [[] for _ in range(slots)]
    after[0].append(("retain_state",))
    for i in range(5):
        after[i].append(("retain", i))
    after[2].append(("retain_out", 0))
    after[4].append(("retain_out", 1))
    for i, step in [(2, ("chunk_b", 0)), (3, ("chunk_b", 1)), (INV0, ("inverse_x", 16)), (INV0 + 1, ("inverse_y", 16)), (INV0 + 2, ("inverse_yt", 16)),
                    (INV0 + 3, ("inverse_x", 32)), (INV0 + 4, ("inverse_yt", 32)), (9, ("ret_stat",)), (10, ("chunk_uw",)),
                    (11, ("chunk_g", 0)), (12, ("chunk_g", 1)), (12, ("to_rows", "mv")), (13, ("chunk_h", 0)), (14, ("chunk_h", 1)),
                    (16, ("chunk_q", 0)), (17, ("chunk_q", 1)), (18, ("chunk_y1", 0)), (19, ("chunk_y1", 1)),
                    (21, ("chunk_y",)), (22, ("ln_mean",)), (22, ("ln_square",)), (23, ("ln_var",))]:
        mid[i].append(step)
    for c in range(1, NCH - 1):
        mid[14 + c].insert(0, ("chain", c))
    after[10] += [("ret_root",), ("ret_recip", 0)]
    for g in range(18):
        after[11 + g].append(("attend", g))
        if g in (9, 17):
            after[11 + g].append(("attend_out", g // 10))
    for i, step in [(11, ("ret_recip", 1)), (12, ("ret_recip", 2)), (13, ("ret_recip", 3)), (15, ("ret_finish", 0)), (17, ("ret_finish", 1)),
                    (21, ("conv_taps", 0)), (24, ("conv_taps", 1)), (23, ("ln_recip", 0)), (25, ("ln_recip", 1)), (26, ("ln_recip", 2)), (27, ("ln_recip", 3)),
                    (27, ("ln_scale", 0)), (28, ("ln_scale", 1)), (29, ("rwkv_finish", 0)), (30, ("rwkv_finish", 1)), (30, ("conv_out", 0))]:
        after[i].append(step)
    for i in range(slots):
        step, job = last[i // 2], project_name(last[i // 2])
        s += [("quarter", job, 2 * (i % 2))] + mid[i] + [("quarter", job, 2 * (i % 2) + 1)]
        if i < slots - 1:
            s += [step] * (i % 2) + after[i]
    s += [("split_y", k) for k in Y_ORDER[:5]] + [last[-1]]
    s += [("conv_out", 1)] + [("split_y", k) for k in Y_ORDER[5:]] + [("project_out", m) for m in range(KT)]
    return s


INV0 = 4


def project_name(step):
    kind = step[0]
    if kind == "gate":
        return f"{step[1]}_g{step[2]}"
    if kind in ("conv_c", "conv_h", "conv_b"):
        return {"conv_c": "cc", "conv_h": "ch", "conv_b": "cb"}[kind] + str(step[1])
    return step[1]


Y_ORDER = [6, 7, 4, 5, 0, 1, 2, 3]
STEPS = layer_steps()


def bank_jobs():
    pro = [("norm_cols", 7, 1)] + [(f"x_in{m}", m, 1) for m in range(KT)] + [("params0", 3, 1), ("params1", 4, 1)]
    layer = []
    projections = []

    def proj(name, readers):
        if name not in projections:
            layer.append((name, 2 if name == "wa" else (len(projections) - (len(projections) > 2)) % 2, readers))
            projections.append(name)

    turn = [0]

    def any6(name, readers=1, banks=(2, 3, 4, 5, 6, 7)):
        layer.append((name, banks[turn[0] % len(banks)], readers))
        turn[0] += 1

    for step in STEPS:
        kind = step[0]
        if kind == "norm":
            layer.append(("rn", 2, 0))
        elif kind == "k_pair":
            proj("k0", 2), proj("k1", 2)
        elif kind == "quarter":
            proj(step[1], 2 if "_g" in step[1] else 1)
        elif kind == "shift":
            proj(step[1], 2)
        elif kind == "copy":
            proj(step[1], 1)
        elif kind == "gate":
            proj(f"{step[1]}_g{step[2]}", 2)
        elif kind == "kk_square":
            any6("kk0"), any6("kk1")
        elif kind == "lora":
            for n in ("zw0", "zw1", "za0", "za1"):
                any6(n)
        elif kind == "bonus":
            any6("bonus0"), any6("bonus1")
        elif kind == "to_rows":
            for p in range(2):
                if step[1] == "mv":
                    layer.append((f"rows_mv{p}", 7 - 2 * p, 1))
                else:
                    any6(f"rows_{step[1]}{p}")
        elif kind == "scores":
            for p in range(2):
                for hh in range(2):
                    any6(f"scores{step[1]}{p}{hh}")
        elif kind == "inverse_x":
            layer += [(f"x{step[1]}_0", 5, 1), (f"x{step[1]}_1", 6, 1)]
        elif kind == "inverse_y":
            layer += [(f"y{step[1]}_0", 5, 1), (f"y{step[1]}_1", 6, 1)]
        elif kind == "inverse_yt":
            layer += [(f"yt{step[1]}_0", 7, 1), (f"yt{step[1]}_1", 5, 1)]
        elif kind == "rotate":
            any6(f"rot_{step[1]}")
        elif kind == "attend":
            g = step[1]
            if g == 2 or g == 10:
                layer.append((f"moba_y{g // 10}", 4, 1))
            if 1 <= g <= 16:
                layer.append((f"pt{g - 1}", 3, 1))
            if g <= 15:
                layer.append((f"s{g}", 2, 1))
        elif kind == "chunk_b":
            layer.append((f"b{step[1]}", 5 + step[1], 1))
        elif kind == "chunk_uw":
            layer += [(f"uw{t}", (7, 5, 6, 7)[t], 1) for t in range(NT)]
        elif kind == "chunk_g":
            layer.append((f"g{step[1]}", 5 + step[1], 1))
        elif kind == "chunk_h":
            layer.append((f"h{step[1]}", 7 - 2 * step[1], 1))
        elif kind == "chunk_q":
            layer.append((f"q{step[1]}", 6 - step[1], 1))
        elif kind == "chunk_y1":
            layer.append((f"y1{step[1]}", 5 + step[1], 1))
        elif kind == "chain":
            layer.append((f"chain{step[1]}", 7, 1))
        elif kind == "chunk_y":
            layer += [("y20", 5, 1), ("y21", 6, 1)]
        elif kind == "retain":
            i = step[1]
            if i == 1 or i == 3:
                layer.append((f"ret_y{i // 3}", 4, 1))
            if i < HEADS:
                layer.append((f"rs{i}", 2 + i % 2, 1))
        elif kind == "retain_state":
            layer.append(("ret_state", 4, 1))
        elif kind == "ln_mean":
            layer += [("mean0", 5, 1), ("mean1", 6, 1)]
        elif kind == "ln_var":
            layer += [("var0", 7, 1), ("var1", 5, 1)]
        elif kind == "ret_stat":
            layer += [("ret_ms0", 2, 1), ("ret_ms1", 3, 1)]
        elif kind == "project_out":
            proj(f"out{step[1]}", 1)
            if step[1] == KT - 1:
                layer.append(("stat", 2, 1))
    epi = [(f"row{m}", 3 + m % 5, 1) for m in range(KT)]
    return pro, layer, epi


def trunk_kernel(nc, x, norm_w, w_in, w_out, rwkv_mu, rwkv_w0, rwkv_w2, rwkv_a0, rwkv_a2, rwkv_k_k,
                 rwkv_k_a, rwkv_r_k, rwkv_lnx_w, rwkv_lnx_b, conv_w, rel_bias, final_norm_w,
                 consts, level_masks, ret_eps, x_scratch, bias_scratch, a_scratch, t_scratch, tt_scratch, out):
    pro, per_layer, epi = bank_jobs()
    place = {}
    full_count, read_count = [0] * 8, [0] * 8
    for part, names in (("pro", pro), ("layer", per_layer), ("epi", epi)):
        if part == "layer":
            pro_full, pro_read = list(full_count), list(read_count)
            full_count, read_count = [0] * 8, [0] * 8
        if part == "epi":
            lay_full, lay_read = list(full_count), list(read_count)
            full_count, read_count = [0] * 8, [0] * 8
        for name, bank, readers in names:
            place[part, name] = (bank, full_count[bank], read_count[bank], readers)
            full_count[bank] += 1
            read_count[bank] += readers

    def locate(name, layer):
        part = "pro" if layer < 0 else "epi" if layer >= DEPTH else "layer"
        bank, nf, nr, readers = place[part, name]
        if part != "pro":
            nf += pro_full[bank] + layer * lay_full[bank]
            nr += pro_read[bank] + layer * lay_read[bank]
        return bank, nf, nr, readers

    with ExitStack() as ctx:
        def sb(name, shape, dt=F32):
            return ctx.enter_context(nc.sbuf_tensor(name, shape, dt))

        bank = [ctx.enter_context(nc.psum_tensor(f"bank{i}", [P, 512], F32)) for i in range(8)]
        XY = sb("x_or_y", [P, KT, T])
        act_hi = sb("act_hi", [P, KT, T], F32R)
        act_lo = sb("act_lo", [P, KT, T], F32R)
        w_raw = sb("w_raw", [P, RAW, KT, P])
        w_hi = sb("w_hi", [P, HI, KT, P], F32R)
        w_lo = sb("w_lo", [P, LO, KT, P], F32R)
        PG = 1040
        pages = sb("pages", [P, 25 * PG])
        cst = sb("constants", [P, N_CONST])
        lmask = sb("level_mask", [P, 2, len(LEVELS), CH], U8)
        bias = sb("bias", [P, HEADS, T])
        par = sb("params", [P, DEPTH, N_PAR])
        der = sb("params_derived", [P, DEPTH, N_DER])
        lora_w = sb("lora_w", [2 * LORA, DEPTH, G])
        small = sb("small", [P, 32])
        w_end = sb("chunk_decay", [P, 2, NCH])

        def page(i, n=1):
            return pages[:, i * PG:(i + n - 1) * PG + 1024]

        def pair(i):
            return page(i).rearrange("p (a t) -> p a t", a=2)

        def half(i, j):
            return pages[:, i * PG + 512 * j:i * PG + 512 * (j + 1)]

        def const(name):
            a, b = COL[name]
            return cst[:, a:b]

        ident, head_mean, all_mean = const("ident"), const("head_mean"), const("all_mean")
        R, K, V, TH, TA, KN, PI = (pair(i) for i in (0, 1, 2, 3, 4, 5, 7))
        Pd = pages[:, 6 * PG:7 * PG].rearrange("p (a c t) -> p a c t", a=2, c=NCH)
        AR = pages[:, 8 * PG:8 * PG + 2048].rearrange("p (x a t) -> p x a t", x=2, a=2)
        WA = page(10)[:, 0:T]
        KF = pair(24)
        RRAW, MVRAW = pair(24), pair(10)
        BA = pages[:, 11 * PG:11 * PG + 2048].rearrange("p (m x i) -> p m x i", m=MATS, x=2)
        rows = {n: page(i).rearrange("p (t c) -> p t c", t=NT)
                for n, i in (("bet", 13), ("kap", 14), ("v", 15), ("mv", 2), ("rv", 23), ("rk", 20))}
        SC = pages[:, 16 * PG:16 * PG + MATS * 256].rearrange("p (m c) -> p m c", m=MATS)
        MQ, MK = pair(4), pair(7)
        Ti, TiT, Xm = (page(i).rearrange("p (m c) -> p m c", m=MATS) for i in (3, 5, 6))
        RQ, RK = pair(21), pair(22)
        bias_rows = pages[:, 21 * PG:21 * PG + HEADS * DIST].rearrange("p (h c) -> p h c", h=HEADS)
        bias_table = pages[:, 21 * PG + HEADS * DIST:21 * PG + HEADS * DIST + BUCKETS * HEADS].rearrange("p (b h) -> p b h", h=HEADS)
        out_rows = pages[:, 17 * PG:(17 + NT) * PG].rearrange("p (t c) -> p t c", c=PG)
        norm_rows = page(10)[0:DEPTH * KT, 0:P]
        par_rows = page(24)[0:N_ROWS, 0:DEPTH * P].rearrange("r (l c) -> r l c", l=DEPTH)
        mask_words = page(11)[:, 0:2 * len(LEVELS) * CH].bitcast(I32)
        A_blk, T_blk, TT_blk, AT_prod = (page(6)[:, 256 * i:256 * (i + 1)].rearrange("p (i j) -> p i j", i=BLK) for i in range(4))
        zeros = page(9)
        eps_page = page(2)
        fnorm = page(2)
        mean_sq, root, rms = small[:, 8:12], small[:, 12:16], small[:, 16:20]
        UW = pages[:, 21 * PG:21 * PG + 2048].rearrange("p (m x i) -> p m x i", m=MATS, x=2)
        GT, HP, ST = (page(i).rearrange("p (a c i) -> p a c i", a=2, c=NCH) for i in (5, 3, 6))
        RSB, PB, PT = pair(1), pair(1), pair(10)
        Y1 = pair(24)
        CU = pages[:, 23 * PG:24 * PG].rearrange("p (a t) -> p a t", a=2)
        CA = pair(12)
        RST = half(24, 1)[:, 0:2 * 3 * N].rearrange("p (a c i) -> p a c i", a=2, c=NT - 1)
        LNS, RY, RSQ = pair(11), pair(8), pair(24)

        sem = {}

        def s(name):
            if name not in sem:
                sem[name] = ctx.enter_context(nc.semaphore(name))
            return sem[name]

        bank_full = [s(f"bank{i}_full") for i in range(8)]
        bank_read = [s(f"bank{i}_read") for i in range(8)]

        SIGNALS = {
            "h_raw": KT, "h_hi": KT, "h_split": KT,
            "kk_sq": 2, "kk_unit": 2, "lora_in": 1, "decay_sum": 2,
            "decay_exp": 4, "beta": 1, "kappa": 1, "alpha": 1, "rho": 1, "rkv": 2, "pads": 1, "blocks_done": 1, "ret_prefix": 1, "conv_tap": 2, "ln_scaled": 2, "ln_affine": 2,
            "rotated": 4, "logit_max": 16, "prob": 16, "prob_norm": 16, "first_state": 1, "ln_sq": 2,
            "ret_sq": 2, "ret_root": 2, "y_hi": KT, "y_split": KT, "y_conv": 2, "y_ret": 2, "y_rwkv": 2,
            "conv_pad": 1,
        }

        def at(name, layer, n=None):
            return s(name), layer * SIGNALS[name] + (SIGNALS[name] if n is None else n)

        def full(job, layer):
            b, nf, _, _ = locate(job, layer)
            return bank_full[b], nf + 1

        def read(job, layer, n=None):
            b, _, nr, readers = locate(job, layer)
            return bank_read[b], nr + (readers if n is None else n)

        def ps(job, layer):
            return bank[locate(job, layer)[0]]

        def done(job, layer):
            return bank_read[locate(job, layer)[0]]

        def unit(u):
            h, blk = divmod(u, NT)
            return h, h // 2, slice(64 * (h % 2), 64 * (h % 2) + 64), blk

        block = ctx.enter_context(nc.Block())

        @block.sync
        def _(sp):
            def load(dst, src, name):
                sp.dma_start(dst, src).then_inc(s(name), 16)

            a0, a1 = COL["ident"][0], COL["one"][1]
            load(cst[:, a0:a1], consts[:, a0:a1], "const_a")
            load(norm_rows, norm_w.rearrange("l (k c) -> (l k) c", c=P), "norm_loaded")

            n_stream = len(STREAM)

            def load_weights(i):
                layer, j = divmod(i, n_stream)
                if i >= RAW:
                    sp.wait_ge(s("w_split"), i - RAW + 1)
                if j < len(TILES):
                    c = TILE_COLS[TILES[j]]
                    src = w_in[layer, :, c:c + P]
                else:
                    src = w_out[layer, :, (j - len(TILES)) * P:(j - len(TILES) + 1) * P]
                sp.dma_start(w_raw[:, i % RAW, :, :], src.rearrange("(k p) c -> p k c", p=P)).then_inc(s(f"w_loaded{i % RAW}"), 16)

            def load_x(t):
                load(page(17 + t), x[0, t * P:(t + 1) * P, :], f"x_loaded{t}")

            load_x(0)
            load(bias_table, rel_bias.partition_broadcast(P), "bias_in")
            load_weights(0)
            load_x(1)
            load_x(2)
            load_x(3)
            load_weights(1)
            sp.wait_ge(s("par_clear"), 1)
            rws = lambda a, n: a.rearrange("l (r c) -> r l c", c=P)[0:n]
            load(par_rows[0:6], rws(rwkv_mu[:, 0:768], 6), "par_loaded")
            load(par_rows[6:7, :, 0:64], rwkv_mu[:, 768:832].rearrange("l (r c) -> r l c", r=1), "par_loaded")
            for r0, a in ((W0, rwkv_w0), (A0, rwkv_a0), (KKP, rwkv_k_k), (KAP, rwkv_k_a), (LNW, rwkv_lnx_w), (LNB, rwkv_lnx_b)):
                load(par_rows[r0:r0 + 2], rws(a, 2), "par_loaded")
            load(par_rows[RKP:RKP + 2], rwkv_r_k.rearrange("l (r h) n -> r l (h n)", r=2), "par_loaded")
            load(par_rows[CONVW:CONVW + 6], conv_w.rearrange("l j (p c) -> (j p) l c", p=2), "par_loaded")
            load_weights(2)
            load(cst[:, a1:], consts[:, a1:], "const_b")
            load(mask_words, level_masks, "const_b")
            load(lora_w[0:LORA], rwkv_w2.rearrange("l k c -> k l c"), "const_b")
            load(lora_w[LORA:2 * LORA], rwkv_a2.rearrange("l k c -> k l c"), "const_b")

            def blocks_of(scratch):
                v = scratch.rearrange("m (c x) y -> (m c) x y", c=2)
                return [v[:, g * BLK:(g + 1) * BLK, g * BLK:(g + 1) * BLK] for g in range(CH // BLK)]

            def clear_inverses():
                sp.wait_ge(s("zeros"), 1)
                for scratch in (t_scratch, tt_scratch):
                    load(scratch.rearrange("m q y -> q m y"), zeros.rearrange("q (m y) -> q m y", y=CH), "cleared")

            def blocks_out(layer):
                sp.wait_ge(*read("scores311", layer))
                load(a_scratch.rearrange("m q y -> q m y"), SC[:, :, 128:192], "a_out")
                sp.wait_ge(s("a_out"), 16 * (layer + 1))
                for g, src in enumerate(blocks_of(a_scratch)):
                    load(A_blk[32 * g:32 * g + 32], src, "blocks_in")

            def inverses_back(layer):
                sp.wait_ge(*at("blocks_done", layer))
                sp.wait_ge(s("cleared"), 32)
                for scratch, blk in ((t_scratch, T_blk), (tt_scratch, TT_blk)):
                    for g, dst in enumerate(blocks_of(scratch)):
                        load(dst, blk[32 * g:32 * g + 32], "t_out")
                sp.wait_ge(s("t_out"), 128 * (layer + 1))
                load(Ti, t_scratch.rearrange("m q y -> q m y"), "t_back")
                load(TiT, tt_scratch.rearrange("m q y -> q m y"), "t_back")

            def spill_first_x():
                for m in range(KT):
                    sp.wait_ge(*read(f"x_in{m}", -1))
                    load(x_scratch[m], XY[:, m, :], "x_spill")

            def skew_bias():
                sp.wait_ge(s("bias_rows"), 1)
                load(bias_scratch.rearrange("h q c -> q h c")[:, :, 0:DIST], bias_rows, "bias_out")
                sp.wait_ge(s("bias_out"), 16)
                skewed = bias_scratch.rearrange("h q c -> h (q c)")[:, 0:P * DIST].rearrange("h (q c) -> q h c", c=DIST)
                load(bias[:, :, :], skewed[:, :, P - 1:P - 1 + T], "bias_back")

            i = RAW
            for layer in range(DEPTH):
                while i < (layer + 1) * n_stream:
                    j = i - layer * n_stream
                    if j == len(TILES) + 4:
                        for k, m in enumerate(Y_ORDER):
                            sp.wait_ge(*at("y_split", layer, k + 1))
                            sp.wait_ge(s("x_spill"), 16 * KT * (layer + 1))
                            load(XY[:, m, :], x_scratch[m], f"x_back{m}")
                    if i == 2 * RAW:
                        spill_first_x()
                    if i == 3 * RAW:
                        skew_bias()
                    if layer == DEPTH - 1 and j == len(TILES):
                        sp.wait_ge(*full("moba_y1", layer))
                        load(fnorm, final_norm_w.rearrange("(r d) -> r d", r=1)[0].partition_broadcast(P), "fnorm_loaded")
                    if i == 4 * RAW:
                        clear_inverses()
                    if j == TILES.index("mq1"):
                        blocks_out(layer)
                    if j == TILES.index("mk1"):
                        inverses_back(layer)
                    if j == TILES.index("mq0"):
                        sp.wait_ge(*full("rows_v1", layer))
                        for p in range(2):
                            sp.wait_ge(*read(f"bonus{p}", layer))
                        load(eps_page, ret_eps, "ret_eps")
                    load_weights(i)
                    i += 1
                if layer < DEPTH - 1:
                    for k in range(RAW):
                        load_weights(i)
                        i += 1
                    for m in range(KT):
                        sp.wait_ge(*read(f"out{m}", layer))
                        load(x_scratch[m], XY[:, m, :], "x_spill")
            for t in range(NT):
                sp.wait_ge(s(f"scaled{t}"), 1)
                sp.dma_start(out[0, t * P:(t + 1) * P, :], page(17 + t)).then_inc(s("stored"), 16)
            sp.wait_ge(s("stored"), 16 * NT)

        @block.gpsimd
        def _(pool):
            pool.memset(par_rows, 0.0).then_inc(s("par_clear"), 1)
            pool.memset(zeros, 0.0).then_inc(s("zeros"), 1)
            H = KT // 2
            pool.wait_ge(s("const_a"), 16)
            n_stream = len(STREAM)
            for i in range(DEPTH * n_stream):
                pool.wait_ge(s(f"w_loaded{i % RAW}"), 16 * (i // RAW + 1))
                if i >= HI:
                    before = divmod(i - HI, n_stream)
                    pool.wait_ge(*full(STREAM[before[1]], before[0]))
                for a in range(2):
                    k = slice(a * H, (a + 1) * H)
                    raw = w_raw[:, i % RAW, k, :]
                    pool.tensor_tensor(w_hi[:, i % HI, k, :], raw, const("one").unsqueeze(2).to_broadcast([P, H, P]), ALU.mult).then_inc(s("w_high"), 1)
                if i >= LO:
                    before = divmod(i - LO, n_stream)
                    pool.wait_ge(*full(STREAM[before[1]], before[0]))
                for a in range(2):
                    k = slice(a * H, (a + 1) * H)
                    pool.wait_ge(s("w_high"), 2 * i + a + 1)
                    ins = pool.tensor_tensor(w_lo[:, i % LO, k, :], w_raw[:, i % RAW, k, :], w_hi[:, i % HI, k, :].bitcast(F32), ALU.subtract)
                ins.then_inc(s("w_split"), 1)

        @block.tensor
        def _(pe):
            mm = pe.matmul

            def begin(job, layer):
                b, nf, nr, _ = locate(job, layer)
                if nr > 0:
                    pe.wait_ge(bank_read[b], nr)
                return bank[b]

            def end(ins, job, layer):
                ins.then_inc(bank_full[locate(job, layer)[0]], 1)

            pe.wait_ge(s("const_a"), 16)
            pe.wait_ge(s("norm_loaded"), 16)
            b = begin("norm_cols", -1)
            end(pe.transpose(b[:, 0:DEPTH * KT], norm_rows, ident[0:DEPTH * KT, 0:DEPTH * KT]), "norm_cols", -1)
            for t in range(NT):
                pe.wait_ge(s(f"x_loaded{t}"), 16)
                for m in range(KT):
                    b = begin(f"x_in{m}", -1) if t == 0 else ps(f"x_in{m}", -1)
                    ins = pe.transpose(b[:, t * P:(t + 1) * P], page(17 + t)[:, m * P:(m + 1) * P], ident)
                    if t == NT - 1:
                        end(ins, f"x_in{m}", -1)

            def stat(layer, last):
                b = ps("stat", layer) if last else begin("stat", layer)
                if last:
                    pe.wait_ge(s("x_sq"), (layer + 1) * KT)
                else:
                    pe.wait_ge(s("sq_added"), (layer + 1) * (KT - 2))
                src = half(24, 1) if last else half(11, 0)
                for t in range(NT):
                    ins = mm(b[:, t:t + 1], src[:, t * P:(t + 1) * P], const("all_mean"),
                             start=not last and t == 0, stop=last, skip_group_check=True)
                if last:
                    end(ins, "stat", layer)

            def row(m):
                pe.wait_ge(*read(f"out{m}", DEPTH - 1))
                b = begin(f"row{m}", DEPTH)
                for t in range(NT):
                    ins = pe.transpose(b[:, t * P:(t + 1) * P], XY[:, m, t * P:(t + 1) * P], ident)
                end(ins, f"row{m}", DEPTH)

            for layer in range(DEPTH):
                in_quarters = set()

                def product(job, n):
                    i = layer * len(STREAM) + STREAM.index(job)
                    if n == 0:
                        pe.wait_ge(s("w_split"), i + 1)
                        begin(job, layer)
                    is_out = job in OUT_TILES
                    k = Y_ORDER[n] if is_out or job == LAST_TILE else n
                    if job in ("k0", "out0"):
                        pe.wait_ge(*at("y_split" if is_out else "h_split", layer, n + 1))
                    b = ps(job, layer)
                    hi, lo = w_hi[:, i % HI, k, :], w_lo[:, i % LO, k, :]
                    mm(b[:, :], hi, act_hi[:, k, :], start=n == 0, stop=False)
                    mm(b[:, :], lo, act_hi[:, k, :], start=False, stop=False)
                    ins = mm(b[:, :], hi, act_lo[:, k, :], start=False, stop=n == KT - 1)
                    if job == LAST_TILE and n < KT - 1:
                        ins.then_inc(s("h_used"), 1)
                    if n == KT - 1:
                        end(ins, job, layer)

                def quarter(job, q):
                    in_quarters.add(job)
                    for n in range(q * KT // 4, (q + 1) * KT // 4):
                        product(job, n)

                def project(job):
                    if job not in in_quarters:
                        for n in range(KT):
                            product(job, n)

                def keep_warm():
                    b = begin("k0", layer)
                    for _ in range(8):
                        mm(b[:, 0:P], ident, ident, start=True, stop=True)

                def norm():
                    pe.wait_ge(s("rms"), layer + 1)
                    b = begin("rn", layer)
                    for t in range(NT):
                        ins = mm(b[:, t * P:(t + 1) * P], rms[:, t:t + 1].to_broadcast([P, P]), ident, start=True, stop=True)
                    end(ins, "rn", layer)
                    if layer == 0:
                        pe.wait_ge(s("par_loaded"), 16 * 10)
                        for l in range(DEPTH):
                            b = begin(f"params{l}", -1)
                            end(pe.transpose(b[:, 0:N_ROWS], par_rows[:, l, :], ident[0:N_ROWS, 0:N_ROWS]), f"params{l}", -1)

                def k_pair():
                    keep_warm()
                    for n in range(KT):
                        product("k0", n)
                        product("k1", n)

                def shift(job):
                    if job not in ("k0", "k1"):
                        project(job)

                def copy(job):
                    project(job)

                def gate(group, p):
                    project(f"{group}_g{p}")

                def conv_c(p):
                    project(f"cc{p}")

                def conv_h(p):
                    project(f"ch{p}")

                def conv_b(p):
                    project(f"cb{p}")

                def kk_square():
                    if layer == 0:
                        pe.wait_ge(s("const_b"), 16 * 4)
                    for p in range(2):
                        pe.wait_ge(*at("kk_sq", layer, p + 1))
                        b = begin(f"kk{p}", layer)
                        end(mm(b[:, :], head_mean, KN[:, p, :], start=True, stop=True), f"kk{p}", layer)

                def lora():
                    pe.wait_ge(*at("lora_in", layer))
                    for z, r0 in (("zw", 0), ("za", LORA)):
                        for p in range(2):
                            b = begin(f"{z}{p}", layer)
                            end(mm(b[:, :], lora_w[r0:r0 + LORA, layer, p * P:(p + 1) * P], WA[r0:r0 + LORA, :], start=True, stop=True), f"{z}{p}", layer)

                def bonus():
                    for p in range(2):
                        pe.wait_ge(*at("rkv", layer, p + 1))
                        b = begin(f"bonus{p}", layer)
                        end(mm(b[:, :], head_mean, R[:, p, :], start=True, stop=True), f"bonus{p}", layer)

                def to_rows(what):
                    src = {"v": V, "kap": PI, "bet": TA, "alp": AR[:, 0], "mv": MVRAW, "rv": MVRAW, "rk": RK}[what]
                    for p in range(2):
                        if what in ("mv", "rv"):
                            pe.wait_ge(*read(f"{what}{p}", layer))
                        elif what == "rk":
                            pe.wait_ge(*at("rotated", layer, 3 + p))
                        elif what == "v":
                            pe.wait_ge(*read(f"v{p}", layer))
                        else:
                            pe.wait_ge(*at({"kap": "kappa", "bet": "beta", "alp": "alpha"}[what], layer))
                        b = begin(f"rows_{what}{p}", layer)
                        for t in range(NT):
                            ins = pe.transpose(b[:, t * P:(t + 1) * P], src[:, p, t * P:(t + 1) * P], ident)
                        end(ins, f"rows_{what}{p}", layer)

                def scores(t):
                    if t == 0:
                        pe.wait_ge(*at("rho", layer))
                    for p in range(2):
                        for hh in range(2):
                            job = f"scores{t}{p}{hh}"
                            b = begin(job, layer)
                            hr = slice(64 * hh, 64 * hh + 64)
                            for c in (2 * t, 2 * t + 1):
                                cs = slice(c * CH, (c + 1) * CH)
                                o = b[64 * (c % 2):64 * (c % 2) + 64, :]
                                mm(o[:, 0:128], PI[hr, p, cs], AR[hr, :, p, cs], start=True, stop=True)
                                ins = mm(o[:, 128:256], TA[hr, p, cs], AR[hr, :, p, cs], start=True, stop=True)
                            end(ins, job, layer)

                def inverse_x(n):
                    for g in range(2):
                        if n == LEVELS[0]:
                            pe.wait_ge(s("t_back"), 32 * (layer + 1))
                        else:
                            pe.wait_ge(*read(f"y{n // 2}_{g}", layer))
                        each_matrix(f"x{n}_{g}", SC[:, :, 128:192], Ti, g)

                def inverse_y(n):
                    for g in range(2):
                        pe.wait_ge(*read(f"x{n}_{g}", layer))
                        each_matrix(f"y{n}_{g}", TiT, Xm, g)

                def inverse_yt(n):
                    for g in range(2):
                        pe.wait_ge(*read(f"x{n}_{g}", layer))
                        if n > LEVELS[0]:
                            pe.wait_ge(*read(f"yt{n // 2}_{g}", layer))
                        each_matrix(f"yt{n}_{g}", Xm, TiT, g)

                def each_matrix(job, lhs, rhs, g):
                    b = begin(job, layer)
                    for i in range(8):
                        for c in range(2):
                            r = slice(64 * c, 64 * c + 64)
                            ins = mm(b[r, i * CH:(i + 1) * CH], lhs[r, 8 * g + i, :], rhs[r, 8 * g + i, :], start=True, stop=True)
                    end(ins, job, layer)

                def rotate(job):
                    pe.wait_ge(*read(job, layer))
                    b = begin(f"rot_{job}", layer)
                    end(mm(b[:, :], const("rot"), RRAW[:, int(job[-1]), :], start=True, stop=True), f"rot_{job}", layer)

                def attend(g):
                    if 2 <= g:
                        h, p, hr, qb = unit(g - 2)
                        if g == 2:
                            for q in range(2):
                                pe.wait_ge(*read(f"rows_mv{q}", layer))
                        pe.wait_ge(*read(f"pt{g - 2}", layer))
                        yb = begin(f"moba_y{p}", layer) if g in (2, 10) else ps(f"moba_y{p}", layer)
                        for kb in range(qb + 1):
                            ins = mm(yb[hr, qb * P:(qb + 1) * P], rows["mv"][:, kb, h * N:(h + 1) * N],
                                     PT[:, (g - 1) % 2, kb * P:(kb + 1) * P], start=kb == 0, stop=kb == qb)
                        if g in (9, 17):
                            end(ins, f"moba_y{p}", layer)
                    if 1 <= g <= 16:
                        pe.wait_ge(*at("prob_norm", layer, g))
                        b = begin(f"pt{g - 1}", layer)
                        for kb in range((g - 1) % NT + 1):
                            ins = pe.transpose(b[:, kb * P:(kb + 1) * P], PB[:, (g - 1) % 2, kb * P:(kb + 1) * P], ident)
                        end(ins, f"pt{g - 1}", layer)
                    if g <= 15:
                        h, p, hr, qb = unit(g)
                        if g == 0:
                            for j in ("mq0", "mq1", "mk0", "mk1"):
                                pe.wait_ge(*read(j, layer))
                        b = begin(f"s{g}", layer)
                        end(mm(b[:, 0:(qb + 1) * P], MQ[hr, p, qb * P:(qb + 1) * P], MK[hr, p, 0:(qb + 1) * P], start=True, stop=True), f"s{g}", layer)

                def chunk_b(g):
                    if g == 0:
                        for q in range(2):
                            pe.wait_ge(*read(f"rows_v{q}", layer))
                    b = begin(f"b{g}", layer)
                    for i in range(8):
                        m = 8 * g + i
                        t, h = divmod(m, HEADS)
                        for c in range(2):
                            r = slice(64 * c, 64 * c + 64)
                            ins = mm(b[r, i * CH:(i + 1) * CH], SC[r, m, 0:64], rows["v"][r, t, h * N:(h + 1) * N], start=True, stop=True)
                    end(ins, f"b{g}", layer)

                def chunk_uw():
                    for q in range(2):
                        pe.wait_ge(*read(f"rows_alp{q}", layer))
                        pe.wait_ge(*read(f"b{q}", layer))
                        pe.wait_ge(*read(f"yt{LEVELS[-1]}_{q}", layer))
                    for t in range(NT):
                        b = begin(f"uw{t}", layer)
                        for h in range(HEADS):
                            for c in range(2):
                                r = slice(64 * c, 64 * c + 64)
                                ins = mm(b[r, h * P:(h + 1) * P], TiT[r, t * HEADS + h, :], BA[r, t * HEADS + h, :, :], start=True, stop=True)
                        end(ins, f"uw{t}", layer)

                def chunk_g(c):
                    if c == 0:
                        for t in range(NT):
                            pe.wait_ge(*read(f"uw{t}", layer))
                        for q in range(2):
                            pe.wait_ge(*read(f"rows_bet{q}", layer))
                            pe.wait_ge(*read(f"rows_kap{q}", layer))
                    by_chunk("g", c)

                def chunk_h(c):
                    by_chunk("h", c)

                def chunk_q(c):
                    by_chunk("q", c)

                def chunk_y1(c):
                    by_chunk("y", c)

                def by_chunk(what, c):
                    U, W = UW[:, :, 0, :], UW[:, :, 1, :]
                    job = f"{what}{c}" if what != "y" else f"y1{c}"
                    b = begin(job, layer)
                    r = slice(64 * c, 64 * c + 64)
                    for p in range(2):
                        for t in range(NT):
                            for hh in range(2):
                                h = 2 * p + hh
                                m = t * HEADS + h
                                o = b[64 * hh:64 * hh + 64, (p * NT + t) * CH:(p * NT + t + 1) * CH]
                                bet, kap, v = (rows[x][r, t, h * N:(h + 1) * N] for x in ("bet", "kap", "v"))
                                if what == "g":
                                    ins = mm(o, W[r, m, :], bet, start=True, stop=True)
                                elif what == "q":
                                    ins = mm(o, W[r, m, :], SC[r, m, 192:256], start=True, stop=True)
                                elif what == "h":
                                    mm(o, kap, v, start=True, stop=False)
                                    ins = mm(o, bet, U[r, m, :], start=False, stop=True)
                                else:
                                    mm(o, v, SC[r, m, 64:128], start=True, stop=False)
                                    ins = mm(o, U[r, m, :], SC[r, m, 192:256], start=False, stop=True)
                    end(ins, job, layer)

                def chain(c):
                    if c == 1:
                        for j in ("g0", "g1"):
                            pe.wait_ge(*read(j, layer))
                        pe.wait_ge(*at("first_state", layer))
                    else:
                        pe.wait_ge(*read(f"chain{c - 1}", layer))
                    b = begin(f"chain{c}", layer)
                    for p in range(2):
                        for hh in range(2):
                            r = slice(64 * hh, 64 * hh + 64)
                            ins = mm(b[r, p * N:(p + 1) * N], GT[r, p, c, :], ST[r, p, c, :], start=True, stop=True)
                    end(ins, f"chain{c}", layer)

                def chunk_y():
                    pe.wait_ge(*read(f"chain{NCH - 2}", layer))
                    for c in range(2):
                        pe.wait_ge(*read(f"q{c}", layer))
                    for p in range(2):
                        b = begin(f"y2{p}", layer)
                        for c in range(1, NCH):
                            for hh in range(2):
                                r = slice(64 * hh, 64 * hh + 64)
                                ins = mm(b[r, c * CH:(c + 1) * CH], ST[r, p, c, :], AR[r, 1, p, c * CH:(c + 1) * CH], start=True, stop=True)
                        end(ins, f"y2{p}", layer)

                def retain_state():
                    for q in range(2):
                        pe.wait_ge(*read(f"rows_rv{q}", layer))
                        pe.wait_ge(*read(f"rows_rk{q}", layer))
                    b = begin("ret_state", layer)
                    for h in range(HEADS):
                        hs = slice(h * N, (h + 1) * N)
                        for c in range(NT - 1):
                            ins = mm(b[64 * (h % 2):64 * (h % 2) + 64, (h // 2 * (NT - 1) + c) * N:(h // 2 * (NT - 1) + c + 1) * N],
                                     rows["rk"][:, c, hs], rows["rv"][:, c, hs], start=True, stop=True)
                    end(ins, "ret_state", layer)

                def retain(i):
                    if i > 0:
                        h = i - 1
                        p, hr = h // 2, slice(64 * (h % 2), 64 * (h % 2) + 64)
                        if h == 0:
                            pe.wait_ge(*at("ret_prefix", layer))
                        pe.wait_ge(*read(f"rs{h}", layer))
                        yb = begin(f"ret_y{p}", layer) if h % 2 == 0 else ps(f"ret_y{p}", layer)
                        for c in range(NT):
                            ts = slice(c * P, (c + 1) * P)
                            ins = mm(yb[hr, ts], rows["rv"][:, c, h * N:(h + 1) * N], RSB[:, h % 2, ts], start=True, stop=c == 0)
                            if c > 0:
                                ins = mm(yb[hr, ts], RST[hr, p, c - 1, :], RQ[hr, p, ts], start=False, stop=True)
                        if h % 2:
                            end(ins, f"ret_y{p}", layer)
                    if i < HEADS:
                        p, hr = i // 2, slice(64 * (i % 2), 64 * (i % 2) + 64)
                        b = begin(f"rs{i}", layer)
                        for c in range(NT):
                            ts = slice(c * P, (c + 1) * P)
                            ins = mm(b[:, ts], RK[hr, p, ts], RQ[hr, p, ts], start=True, stop=True)
                        end(ins, f"rs{i}", layer)

                def ln_mean():
                    for p in range(2):
                        pe.wait_ge(*read(f"y2{p}", layer))
                        b = begin(f"mean{p}", layer)
                        end(mm(b[:, :], head_mean, Y1[:, p, :], start=True, stop=True), f"mean{p}", layer)

                def ln_var():
                    for p in range(2):
                        pe.wait_ge(*at("ln_sq", layer, p + 1))
                        b = begin(f"var{p}", layer)
                        end(mm(b[:, :], head_mean, LNS[:, p, :], start=True, stop=True), f"var{p}", layer)

                def ret_stat():
                    for p in range(2):
                        pe.wait_ge(*at("ret_sq", layer, p + 1))
                        b = begin(f"ret_ms{p}", layer)
                        end(mm(b[:, :], head_mean, RSQ[:, p, :], start=True, stop=True), f"ret_ms{p}", layer)

                def project_out(m):
                    project(f"out{m}")
                    for n in (m - 1, m) if m == KT - 1 else (m - 1,) if m > 0 else ():
                        if layer == DEPTH - 1:
                            row(n)
                        if n >= KT - 2:
                            stat(layer, n == KT - 1)

                run = dict(norm=norm, k_pair=k_pair, quarter=quarter, shift=shift, copy=copy, gate=gate, conv_c=conv_c, conv_h=conv_h,
                           conv_b=conv_b, kk_square=kk_square, lora=lora, bonus=bonus, to_rows=to_rows, scores=scores,
                           inverse_x=inverse_x, inverse_y=inverse_y, inverse_yt=inverse_yt, rotate=rotate, attend=attend,
                           chunk_b=chunk_b, chunk_uw=chunk_uw, chunk_g=chunk_g, chunk_h=chunk_h, chunk_q=chunk_q, chunk_y1=chunk_y1,
                           chain=chain, chunk_y=chunk_y, retain_state=retain_state, retain=retain,
                           ln_mean=ln_mean, ln_var=ln_var, ret_stat=ret_stat, project_out=project_out)
                for name, *args in STEPS:
                    if name in run:
                        run[name](*args)

        @block.scalar
        def _(act):
            go = act.activation
            act.wait_ge(s("const_a"), 16)
            go(small[:, 24:25], const("eps")[:, 0:1], ACT.Sqrt)
            act.wait_ge(*full("norm_cols", -1))
            go(par[:, :, NORMW:NORMW + KT], ps("norm_cols", -1)[:, 0:DEPTH * KT].rearrange("p (l k) -> p l k", l=DEPTH), ACT.Copy)\
                .then_inc(done("norm_cols", -1), 1)
            for t in range(NT):
                act.wait_ge(s(f"x_loaded{t}"), 16)
                go(page(12), page(17 + t), ACT.Square, scale=D ** -0.5, accum_out=mean_sq[:, t:t + 1]).then_inc(s("x_mean"), 1)
                act.wait_ge(s("x_mean"), t + 1)
            go(root, mean_sq, ACT.Sqrt, bias=const("eps")[:, 0:1]).then_inc(s("root"), 1)
            for m in range(1, KT, 2):
                act.wait_ge(*full(f"x_in{m}", -1))
                go(XY[:, m, :], ps(f"x_in{m}", -1)[:, :], ACT.Copy).then_inc(done(f"x_in{m}", -1), 1)

            def square_x(layer, m):
                act.wait_ge(*read(f"out{m}", layer))
                if m >= 3:
                    act.wait_ge(s("sq_added"), layer * (KT - 2) + m - 2)
                go(half(24, m % 2) if m > 0 else half(11, 0), XY[:, m, :], ACT.Square).then_inc(s("x_sq"), 1)

            for layer in range(DEPTH + 1):
                if layer > 0:
                    act.wait_ge(*full("stat", layer - 1))
                    go(root, ps("stat", layer - 1)[:, 0:NT], ACT.Sqrt, bias=const("eps")[:, 0:1]).then_inc(done("stat", layer - 1), 1)
                if layer == DEPTH:
                    act.wait_ge(s("rms"), DEPTH + 1)
                    act.wait_ge(*read(f"row{KT - 1}", DEPTH))
                    t = 1
                    go(page(17 + t), page(17 + t), ACT.Copy, scale=rms[:, t:t + 1]).then_inc(s(f"scaled{t}"), 1)
                    break

                def norm():
                    for k in range(KT):
                        act.wait_ge(*at("h_raw", layer, k + 1))
                        go(act_hi[:, k, :], half(13 + k // 2, k % 2), ACT.Copy).then_inc(s("h_hi"), 1)

                def shift(job):
                    act.wait_ge(*full(job, layer))
                    dst = {"k": K, "r": R, "v": V}[job[0]][:, int(job[1]), :] if job != "wa" else WA
                    n = 64 if job == "wa" else P
                    c = MUC + MU_ROW[job]
                    if job == "k0":
                        if layer == 0:
                            for l in range(DEPTH):
                                act.wait_ge(*full(f"params{l}", -1))
                                go(par[:, l, 0:N_ROWS], ps(f"params{l}", -1)[:, 0:N_ROWS], ACT.Copy).then_inc(done(f"params{l}", -1), 1)
                        act.wait_ge(s("derived"), 5)
                    go(dst[0:n], ps(job, layer)[0:n, :], ACT.Identity, scale=der[0:n, layer, c:c + 1]).then_inc(done(job, layer), 1)

                def kk_input():
                    for p in range(2):
                        act.wait_ge(*read(f"k{p}", layer))
                        go(KN[:, p, :], K[:, p, :], ACT.Square, scale=par[:, layer, KKP + p:KKP + p + 1]).then_inc(s("kk_sq"), 1)

                def kk_norm():
                    for p in range(2):
                        act.wait_ge(*full(f"kk{p}", layer))
                        go(KN[:, p, :], ps(f"kk{p}", layer)[:, :], ACT.Sqrt, scale=64.0).then_inc(done(f"kk{p}", layer), 1)

                def lora_tanh():
                    act.wait_ge(*read("wa", layer))
                    go(WA[0:LORA], WA[0:LORA], ACT.Tanh).then_inc(s("lora_in"), 1)

                def lora():
                    for z, dst, c in (("zw", TH, HW0), ("za", TA, HA0)):
                        for p in range(2):
                            act.wait_ge(*full(f"{z}{p}", layer))
                            go(dst[:, p, :], ps(f"{z}{p}", layer)[:, :], ACT.Tanh, scale=0.5, bias=der[:, layer, c + p:c + p + 1])\
                                .then_inc(done(f"{z}{p}", layer), 1)

                def decay_exp():
                    for p in range(2):
                        act.wait_ge(*at("decay_sum", layer, p + 1))
                        src = TH[:, p, :].rearrange("p (c t) -> p c t", t=CH)
                        go(Pd[:, p, :, 1:CH + 1], src, ACT.Exp, scale=-0.5 * DECAY).then_inc(s("decay_exp"), 1)
                        go(PI[:, p, :], TH[:, p, :], ACT.Exp, scale=0.5 * DECAY).then_inc(s("decay_exp"), 1)

                def gate(group, p):
                    k = {"rwkv": 0, "conv": 2, "moba": 4, "ret": 6}[group] + p
                    job = f"{group}_g{p}"
                    act.wait_ge(*full(job, layer))
                    act.wait_ge(s("x_spill"), 16 * KT * (layer + 1))
                    go(XY[:, k, :], ps(job, layer)[:, :], ACT.Tanh, scale=0.5).then_inc(done(job, layer), 1)

                def copy(job):
                    act.wait_ge(*full(job, layer))
                    p = int(job[2])
                    if job == "rq0":
                        act.wait_ge(*at("kappa", layer))
                    if job[:2] == "rk":
                        act.wait_ge(*at("rotated", layer, 1 + p))
                    if job == "rv0":
                        act.wait_ge(*full("za1", layer))
                    if job in ("mq0", "mk0"):
                        act.wait_ge(*full("scores311", layer))
                    if job == "mv0":
                        act.wait_ge(*full("rows_rv1", layer))
                    dst = {"mq": MQ, "mk": MK, "mv": MVRAW, "rv": MVRAW}.get(job[:2], RRAW)[:, p, :]
                    go(dst, ps(job, layer)[:, :], ACT.Copy).then_inc(done(job, layer), 1)

                def to_rows(what):
                    for p in range(2) if what != "rv" else ():
                        job = f"rows_{what}{p}"
                        act.wait_ge(*full(job, layer))
                        src = ps(job, layer)[:, :]
                        if what == "alp":
                            for t in range(NT):
                                ins = go(BA[:, t * HEADS + 2 * p:t * HEADS + 2 * p + 2, 1, :],
                                         src[:, t * P:(t + 1) * P].rearrange("p (h n) -> p h n", h=2), ACT.Copy)
                            ins.then_inc(done(job, layer), 1)
                        else:
                            if what == "mv":
                                act.wait_ge(*read(f"ret_ms{1}", layer))
                            go(rows[what][:, :, p * P:(p + 1) * P], src.rearrange("p (t c) -> p t c", t=NT), ACT.Copy).then_inc(done(job, layer), 1)

                def inverse_x(n):
                    for g in range(2):
                        act.wait_ge(*full(f"x{n}_{g}", layer))
                        if n > LEVELS[0]:
                            act.wait_ge(*full(f"yt{n // 2}_{g}", layer))
                        go(Xm[:, 8 * g:8 * g + 8, :], ps(f"x{n}_{g}", layer)[:, :].rearrange("p (m c) -> p m c", m=8), ACT.Copy)\
                            .then_inc(done(f"x{n}_{g}", layer), 1)

                def attend(g):
                    if 1 <= g <= 16:
                        w = ((g - 1) % NT + 1) * P
                        act.wait_ge(*full(f"pt{g - 1}", layer))
                        go(PT[:, g % 2, 0:w], ps(f"pt{g - 1}", layer)[:, 0:w], ACT.Copy).then_inc(done(f"pt{g - 1}", layer), 1)
                    if g <= 15:
                        pb = PB[:, g % 2, 0:(g % NT + 1) * P]
                        act.wait_ge(*at("logit_max", layer, g + 1))
                        go(pb, pb, ACT.Exp, bias=small[:, g % 2:g % 2 + 1], accum_out=small[:, 2 + g % 2:3 + g % 2]).then_inc(s("prob"), 1)

                def conv_h(p):
                    act.wait_ge(*read(f"ch{p}", layer))
                    act.wait_ge(*at("conv_pad", layer))
                    go(CA[:, p, :], CU[:, p, 0:T], ACT.Copy, scale=par[:, layer, CONVW + p:CONVW + p + 1]).then_inc(s("conv_tap"), 1)

                def conv_c(p):
                    act.wait_ge(*full(f"cc{p}", layer))
                    if p == 0:
                        act.wait_ge(*full("ret_y1", layer))
                    go(CU[:, p, 2:T + 2], ps(f"cc{p}", layer)[:, :], ACT.Copy).then_inc(done(f"cc{p}", layer), 1)

                def chunk_b(g):
                    act.wait_ge(*full(f"b{g}", layer))
                    go(BA[:, 8 * g:8 * g + 8, 0, :], ps(f"b{g}", layer)[:, :].rearrange("p (m c) -> p m c", m=8), ACT.Copy)\
                        .then_inc(done(f"b{g}", layer), 1)

                def chunk_uw():
                    for t in range(NT):
                        act.wait_ge(*full(f"uw{t}", layer))
                        go(UW[:, t * HEADS:(t + 1) * HEADS, :, :],
                           ps(f"uw{t}", layer)[:, :].rearrange("p (m x i) -> p m x i", m=HEADS, x=2), ACT.Copy)\
                            .then_inc(done(f"uw{t}", layer), 1)

                def chunk_y1(c):
                    if c == 0:
                        act.wait_ge(*at("y_ret", layer))
                    act.wait_ge(*full(f"y1{c}", layer))
                    for p in range(2):
                        ins = go(Y1[:, p, :].rearrange("p (t c i) -> p t c i", c=2, i=CH)[:, :, c, :],
                                 ps(f"y1{c}", layer)[:, p * 256:(p + 1) * 256].rearrange("p (t i) -> p t i", i=CH), ACT.Copy)
                    ins.then_inc(done(f"y1{c}", layer), 1)

                def retain_state():
                    if layer == 0:
                        act.wait_ge(s("const_b"), 16 * 4)
                    act.wait_ge(*full("ret_state", layer))
                    act.wait_ge(*at("rotated", layer))
                    go(RST, ps("ret_state", layer)[:, 0:2 * (NT - 1) * N].rearrange("p (a c i) -> p a c i", a=2, c=NT - 1), ACT.Copy)\
                        .then_inc(done("ret_state", layer), 1)

                def retain_out(p):
                    act.wait_ge(*full(f"ret_y{p}", layer))
                    go(RSQ[:, p, :], ps(f"ret_y{p}", layer)[:, :], ACT.Square).then_inc(s("ret_sq"), 1)
                    go(RY[:, p, :], ps(f"ret_y{p}", layer)[:, :], ACT.Copy).then_inc(done(f"ret_y{p}", layer), 1)

                def ln_scale(p):
                    act.wait_ge(*at("ln_scaled", layer, p + 1))
                    go(Y1[:, p, :], Y1[:, p, :], ACT.Identity, scale=par[:, layer, LNW + p:LNW + p + 1], bias=par[:, layer, LNB + p:LNB + p + 1])\
                        .then_inc(s("ln_affine"), 1)

                def ln_square():
                    for p in range(2):
                        act.wait_ge(*read(f"mean{p}", layer))
                        go(LNS[:, p, :], Y1[:, p, :], ACT.Square).then_inc(s("ln_sq"), 1)

                def ln_var():
                    for p in range(2):
                        act.wait_ge(*full(f"var{p}", layer))
                        go(LNS[:, p, :], ps(f"var{p}", layer)[:, :], ACT.Sqrt, bias=const("eps")[:, 1:2]).then_inc(done(f"var{p}", layer), 1)

                def ret_root():
                    for p in range(2):
                        act.wait_ge(*read(f"ret_ms{p}", layer))
                        go(RSQ[:, p, :], RSQ[:, p, :], ACT.Sqrt).then_inc(s("ret_root"), 1)

                def split_y(k):
                    n = Y_ORDER.index(k)
                    if n < KT - 1:
                        act.wait_ge(s("h_used"), layer * (KT - 1) + n + 1)
                    else:
                        act.wait_ge(*full(LAST_TILE, layer))
                    if k // 2 == 2:
                        act.wait_ge(*read(f"moba_y{k % 2}", layer))
                    else:
                        act.wait_ge(*at({0: "y_rwkv", 1: "y_conv", 3: "y_ret"}[k // 2], layer, k % 2 + 1))
                    go(act_hi[:, k, :], XY[:, k, :], ACT.Copy).then_inc(s("y_hi"), 1)

                def project_out(m):
                    square_x(layer, m)
                    if m == KT - 3:
                        go(small[:, 24:25], const("eps")[:, 0:1], ACT.Sqrt)

                run = dict(norm=norm, shift=shift, kk_input=kk_input, kk_norm=kk_norm, lora_tanh=lora_tanh, lora=lora,
                           decay_exp=decay_exp, gate=gate, copy=copy, to_rows=to_rows,
                           inverse_x=inverse_x, attend=attend, conv_c=conv_c, conv_h=conv_h, chunk_b=chunk_b,
                           chunk_uw=chunk_uw, chunk_y1=chunk_y1, retain_state=retain_state, retain_out=retain_out,
                           ln_square=ln_square, ln_scale=ln_scale, ln_var=ln_var, ret_root=ret_root, split_y=split_y, project_out=project_out)
                for name, *args in STEPS:
                    if name in run:
                        run[name](*args)

        @block.vector
        def _(dve):
            tt, ts, stt = dve.tensor_tensor, dve.tensor_scalar, dve.scalar_tensor_tensor
            n_step = [0]

            def mark(ins):
                n_step[0] += 1
                ins.then_inc(s("dve_step"), 1)
                return n_step[0]

            def link(ins):
                dve.wait_ge(s("dve_step"), mark(ins))

            def reciprocal_of_root(layer):
                if layer > 0:
                    dve.wait_ge(*read("stat", layer - 1))
                else:
                    dve.wait_ge(s("root"), 1)
                dve.reciprocal(rms, root).then_inc(s("rms"), 1)

            dve.memset(bias_rows[:, :, T:DIST], MASKED)
            dve.wait_ge(s("bias_in"), 16)
            for bucket, start, stop in bucket_runs():
                ins = dve.tensor_copy(bias_rows[:, :, start:stop], bias_table[:, bucket, :].unsqueeze(2).to_broadcast([P, HEADS, stop - start]))
            ins.then_inc(s("bias_rows"), 1)
            reciprocal_of_root(0)
            for m in range(0, KT, 2):
                dve.wait_ge(*full(f"x_in{m}", -1))
                dve.tensor_copy(XY[:, m, :], ps(f"x_in{m}", -1)[:, :]).then_inc(done(f"x_in{m}", -1), 1)
            dve.wait_ge(*read("norm_cols", -1))

            def evacuate_row(m):
                if m == 0:
                    dve.wait_ge(s("fnorm_loaded"), 16)
                dve.wait_ge(*full(f"row{m}", DEPTH))
                tt(out_rows[:, :, m * P:(m + 1) * P], ps(f"row{m}", DEPTH)[:, :].rearrange("p (t c) -> p t c", t=NT),
                   fnorm[:, m * P:(m + 1) * P].unsqueeze(1).to_broadcast([P, NT, P]), ALU.mult).then_inc(done(f"row{m}", DEPTH), 1)

            for layer in range(DEPTH + 1):
                def scaled(k):
                    stt(half(13 + k // 2, k % 2), XY[:, k, :], par[:, layer, NORMW + k:NORMW + k + 1], ps("rn", layer)[:, :], ALU.mult, ALU.mult)\
                        .then_inc(s("h_raw"), 1)

                def low(k):
                    dve.wait_ge(*at("h_hi", layer, k + 1))
                    ins = tt(act_lo[:, k, :], half(13 + k // 2, k % 2), act_hi[:, k, :].bitcast(F32), ALU.subtract)
                    ins.then_inc(s("h_split"), 1)

                def norm():
                    dve.wait_ge(*full("rn", layer))
                    for k in range(KT):
                        if layer == 0 and k % 2:
                            dve.wait_ge(*read(f"x_in{k}", -1))
                        scaled(k)
                        if k >= 1:
                            low(k - 1)
                    low(KT - 1)
                    if layer == 0:
                        derive()

                def derive():
                    for l in range(DEPTH):
                        dve.wait_ge(*read(f"params{l}", -1))
                    for c, n, src, a, b in ((MUC, 7, MU, -1.0, 1.0), (HW0, 2, W0, 0.5, 0.0), (HA0, 2, A0, 0.5, 0.0),
                                            (KA2, 2, KAP, 0.5, 0.0), (KA1, 2, KAP, -0.5, 1.0)):
                        ts(der[:, :, c:c + n], par[:, :, src:src + n], a, b, ALU.mult, ALU.add).then_inc(s("derived"), 1)
                    dve.wait_ge(s("derived"), 5)
                    dve.wait_ge(s("const_b"), 16 * 4)
                    link(dve.tensor_copy(lmask[:].rearrange("p a l c -> p (a l c)"), mask_words))

                if layer > 0:
                    reciprocal_of_root(layer)
                if layer == DEPTH:
                    dve.wait_ge(*read(f"row{KT - 1}", DEPTH))
                    dve.wait_ge(s("rms"), DEPTH + 1)
                    for t in (0, 2, 3):
                        ts(page(17 + t), page(17 + t), rms[:, t:t + 1], None, ALU.mult).then_inc(s(f"scaled{t}"), 1)
                    break

                def pads():
                    dve.memset(Pd[:, :, :, 0:1], 1.0).then_inc(s("pads"), 1)

                def shift(job):
                    dve.wait_ge(*read(job, layer, 1))
                    dst = {"k": K, "r": R, "v": V}[job[0]][:, int(job[1]), :] if job != "wa" else WA
                    n = 64 if job == "wa" else P
                    c = MU + MU_ROW[job]
                    b = ps(job, layer)
                    stt(dst[0:n, 1:T], b[0:n, 0:T - 1], par[0:n, layer, c:c + 1], dst[0:n, 1:T], ALU.mult, ALU.add)\
                        .then_inc(done(job, layer), 1)

                def kk_norm():
                    for p in range(2):
                        dve.wait_ge(*read(f"kk{p}", layer))
                    link(ts(KN, KN, 1e-12, None, ALU.max))
                    link(dve.reciprocal(KN, KN))
                    for p in range(2):
                        stt(KN[:, p, :], K[:, p, :], par[:, layer, KKP + p:KKP + p + 1], KN[:, p, :], ALU.mult, ALU.mult).then_inc(s("kk_unit"), 1)

                def decay_scan():
                    for p in range(2):
                        dve.wait_ge(*read(f"zw{p}", layer))
                    link(ts(TH, TH, 1.0, None, ALU.add))
                    for p in range(2):
                        dve.tensor_tensor_scan(TH[:, p, :], const("chunk_reset"), TH[:, p, :], 0.0, ALU.mult, ALU.add).then_inc(s("decay_sum"), 1)

                def factors(part):
                    flat = Pd.rearrange("p a c t -> p (a c) t")
                    chunks = lambda v: v.rearrange("p a (c t) -> p (a c) t", t=CH)
                    if part == 0:
                        for p in range(2):
                            dve.wait_ge(*read(f"za{p}", layer))
                        for p in range(2):
                            c = mark(ts(KF[:, p, :], TA[:, p, :], der[:, layer, KA2 + p:KA2 + p + 1], der[:, layer, KA1 + p:KA1 + p + 1], ALU.mult, ALU.add))
                        dve.wait_ge(*at("kk_unit", layer))
                        dve.wait_ge(s("dve_step"), c)
                        mark(stt(TA, TA, 1.0, KN, ALU.add, ALU.mult))
                        mark(tt(K, K, KF, ALU.mult))
                    elif part == 1:
                        dve.wait_ge(*at("decay_exp", layer))
                        dve.wait_ge(s("dve_step"), n_step[0])
                        stt(TA, TA, -0.5, PI, ALU.mult, ALU.mult).then_inc(s("beta"), 1)
                        dve.wait_ge(*at("beta", layer))
                        tt(PI, K, PI, ALU.mult).then_inc(s("kappa"), 1)
                        dve.wait_ge(*at("pads", layer))
                        if layer == 0:
                            dve.wait_ge(s("cleared"), 32)
                        tt(chunks(AR[:, 0]), chunks(KN), flat[:, :, 0:CH], ALU.mult).then_inc(s("alpha"), 1)
                    else:
                        tt(chunks(AR[:, 1]), chunks(R), flat[:, :, 1:CH + 1], ALU.mult).then_inc(s("rho"), 1)
                        mark(dve.tensor_copy(w_end[:].rearrange("p a c -> p (a c)").unsqueeze(2), flat[:, :, CH:CH + 1]))
                        dve.wait_ge(*at("rho", layer))
                        for p in range(2):
                            stt(R[:, p, :], R[:, p, :], par[:, layer, RKP + p:RKP + p + 1], K[:, p, :], ALU.mult, ALU.mult).then_inc(s("rkv"), 1)

                def bonus():
                    for p in range(2):
                        dve.wait_ge(*full(f"bonus{p}", layer))
                        stt(R[:, p, :], ps(f"bonus{p}", layer)[:, :], 64.0, V[:, p, :], ALU.mult, ALU.mult).then_inc(done(f"bonus{p}", layer), 1)

                def gate(group, p):
                    k = {"rwkv": 0, "conv": 2, "moba": 4, "ret": 6}[group] + p
                    job = f"{group}_g{p}"
                    dve.wait_ge(*read(job, layer, 1))
                    stt(XY[:, k, :], XY[:, k, :], 1.0, ps(job, layer)[:, :], ALU.add, ALU.mult).then_inc(done(job, layer), 1)

                def scores(t):
                    for p in range(2):
                        for hh in range(2):
                            job = f"scores{t}{p}{hh}"
                            dve.wait_ge(*full(job, layer))
                            tt(SC[:, t * HEADS + 2 * p + hh, :], ps(job, layer)[:, 0:256], const("score_mask"), ALU.mult).then_inc(done(job, layer), 1)

                def mask(level, transposed, n):
                    return lmask[:, transposed, LEVELS.index(level), :].unsqueeze(1).to_broadcast([P, n, CH])

                def block_rows(part):
                    if part == 0:
                        dve.wait_ge(s("blocks_in"), 64 * (layer + 1))
                        flat = T_blk.rearrange("p i j -> p (i j)")
                        link(dve.memset(flat, 0.0))
                        link(dve.memset(flat[:, ::BLK + 1], 1.0))
                    for i in range(*((1, 8), (8, 12), (12, BLK))[part]):
                        prod = AT_prod[:, 0:i, 0:i]
                        link(tt(prod, T_blk[:, 0:i, 0:i].rearrange("p j k -> p k j"), A_blk[:, 0:i, i].unsqueeze(1).to_broadcast([P, i, i]), ALU.mult))
                        link(dve.tensor_reduce(T_blk[:, i, 0:i], prod, AX_X, ALU.add))
                    if part == 2:
                        dve.tensor_copy(TT_blk, T_blk.rearrange("p i j -> p j i")).then_inc(s("blocks_done"), 1)

                def inverse_y(n):
                    for g in range(2):
                        m8 = slice(8 * g, 8 * g + 8)
                        dve.wait_ge(*full(f"y{n}_{g}", layer))
                        dve.copy_predicated(Ti[:, m8, :], mask(n, 0, 8), ps(f"y{n}_{g}", layer)[:, :].rearrange("p (m c) -> p m c", m=8))\
                            .then_inc(done(f"y{n}_{g}", layer), 1)

                def inverse_yt(n):
                    for g in range(2):
                        m8 = slice(8 * g, 8 * g + 8)
                        dve.wait_ge(*full(f"yt{n}_{g}", layer))
                        dve.copy_predicated(TiT[:, m8, :], mask(n, 1, 8), ps(f"yt{n}_{g}", layer)[:, :].rearrange("p (m c) -> p m c", m=8))\
                            .then_inc(done(f"yt{n}_{g}", layer), 1)

                def rotate(job):
                    p = int(job[-1])
                    j = ["rq0", "rq1", "rk0", "rk1"].index(job)
                    dst = (RQ if job[1] == "q" else RK)[:, p, :]
                    dve.wait_ge(*full(f"rot_{job}", layer))
                    if j == 0 and layer == 0:
                        dve.wait_ge(s("bias_out"), 16)
                    raw = RRAW[:, p, :]
                    c = mark(tt(dst, raw, const("cos"), ALU.mult))
                    dve.wait_ge(s("dve_step"), c)
                    tt(raw, ps(f"rot_{job}", layer)[:, :], const("sin"), ALU.mult).then_inc(done(f"rot_{job}", layer), 1)
                    dve.wait_ge(*read(f"rot_{job}", layer))
                    tt(dst, dst, raw, ALU.add).then_inc(s("rotated"), 1)

                def attend(g):
                    if g > 15:
                        return
                    h, _, _, qb = unit(g)
                    w = (qb + 1) * P
                    pb = PB[:, g % 2, 0:w]
                    if layer == 0 and g == 0:
                        dve.wait_ge(s("bias_back"), 16)
                    dve.wait_ge(*full(f"s{g}", layer))
                    stt(pb, ps(f"s{g}", layer)[:, 0:w], 0.125, bias[:, h, T - w:T], ALU.mult, ALU.add).then_inc(done(f"s{g}", layer), 1)
                    dve.wait_ge(*read(f"s{g}", layer))
                    dve.tensor_reduce(small[:, g % 2:g % 2 + 1], pb, AX_X, ALU.max, negate=True).then_inc(s("logit_max"), 1)
                    dve.wait_ge(*at("prob", layer, g + 1))
                    r = small[:, 4 + g % 2:5 + g % 2]
                    link(dve.reciprocal(r, small[:, 2 + g % 2:3 + g % 2]))
                    ts(pb, pb, r, None, ALU.mult).then_inc(s("prob_norm"), 1)

                def attend_out(p):
                    dve.wait_ge(*full(f"moba_y{p}", layer))
                    finish_tile(4 + p, ps(f"moba_y{p}", layer)[:, :]).then_inc(done(f"moba_y{p}", layer), 1)

                def finish_tile(k, y):
                    return stt(XY[:, k, :], y, 0.5, XY[:, k, :], ALU.mult, ALU.mult)

                def conv_c(p):
                    if p == 0:
                        dve.wait_ge(*full("ret_y1", layer))
                        dve.memset(CU[:, :, 0:2], 0.0).then_inc(s("conv_pad"), 1)

                def conv_h(p):
                    dve.wait_ge(*full(f"ch{p}", layer))
                    dve.wait_ge(*read(f"cc{p}", layer))
                    tt(CU[:, p, 2:T + 2], CU[:, p, 2:T + 2], ps(f"ch{p}", layer)[:, :], ALU.mult).then_inc(done(f"ch{p}", layer), 1)

                def conv_taps(p):
                    w = lambda j: par[:, layer, CONVW + 2 * j + p:CONVW + 2 * j + p + 1]
                    dve.wait_ge(*at("conv_tap", layer, p + 1))
                    for j in (1, 2):
                        link(stt(CA[:, p, :], CU[:, p, j:T + j], w(j), CA[:, p, :], ALU.mult, ALU.add))

                def conv_b(p):
                    dve.wait_ge(*full(f"cb{p}", layer))
                    tt(CA[:, p, :], CA[:, p, :], ps(f"cb{p}", layer)[:, :], ALU.mult).then_inc(done(f"cb{p}", layer), 1)

                def conv_out(p):
                    dve.wait_ge(*read(f"conv_g{p}", layer))
                    dve.wait_ge(*read(f"cb{p}", layer))
                    finish_tile(2 + p, CA[:, p, :]).then_inc(s("y_conv"), 1)

                par8 = lambda v, c: v.rearrange("p a (t x) i -> p a t x i", x=2)[:, :, :, c, :]
                chunk_ps = lambda j: ps(j, layer)[:, :].rearrange("p (a t i) -> p a t i", a=2, i=N)

                def chunk_g(c):
                    dve.wait_ge(*full(f"g{c}", layer))
                    for p in range(2):
                        ins = tt(par8(GT, c)[:, p], chunk_ps(f"g{c}")[:, p], const("eye64").unsqueeze(1).to_broadcast([P, NT, N]), ALU.add)
                    ins.then_inc(done(f"g{c}", layer), 1)

                def chunk_h(c):
                    we = w_end[:].rearrange("p a (t x) -> p a t x", x=2)
                    dve.wait_ge(*full(f"h{c}", layer))
                    for p in range(2):
                        ins = tt(par8(HP, c)[:, p], chunk_ps(f"h{c}")[:, p], we[:, p, :, c].unsqueeze(2).to_broadcast([P, NT, N]), ALU.mult)
                    ins.then_inc(done(f"h{c}", layer), 1)
                    if c == 1:
                        for j in range(2):
                            dve.wait_ge(*read(f"h{j}", layer))
                        dve.tensor_copy(ST[:, :, 1, :], HP[:, :, 0, :]).then_inc(s("first_state"), 1)

                def chunk_q(c):
                    rho = AR[:, 1].rearrange("p a (t x i) -> p a t x i", x=2, i=CH)
                    dve.wait_ge(*full(f"q{c}", layer))
                    for p in range(2):
                        ins = tt(rho[:, p, :, c, :], rho[:, p, :, c, :], chunk_ps(f"q{c}")[:, p], ALU.add)
                    ins.then_inc(done(f"q{c}", layer), 1)

                def chain(c):
                    dve.wait_ge(*full(f"chain{c}", layer))
                    b = ps(f"chain{c}", layer)
                    for p in range(2):
                        ins = stt(ST[:, p, c + 1, :], b[:, p * N:(p + 1) * N], w_end[:, p, c:c + 1], HP[:, p, c, :], ALU.mult, ALU.add)
                    ins.then_inc(done(f"chain{c}", layer), 1)

                def chunk_y():
                    for c in range(2):
                        dve.wait_ge(*read(f"y1{c}", layer))
                    for p in range(2):
                        dve.wait_ge(*full(f"y2{p}", layer))
                        tt(Y1[:, p, CH:T], Y1[:, p, CH:T], ps(f"y2{p}", layer)[:, CH:T], ALU.add).then_inc(done(f"y2{p}", layer), 1)

                def to_rows(what):
                    if what != "rv":
                        return
                    decay = const("k_decay").rearrange("p (h t) -> p t h", h=HEADS)
                    for p in range(2):
                        dve.wait_ge(*full(f"rows_rv{p}", layer))
                        tt(rows["rv"][:, :, p * P:(p + 1) * P].rearrange("p t (h n) -> p t h n", h=2),
                           ps(f"rows_rv{p}", layer)[:, :].rearrange("p (t h n) -> p t h n", t=NT, h=2),
                           decay[:, :, 2 * p:2 * p + 2].unsqueeze(3).to_broadcast([P, NT, 2, N]), ALU.mult).then_inc(done(f"rows_rv{p}", layer), 1)

                def retain_state():
                    dve.wait_ge(*read("ret_state", layer))
                    for c in range(1, NT - 1):
                        ins = tt(RST[:, :, c, :], RST[:, :, c, :], RST[:, :, c - 1, :], ALU.add)
                        if c < NT - 2:
                            link(ins)
                    ins.then_inc(s("ret_prefix"), 1)

                def retain(i):
                    if i < HEADS:
                        dve.wait_ge(*full(f"rs{i}", layer))
                        tt(RSB[:, i % 2, :].rearrange("p (c t) -> p c t", c=NT), ps(f"rs{i}", layer)[:, :].rearrange("p (c t) -> p c t", c=NT),
                           const("causal").unsqueeze(1).to_broadcast([P, NT, P]), ALU.mult).then_inc(done(f"rs{i}", layer), 1)

                def ln_mean():
                    for p in range(2):
                        dve.wait_ge(*full(f"mean{p}", layer))
                        tt(Y1[:, p, :], Y1[:, p, :], ps(f"mean{p}", layer)[:, :], ALU.subtract).then_inc(done(f"mean{p}", layer), 1)

                def ret_stat():
                    dve.wait_ge(s("ret_eps"), 16 * (layer + 1))
                    for p in range(2):
                        dve.wait_ge(*full(f"ret_ms{p}", layer))
                        tt(RSQ[:, p, :], ps(f"ret_ms{p}", layer)[:, :], eps_page[:, p * T:(p + 1) * T], ALU.add).then_inc(done(f"ret_ms{p}", layer), 1)

                def ret_recip(i):
                    p, a = divmod(i, 2)
                    dve.wait_ge(*at("ret_root", layer, p + 1))
                    v = RSQ[:, p, a * T // 2:(a + 1) * T // 2]
                    mark(dve.reciprocal(v, v))

                def ret_finish(p):
                    if p == 0:
                        dve.wait_ge(s("dve_step"), n_step[0])
                    dve.wait_ge(*read(f"ret_y{p}", layer))
                    link(tt(RY[:, p, :], RY[:, p, :], RSQ[:, p, :], ALU.mult))
                    finish_tile(6 + p, RY[:, p, :]).then_inc(s("y_ret"), 1)

                def ln_recip(i):
                    p, a = divmod(i, 2)
                    dve.wait_ge(*read(f"var{p}", layer))
                    v = LNS[:, p, a * T // 2:(a + 1) * T // 2]
                    mark(dve.reciprocal(v, v))

                def ln_scale(p):
                    dve.wait_ge(s("dve_step"), n_step[0])
                    y = Y1[:, p, :]
                    tt(y, y, LNS[:, p, :], ALU.mult).then_inc(s("ln_scaled"), 1)

                def rwkv_finish(p):
                    dve.wait_ge(*at("ln_affine", layer, p + 1))
                    link(tt(Y1[:, p, :], Y1[:, p, :], R[:, p, :], ALU.add))
                    finish_tile(p, Y1[:, p, :]).then_inc(s("y_rwkv"), 1)

                def split_y(k):
                    dve.wait_ge(*at("y_hi", layer, Y_ORDER.index(k) + 1))
                    tt(act_lo[:, k, :], XY[:, k, :], act_hi[:, k, :].bitcast(F32), ALU.subtract).then_inc(s("y_split"), 1)

                def project_out(m):
                    if m >= 2:
                        dve.wait_ge(s("x_sq"), layer * KT + m)
                        if m >= 3:
                            dve.wait_ge(s("sq_added"), layer * (KT - 2) + m - 2)
                        tt(half(11, 0), half(11, 0), half(24, (m - 1) % 2), ALU.add).then_inc(s("sq_added"), 1)
                    dve.wait_ge(*full(f"out{m}", layer))
                    dve.wait_ge(s(f"x_back{m}"), 16 * (layer + 1))
                    tt(XY[:, m, :], XY[:, m, :], ps(f"out{m}", layer)[:, :], ALU.add).then_inc(done(f"out{m}", layer), 1)
                    if layer == DEPTH - 1:
                        for n in (m - 1, m) if m == KT - 1 else (m - 1,) if m > 0 else ():
                            evacuate_row(n)

                run = dict(norm=norm, shift=shift, kk_norm=kk_norm, decay_scan=decay_scan, factors=factors, bonus=bonus,
                           gate=gate, scores=scores, block_rows=block_rows, inverse_y=inverse_y, inverse_yt=inverse_yt, rotate=rotate,
                           attend=attend, attend_out=attend_out, conv_c=conv_c, conv_h=conv_h, conv_taps=conv_taps, conv_b=conv_b,
                           conv_out=conv_out, chunk_g=chunk_g, chunk_h=chunk_h, chunk_q=chunk_q, chain=chain, chunk_y=chunk_y,
                           to_rows=to_rows, retain_state=retain_state, retain=retain, ln_mean=ln_mean, ret_stat=ret_stat, ret_recip=ret_recip, ret_finish=ret_finish,
                           ln_recip=ln_recip, ln_scale=ln_scale, rwkv_finish=rwkv_finish, split_y=split_y,
                           project_out=project_out, decay_exp=pads)
                for name, *args in STEPS:
                    if name in run:
                        run[name](*args)


def shape_constants():
    c = {}
    i = np.arange(P)
    c["ident"] = np.eye(P)
    c["head_mean"] = (i[:, None] // N == i[None, :] // N) / N
    c["all_mean"] = np.full((P, 1), 1.0 / D)
    c["one"] = np.ones((P, 1))
    rot = np.zeros((P, P))
    rot[i[1::2], i[0::2]] = -1.0
    rot[i[0::2], i[1::2]] = 1.0
    c["rot"] = rot
    c["causal"] = i[:, None] <= i[None, :]
    a, b = np.arange(P)[:, None] % CH, np.arange(CH)[None, :]
    c["score_mask"] = np.concatenate([a < b, a <= b, a < b, a <= b], axis=1)
    c["eye64"] = a == b
    gamma = 1.0 - 2.0 ** (-5.0 - np.arange(HEADS))
    pos = np.arange(T)
    c["k_decay"] = np.stack([gamma[h] ** -(kb * P + i.astype(np.float64)) * N ** -0.5 for h in range(HEADS) for kb in range(NT)], axis=1)
    c["eps"] = np.tile([[NORM_EPS, LNX_EPS]], (P, 1))
    c["chunk_reset"] = np.tile(pos % CH != 0, (P, 1))
    theta = (1.0 / (10000.0 ** np.linspace(0.0, 1.0, N // 2, dtype=np.float32))).astype(np.float32)
    angle = (pos.astype(np.float32)[None, :] * theta[:, None]).astype(np.float32).astype(np.float64)
    angle = angle[(i % N) // 2]
    c["cos"], c["sin"] = np.cos(angle), np.sin(angle)
    ret_eps = np.concatenate([NORM_EPS * gamma[2 * p + i[:, None] // N] ** (-2.0 * pos[None, :]) for p in range(2)], axis=1)
    consts = np.concatenate([np.asarray(c[n], np.float32) for n, _ in CONSTS], axis=1)
    levels = np.stack([(a // (2 * n) == b // (2 * n)) & (a // n % 2 == 1) & (b // n % 2 == 0) for n in LEVELS], axis=1)
    levels_t = np.stack([(a // (2 * n) == b // (2 * n)) & (a // n % 2 == 0) & (b // n % 2 == 1) for n in LEVELS], axis=1)
    level_masks = np.stack([levels, levels_t], axis=1).reshape(P, -1).astype(np.int32)
    return consts, level_masks, ret_eps.astype(np.float32)


def bucket_runs():
    dist = T - 1 - np.arange(T)
    exact = BUCKETS // 2
    d_f = np.maximum(dist, 1).astype(np.float32)
    large = exact + (np.log(d_f / exact) / math.log(P / exact) * (BUCKETS - exact)).astype(np.int32)
    bucket = np.where(dist < exact, dist, np.minimum(large, BUCKETS - 1))
    starts = [0] + [i for i in range(1, T) if bucket[i] != bucket[i - 1]] + [T]
    return [(int(bucket[a]), a, b) for a, b in zip(starts, starts[1:])]


_INS = ["x", "norm_w", "w_in", "w_out", "rwkv_mu", "rwkv_w0", "rwkv_w2", "rwkv_a0", "rwkv_a2", "rwkv_k_k",
        "rwkv_k_a", "rwkv_r_k", "rwkv_lnx_w", "rwkv_lnx_b", "conv_w", "rel_bias", "final_norm_w"]


def kernel(**inputs):
    import numpy as _np
    import concourse.bacc as _bacc
    from concourse.bass_utils import run_bass_kernel_spmd as _run

    nc = _bacc.Bacc("TRN2", target_bir_lowering=False, num_devices=1)
    arrays, args = {}, []

    def give(name, a):
        a = _np.ascontiguousarray(a)
        arrays[f"in_{name}_dram"] = a
        args.append(nc.dram_tensor(f"in_{name}_dram", a.shape, mybir.dt.from_np(a.dtype), kind="ExternalInput").ap())

    for name in _INS:
        give(name, inputs[name])
    for name, a in zip(("consts", "level_masks", "ret_eps"), shape_constants()):
        give(name, a)
    args.append(nc.dram_tensor("x_scratch", (KT, P, T), F32, kind="Internal").ap())
    args.append(nc.dram_tensor("bias_scratch", (HEADS, P, DIST + 1), F32, kind="Internal").ap())
    for n in ("a_scratch", "t_scratch", "tt_scratch"):
        args.append(nc.dram_tensor(n, (MATS, P, CH), F32, kind="Internal").ap())
    args.append(nc.dram_tensor("out_0_dram", (1, T, D), F32, kind="ExternalOutput").ap())
    trunk_kernel(nc, *args)
    r = _run(nc, [arrays], core_ids=[0])
    return r.results[0]["out_0_dram"]
```
